# Optimizing a Trainium2 kernel written in Bass

```python
import math
import jax, jax.numpy as jnp
from jax import lax
import numpy as np

D_MODEL = 2048
BATCH = 1
SEQ = 256
DEPTH = 1

MIX_WIDTH = D_MODEL
RWKV_HEAD_DIM = 64
RWKV_WIDTH = MIX_WIDTH // 2
RWKV_HEADS = RWKV_WIDTH // RWKV_HEAD_DIM
DECAY_LORA = 64
AAA_LORA = 64
GATE_LORA = 160
DIFF_HEAD_DIM = 64
DIFF_V_DIM = 2 * DIFF_HEAD_DIM
DIFF_WIDTH = MIX_WIDTH // 2
DIFF_HEADS = DIFF_WIDTH // DIFF_V_DIM
DIFF_QK_WIDTH = 2 * DIFF_HEADS * DIFF_HEAD_DIM
Q_BLOCK = 128
ROPE_THETA = 10000.0
D_FF = ((8 * D_MODEL // 3 + 255) // 256) * 256
N_BRANCHES = 2
NORM_EPS = 1e-6
RWKV_GN_EPS = 64e-5
SUBLN_EPS = 1e-5

RWKV_SEG_SIZES = (RWKV_WIDTH, RWKV_WIDTH, RWKV_WIDTH, DECAY_LORA, DECAY_LORA, AAA_LORA, AAA_LORA, GATE_LORA)
RWKV_COLS = sum(RWKV_SEG_SIZES)
DIFF_COLS = 2 * DIFF_QK_WIDTH + DIFF_WIDTH
GATE_COLS = N_BRANCHES * D_MODEL
IN_COLS = RWKV_COLS + DIFF_COLS + GATE_COLS

kernel_name = 'hybrid_rwkv7_diffattn_macaron_encoder'

def rms_norm(x, g, eps=NORM_EPS):
    xf = x.astype(jnp.float32)
    y = xf * lax.rsqrt(jnp.mean(xf * xf, axis=-1, keepdims=True) + eps)
    return (y * g.astype(jnp.float32)).astype(x.dtype)

def swiglu_ffn(x, w_gu, w_down):
    gate, up = jnp.split(x @ w_gu, 2, axis=-1)
    return (jax.nn.silu(gate) * up) @ w_down

def centred_token_shift(y, mu_prev, mu_next):
    zero = jnp.zeros_like(y[:, :1])
    y_prev = jnp.concatenate([zero, y[:, :-1]], axis=1)
    y_next = jnp.concatenate([y[:, 1:], zero], axis=1)
    return y + mu_prev * (y_prev - y) + mu_next * (y_next - y)

def rope(x):
    T, dh = x.shape[1], x.shape[-1]
    half = dh // 2
    inv_freq = ROPE_THETA ** (-jnp.arange(half, dtype=jnp.float32) / half)
    ang = jnp.arange(T, dtype=jnp.float32)[:, None] * inv_freq[None, :]
    cos = jnp.cos(ang)[None, :, None, :]
    sin = jnp.sin(ang)[None, :, None, :]
    xf = x.astype(jnp.float32)
    x1, x2 = xf[..., :half], xf[..., half:]
    return jnp.concatenate([x1 * cos - x2 * sin, x2 * cos + x1 * sin], axis=-1).astype(x.dtype)

def heads(z):
    return z.reshape(z.shape[:-1] + (RWKV_HEADS, RWKV_HEAD_DIM))

def wkv7_bidirectional(r, w, k, v, kk, a):
    _, B, T, H, N = r.shape

    def to_scan(z):
        z = jnp.stack([z[0], jnp.flip(z[1], axis=1)]).astype(jnp.float32)
        return jnp.moveaxis(z, 2, 0)

    def step(S, inp):
        r_t, w_t, k_t, v_t, kk_t, a_t = inp
        sa = -jnp.einsum('dbhij,dbhj->dbhi', S, kk_t)
        S = (S * w_t[..., None, :]
             + sa[..., :, None] * (kk_t * a_t)[..., None, :]
             + v_t[..., :, None] * k_t[..., None, :])
        return S, jnp.einsum('dbhij,dbhj->dbhi', S, r_t)

    xs = tuple(to_scan(z) for z in (r, w, k, v, kk, a))
    S0 = jnp.zeros((2, B, H, N, N), jnp.float32)
    _, out = lax.scan(step, S0, xs)
    out = jnp.moveaxis(out, 0, 2)
    return out[0] + jnp.flip(out[1], axis=1)

def rwkv7_branch(rw_seg, w0, w_up, a0, a_up, g_up, k_k, k_a, r_k, gn_w, gn_b):
    split_at = np.cumsum(RWKV_SEG_SIZES)[:-1].tolist()
    r, k, v, wd_f, wd_b, ad_f, ad_b, gd = jnp.split(rw_seg, split_at, axis=-1)
    B, T, _ = r.shape
    wd = jnp.stack([wd_f, wd_b])
    ad = jnp.stack([ad_f, ad_b])
    w_log = -jax.nn.softplus(-(w0[:, None, None, :] + jnp.einsum('dbtr,drc->dbtc', jnp.tanh(wd), w_up))) - 0.5
    decay = jnp.exp(-jnp.exp(w_log.astype(jnp.float32)))
    a = jax.nn.sigmoid(a0[:, None, None, :] + jnp.einsum('dbtr,drc->dbtc', ad, a_up))
    g = jax.nn.sigmoid(gd) @ g_up
    kk = heads((k * k_k).astype(jnp.float32))
    kk = kk * lax.rsqrt(jnp.maximum(jnp.sum(kk * kk, axis=-1, keepdims=True), 1e-24))
    k_dir = heads(k[None] * (1.0 + (a - 1.0) * k_a))
    r_h, v_h = heads(r), heads(v)

    def both(z):
        return jnp.broadcast_to(z[None], (2,) + z.shape)

    o = wkv7_bidirectional(both(r_h), heads(decay), k_dir, both(v_h), both(kk), heads(a))
    mean = jnp.mean(o, axis=-1, keepdims=True)
    var = jnp.mean(jnp.square(o - mean), axis=-1, keepdims=True)
    o = ((o - mean) * lax.rsqrt(var + RWKV_GN_EPS)).reshape(B, T, RWKV_WIDTH)
    o = (o * gn_w.astype(jnp.float32) + gn_b.astype(jnp.float32)).astype(r.dtype)
    bonus = jnp.sum(r_h[None] * k_dir * r_k, axis=-1, keepdims=True) * v_h[None]
    bonus = jnp.sum(bonus, axis=0).reshape(B, T, RWKV_WIDTH)
    return (o + bonus) * g

def diff_attention_branch(q, k, v, lambda_q1, lambda_k1, lambda_q2, lambda_k2, subln_g, lam_init):
    B, T, _ = q.shape
    q = rope(q.reshape(B, T, 2 * DIFF_HEADS, DIFF_HEAD_DIM)) * (DIFF_HEAD_DIM ** -0.5)
    k = rope(k.reshape(B, T, 2 * DIFF_HEADS, DIFF_HEAD_DIM))
    v = v.reshape(B, T, DIFF_HEADS, DIFF_V_DIM)
    lam = (jnp.exp(jnp.sum(lambda_q1.astype(jnp.float32) * lambda_k1.astype(jnp.float32)))
           - jnp.exp(jnp.sum(lambda_q2.astype(jnp.float32) * lambda_k2.astype(jnp.float32)))
           + lam_init)
    n_blk = T // Q_BLOCK
    q_blocks = jnp.moveaxis(q.reshape(B, n_blk, Q_BLOCK, 2 * DIFF_HEADS, DIFF_HEAD_DIM), 1, 0)

    def attend(qb):
        s = jnp.einsum('bqhd,bkhd->bhqk', qb, k).astype(jnp.float32)
        p = jax.nn.softmax(s, axis=-1).reshape(B, DIFF_HEADS, 2, Q_BLOCK, T)
        amap = p[:, :, 0] - lam * p[:, :, 1]
        return jnp.einsum('bhqk,bkhd->bqhd', amap.astype(v.dtype), v)

    o = lax.map(attend, q_blocks)
    o = jnp.moveaxis(o, 0, 1).reshape(B, T, DIFF_HEADS, DIFF_V_DIM)
    o = rms_norm(o, subln_g, SUBLN_EPS) * (1.0 - lam_init)
    return o.reshape(B, T, DIFF_WIDTH)

def setup_inputs(seed: int = 0) -> dict:
    key = jax.random.key(seed)
    ks = iter(jax.random.split(key, 40))
    L = DEPTH
    f32 = jnp.float32

    def nrm(shape, scale):
        return scale * jax.random.normal(next(ks), shape, f32)

    def gain(shape):
        return 1.0 + 0.05 * jax.random.normal(next(ks), shape, f32)

    def unif(shape, lo, hi):
        return jax.random.uniform(next(ks), shape, f32, lo, hi)

    return {
        'x': nrm((BATCH, SEQ, D_MODEL), 1.0),
        'ffn1_pre_g': gain((L, D_MODEL)),
        'ffn1_w_gu': nrm((L, D_MODEL, 2 * D_FF), D_MODEL ** -0.5),
        'ffn1_w_down': nrm((L, D_FF, D_MODEL), D_FF ** -0.5),
        'ffn1_post_g': gain((L, D_MODEL)),
        'mix_pre_g': gain((L, D_MODEL)),
        'w_in': nrm((L, D_MODEL, IN_COLS), D_MODEL ** -0.5),
        'mu_prev': unif((L, RWKV_COLS), 0.0, 0.5),
        'mu_next': unif((L, RWKV_COLS), 0.0, 0.5),
        'w0': unif((L, 2, RWKV_WIDTH), -6.0, 0.0),
        'w_up': nrm((L, 2, DECAY_LORA, RWKV_WIDTH), 0.5 * DECAY_LORA ** -0.5),
        'a0': nrm((L, 2, RWKV_WIDTH), 0.1),
        'a_up': nrm((L, 2, AAA_LORA, RWKV_WIDTH), 0.5 * AAA_LORA ** -0.5),
        'g_up': nrm((L, GATE_LORA, RWKV_WIDTH), GATE_LORA ** -0.5),
        'k_k': 0.85 + nrm((L, RWKV_WIDTH), 0.05),
        'k_a': gain((L, RWKV_WIDTH)),
        'r_k': nrm((L, RWKV_HEADS, RWKV_HEAD_DIM), 0.1),
        'gn_w': gain((L, RWKV_WIDTH)),
        'gn_b': nrm((L, RWKV_WIDTH), 0.01),
        'lambda_q1': nrm((L, DIFF_HEAD_DIM), 0.1),
        'lambda_k1': nrm((L, DIFF_HEAD_DIM), 0.1),
        'lambda_q2': nrm((L, DIFF_HEAD_DIM), 0.1),
        'lambda_k2': nrm((L, DIFF_HEAD_DIM), 0.1),
        'subln_g': gain((L, DIFF_V_DIM)),
        'w_branch_a': nrm((L, RWKV_WIDTH, D_MODEL), RWKV_WIDTH ** -0.5),
        'w_branch_b': nrm((L, DIFF_WIDTH, D_MODEL), DIFF_WIDTH ** -0.5),
        'w_out': nrm((L, D_MODEL, D_MODEL), D_MODEL ** -0.5),
        'mix_post_g': gain((L, D_MODEL)),
        'ffn2_pre_g': gain((L, D_MODEL)),
        'ffn2_w_gu': nrm((L, D_MODEL, 2 * D_FF), D_MODEL ** -0.5),
        'ffn2_w_down': nrm((L, D_FF, D_MODEL), D_FF ** -0.5),
        'ffn2_post_g': gain((L, D_MODEL)),
    }

def reference(x, ffn1_pre_g, ffn1_w_gu, ffn1_w_down, ffn1_post_g, mix_pre_g, w_in, mu_prev, mu_next,
              w0, w_up, a0, a_up, g_up, k_k, k_a, r_k, gn_w, gn_b,
              lambda_q1, lambda_k1, lambda_q2, lambda_k2, subln_g,
              w_branch_a, w_branch_b, w_out, mix_post_g,
              ffn2_pre_g, ffn2_w_gu, ffn2_w_down, ffn2_post_g):
    h = x
    col_split = [RWKV_COLS, RWKV_COLS + DIFF_QK_WIDTH, RWKV_COLS + 2 * DIFF_QK_WIDTH,
                 RWKV_COLS + DIFF_COLS, RWKV_COLS + DIFF_COLS + D_MODEL]
    for i in range(DEPTH):
        lam_init = 0.8 - 0.6 * math.exp(-0.3 * i)
        f = swiglu_ffn(rms_norm(h, ffn1_pre_g[i]), ffn1_w_gu[i], ffn1_w_down[i])
        h = h + 0.5 * rms_norm(f, ffn1_post_g[i])
        u = rms_norm(h, mix_pre_g[i])
        proj = u @ w_in[i]
        rw_seg, q, k, v, gate_a, gate_b = jnp.split(proj, col_split, axis=-1)
        rw_seg = centred_token_shift(rw_seg, mu_prev[i], mu_next[i])
        y_a = rwkv7_branch(rw_seg, w0[i], w_up[i], a0[i], a_up[i], g_up[i], k_k[i], k_a[i], r_k[i],
                           gn_w[i], gn_b[i])
        y_b = diff_attention_branch(q, k, v, lambda_q1[i], lambda_k1[i], lambda_q2[i], lambda_k2[i],
                                    subln_g[i], lam_init)
        merged = jax.nn.sigmoid(gate_a) * (y_a @ w_branch_a[i]) + jax.nn.sigmoid(gate_b) * (y_b @ w_branch_b[i])
        h = h + rms_norm(merged @ w_out[i], mix_post_g[i])
        f = swiglu_ffn(rms_norm(h, ffn2_pre_g[i]), ffn2_w_gu[i], ffn2_w_down[i])
        h = h + 0.5 * rms_norm(f, ffn2_post_g[i])
    return h


_drawn_inputs = setup_inputs


def setup_inputs(seed=0):
    import zlib

    import numpy as np

    out = dict(_drawn_inputs(seed))
    spreads = {}
    factors = {'w_up': 5.977,
     'a0': 3.729,
     'k_k': 3.481,
     'gn_w': 3.157,
     'gn_b': 22.609,
     'lambda_q1': 4.061,
     'lambda_k1': 5.992,
     'lambda_q2': 3.209,
     'lambda_k2': 5.507,
     'ffn2_post_g': 3.637,
     'subln_g': 2.808}
    for name, (base, spread) in spreads.items():
        noise = np.random.default_rng([zlib.crc32(name.encode()), seed]).standard_normal(out[name].shape)
        drawn = base * np.exp(spread * noise) if base else spread * noise
        out[name] = __import__('jax').numpy.asarray(drawn.astype(out[name].dtype))
    for name, factor in factors.items():
        out[name] = (out[name] * factor).astype(out[name].dtype)
    return out
```

```python
import math
from contextlib import ExitStack

import numpy as np

import concourse.bass as bass
from concourse import mybir

F32 = mybir.dt.float32
F32R = mybir.dt.float32r
ALU = mybir.AluOpType
ACT = mybir.ActivationFunctionType
AX = mybir.AxisListType

P = 128
D = 2048
T = 256
NT = T // P
KB = D // P
FF = ((8 * D // 3 + 255) // 256) * 256
CW = 512
RING = 4
SB = 2
FFC = FF // CW
FF_GROUPS = ((0, 6), (6, FFC))
NPAIR = 8
NH = 16
RW = 1024
LORA = 64
GLORA = 160
RCOLS = 3 * RW + 4 * LORA + GLORA
DCOLS = 3 * 1024
NBLK = -(-RCOLS // P)
C = 64
NC_ = T // C
NM = 2 * NPAIR
EPS = 1e-6
GN_EPS = 64e-5
SUBLN_EPS = 1e-5
LAM_INIT = 0.8 - 0.6 * math.exp(-0.3 * 0)
DECAY = math.exp(-0.5)
QSLOTS = 1 + NM * 3 * NC_ + 2 * NC_
K_ID, K_SEL, K_HEAD, K_MN, K_M1, K_MG, K_RESET, K_COS, K_SIN, K_END = np.cumsum(
    [0, P, P, P, C, 4 * C, P, T, 2 * 32, 2 * 32]).tolist()
BLOCKS = list(range(24, NBLK)) + list(range(24))
D_MU, D_W0, D_A0, D_KA, D_KA1, D_SUB = 0, 28, 44, 60, 68, 76
R_F1, R_MIX, R_F2, R_MUP, R_MUN, R_W0 = 0, 16, 32, 48, 76, 104
R_A0, R_KK, R_KA, R_RK, R_GNW, R_GNB, R_SUB = 128, 144, 152, 160, 168, 176, 184


def constants():
    k = np.zeros((P, K_END), np.float32)
    p = np.arange(P)[:, None]
    t = np.arange(C)[None, :]
    k[:, K_ID:K_SEL] = np.eye(P)
    bh = np.arange(P)[None, :]
    k[:, K_SEL:K_HEAD] = (bh % NH == 2 * (bh // NH) + p // C)
    k[:, K_HEAD:K_MN] = (p // C == bh // C)
    s = p % C
    k[:, K_MN:K_M1] = -1.0 * (s < t)
    k[:, K_M1:K_MG] = np.concatenate([s <= t, s >= -1 + 0 * t, s >= -1 + 0 * t, t < s], 1)
    k[:, K_MG:K_RESET] = np.concatenate([(p < C) | (s <= t), s >= -1 + 0 * t], 1)
    k[:, K_RESET:K_COS] = (np.arange(T) % C != 0)[None, :]
    inv = np.float32(10000.0) ** (-np.arange(32, dtype=np.float32) / np.float32(32))
    ang = np.arange(T, dtype=np.float32)[:, None] * inv.astype(np.float32)[None, :]
    for i in range(NT):
        k[:, K_COS + 32 * i:K_COS + 32 * (i + 1)] = np.cos(ang[i * P:(i + 1) * P])
        k[:, K_SIN + 32 * i:K_SIN + 32 * (i + 1)] = np.sin(ang[i * P:(i + 1) * P])
    sel_t = (np.arange(NH)[:, None] == (2 * np.arange(NPAIR)[:, None] + np.arange(P)[None, :] // C).reshape(1, -1))
    return k, sel_t.astype(np.float32)


def layer(nc, a, out):
    x, w_in, mix_post_g, w_up, a_up, g_up, w_branch_a, w_branch_b, w_out, consts, sel_t = (
        a[n] for n in ("x", "w_in", "mix_post_g", "w_up", "a_up", "g_up", "w_branch_a", "w_branch_b", "w_out",
                       "consts", "sel_t"))
    ffn = [(a[f"ffn{i}_pre_g"], a[f"ffn{i}_w_gu"], a[f"ffn{i}_w_down"], a[f"ffn{i}_post_g"]) for i in (1, 2)]

    def rows(v):
        return v.rearrange("(b p) -> b p", p=P)

    def by_direction(v):
        return v.rearrange("d (b p) -> (d b) p", p=P)

    whole = (NBLK - 1) * P
    VECTORS = [(rows(ffn[0][0][0]), R_F1, 16), (rows(a["mix_pre_g"][0]), R_MIX, 16), (rows(ffn[1][0][0]), R_F2, 16),
               (rows(a["mu_prev"][0, 0:whole]), R_MUP, NBLK - 1), (a["mu_prev"][0:1, whole:RCOLS], R_MUP + NBLK - 1, 1),
               (rows(a["mu_next"][0, 0:whole]), R_MUN, NBLK - 1), (a["mu_next"][0:1, whole:RCOLS], R_MUN + NBLK - 1, 1),
               (by_direction(a["w0"][0]), R_W0, 16), (by_direction(a["a0"][0]), R_A0, 16), (rows(a["k_k"][0]), R_KK, 8),
               (rows(a["k_a"][0]), R_KA, 8), (a["r_k"][0].rearrange("(b h) p -> b (h p)", h=2), R_RK, 8),
               (rows(a["gn_w"][0]), R_GNW, 8), (rows(a["gn_b"][0]), R_GNB, 8), (a["subln_g"], R_SUB, 1)]
    N_VEC = len(VECTORS)

    class Pass:

        def __init__(self, chunks, slots, unroll, width, source):
            self.n0, self.q0 = Pass.n, Pass.q
            self.chunks, self.slots, self.unroll, self.width, self.source = chunks, slots, unroll, width, source
            self.turns = chunks // unroll
            assert chunks % unroll == 0
            Pass.n += chunks * slots
            Pass.q += chunks
            assert self.turns == 1 or (unroll * slots % RING == 0 and unroll % 2 == 0)

        def end(self, i, u):
            return self.n0 + (i * self.unroll + u + 1) * self.slots

        def uses(self, i, u):
            return (self.q0 + i * self.unroll + u) // 2 if isinstance(i, int) else \
                i * (self.unroll // 2) + (self.q0 + u) // 2

        def pair(self, u):
            return (self.q0 + u) % 2

    Pass.n = Pass.q = 0

    def rows_cols(w, r0, j, c0, width):
        return w[r0 + j * SB * P:r0 + (j + 1) * SB * P, bass.ds(c0, width)].rearrange("(k p) n -> p k n", p=P)

    def gate_up(wgu, f0):
        return lambda i, u, j: rows_cols(wgu, 0, j, u * FF + (f0 + i) * CW, CW)

    def down(wd, f0):
        return lambda i, u, j: rows_cols(wd, f0 * CW, j, (2 * i + u) * CW, CW)

    def make_ffn(w):
        ps = []
        for f0, f1 in FF_GROUPS:
            ps.append((Pass(2 * (f1 - f0), KB // SB, 2, CW, gate_up(w[1][0], f0)),
                       Pass(D // CW, (f1 - f0) * CW // (SB * P), 2, CW, down(w[2][0], f0))))
        return ps

    wi = w_in[0]
    ffn1 = make_ffn(ffn[0])
    p_rw = Pass(6, 8, 2, CW, lambda i, u, j: rows_cols(wi, 0, j, (2 * i + u) * CW, CW))
    p_rw7 = Pass(1, 8, 1, RCOLS - 6 * CW, lambda i, u, j: rows_cols(wi, 0, j, 6 * CW, RCOLS - 6 * CW))
    p_dif = Pass(6, 8, 2, CW, lambda i, u, j: rows_cols(wi, 0, j, RCOLS + (2 * i + u) * CW, CW))
    p_gate = Pass(8, 8, 2, CW, lambda i, u, j: rows_cols(wi, 0, j, RCOLS + DCOLS + (2 * i + u) * CW, CW))
    p_br = Pass(8, 4, 2, CW, lambda i, u, j: rows_cols((w_branch_a[0], w_branch_b[0])[u], 0, j, i * CW, CW))
    p_out = Pass(4, 8, 2, CW, lambda i, u, j: rows_cols(w_out[0], 0, j, (2 * i + u) * CW, CW))
    ffn2 = make_ffn(ffn[1])
    passes = [p for g in ffn1 for p in g] + [p_rw, p_rw7, p_dif, p_gate, p_br, p_out] + [p for g in ffn2 for p in g]

    def scratch(name, shape):
        return nc.dram_tensor(name, shape, F32).ap()

    h_dram = scratch("h_dram", (T, D))
    dif_dram = scratch("dif_dram", (T, DCOLS))
    gate_dram = scratch("gate_dram", (T, 2 * D))
    v_dram = scratch("v_dram", (NPAIR, P, T))
    g_dram = scratch("g_dram", (NPAIR, P, T))
    bonus_dram = scratch("bonus_dram", (NPAIR, P, T))
    n_dram = scratch("n_dram", (2, NM, NC_, C, C))
    z_dram = scratch("z_dram", (2, NM, NC_, C, C))

    ctx = ExitStack()
    with ctx:
        def sem(name):
            return ctx.enter_context(nc.semaphore(name))

        def sb(scope, name, shape, dt=F32):
            return scope.enter_context(nc.sbuf_tensor(name, shape, dt))

        ps = ctx.enter_context(nc.psum_tensor("ps", [P, 8, 512], F32))

        kc = sb(ctx, "kc", [P, K_END])
        vec = sb(ctx, "vec", [P, 256])
        seltA = sb(ctx, "seltA", [NH, NPAIR * P])
        sm = sb(ctx, "sm", [P, 64])
        vecd = sb(ctx, "vecd", [P, 80])
        dg = sb(ctx, "dg", [P, NT, P])
        raw = sb(ctx, "raw", [P, RING, SB, CW])
        whi = sb(ctx, "whi", [P, RING, SB, CW], F32R)
        wlo = sb(ctx, "wlo", [P, RING, SB, CW], F32R)
        uhi = sb(ctx, "uhi", [P, KB, T], F32R)
        ulo = sb(ctx, "ulo", [P, KB, T], F32R)
        ident = kc[:, K_ID:K_SEL]
        headsum = kc[:, K_HEAD:K_MN]

        def room(*names):
            scope = ExitStack()
            tiles = [sb(scope, *n) for n in names]
            return scope, tiles

        def ffn_room(tag):
            return room(("h" + tag, [P, NT, D]), ("f" + tag, [P, NT, D]),
                        ("hthi" + tag, [P, 24, T], F32R), ("htlo" + tag, [P, 24, T], F32R),
                        ("sg" + tag, [P, NT, CW]), ("hm" + tag, [P, NT, CW]), ("gain" + tag, [P, D]))

        s1, F1 = ffn_room("1")
        vrows = F1[1]
        s1.close()
        s_proj, (proj, ybuf, vst, dst_a) = room(
            ("proj", [P, NT, NBLK * P]), ("ybuf", [P, 2, T + 2]), ("vst", [P, 2, T]), ("dst_a", [P, 2, NT, CW]))
        s_proj.close()
        s_q, (q, beta, pend) = room(("q", [P, QSLOTS, C]), ("beta", [P, NM, T]), ("pend", [P, NM, NC_]))
        s_rk, (rr, kr, kkn, wup, aup, lwa) = room(
            ("rr", [P, NPAIR, T]), ("kr", [P, NPAIR, T]), ("kkn", [P, NPAIR, T]),
            ("wup", [P, RW]), ("aup", [P, RW]), ("lwa", [P, 2, T]))
        s_g, (lgd, gupa, gupb, sqb, s16, gst) = room(
            ("lgd", [P, 2, T]), ("gupa", [P, RW]), ("gupb", [GLORA - P, RW]), ("sqb", [P, 2, T]),
            ("s16", [NH, 2, T]), ("gst", [P, 2, T]))
        s_g.close()
        s_e, (tz, ie, eie, ld, aa, kd, kds, nst, bst, vb1) = room(
            ("tz", [P, 2, T]), ("ie", [P, 2, T]), ("eie", [P, 3, T]), ("ld", [P, T]), ("aa", [P, T]), ("kd", [P, T]),
            ("kds", [P, T]), ("nst", [P, 2, NC_, C]), ("bst", [P, T]), ("vb1", [P, T]))
        s_e.close()
        s_rk.close()
        s_z, (z, zt, gst_g) = room(("z", [P, C, C]), ("zt", [P, 32 * 32]), ("gst_g", [P, 2, NT, CW]))
        s_z.close()
        s_r, (zs, oc, vb, vrev, mb, wt, gh, sv) = room(
            ("zs", [P, NM * NC_, C]), ("oc", [P, NPAIR, T]), ("vb", [P, T]), ("vrev", [P, T]), ("mb", [P, 2, NC_, 4 * C]),
            ("wt", [P, 2, NC_, 2 * C]), ("gh", [P, 2, 2 * NC_, 2 * C]), ("sv", [P, 2, NC_, 2 * C]))
        s_r.close()
        s_q.close()
        s_y, (ythi, ytlo) = room(("ythi", [P, 16, T], F32R), ("ytlo", [P, 16, T], F32R))
        s_n, (osq, o16, bo, gg) = room(
            ("osq", [P, 2, T]), ("o16", [NH, 4, T]), ("bo", [P, NPAIR, T]), ("gg", [P, NPAIR, T]))
        s_n.close()
        s_t, (qk, va, ra, rb, qt_, kt_, lamv, lamb, mx, su, pex, am, amt, ov, oj, os_) = room(
            ("qk", [P, NT, 2 * RW]), ("va", [P, NT, RW]), ("ra", [P, RW]), ("rb", [P, RW]), ("qt_", [P, 8, T]),
            ("kt_", [P, 8, T]), ("lamv", [P, 4, 64]), ("lamb", [P, 8]), ("mx", [P, 4, 2]), ("su", [P, 4, 2]),
            ("pex", [P, 4, 2, T]), ("am", [P, 4, T]), ("amt", [P, 4, T]), ("ov", [P, 4, P]), ("oj", [P, 4, P]),
            ("os_", [P, 16]))
        s_t.close()
        s_m, (gbuf, mg, mt) = room(("gbuf", [P, 2, 2, NT, CW]), ("mg", [P, NT, D]), ("mt", [P, NT, CW]))
        s_m.close()
        s_y.close()
        s2, F2 = ffn_room("2")
        s2.close()

        landed = [sem(f"landed{s}") for s in range(RING)]
        hi_ready = sem("hi_ready")
        lo_ready = sem("lo_ready")
        slots_used = sem("slots_used")
        pair_free = [sem("pair_free0"), sem("pair_free1")]
        act_link, dve_link, pool_link = sem("act_link"), sem("dve_link"), sem("pool_link")
        c_in, x_in, vr_in, sel_in, par_in = (sem(n) for n in ("c_in", "x_in", "vr_in", "sel_in", "par_in"))
        vr_zero, vec_t, vec_copied, vec_ready = (sem(n) for n in ("vr_zero", "vec_t", "vec_copied", "vec_ready"))
        ss_ready, ms_ready, rstd_ready, diag_ready = (sem(n) for n in ("ss_ready", "ms_ready", "rstd_ready", "diag_ready"))
        ut_done, ut_hi, ut_lo = sem("ut_done"), sem("ut_hi"), sem("ut_lo")
        hm_t, ht_hi, ht_lo = sem("hm_t"), sem("ht_hi"), sem("ht_lo")
        gain_in, h_ready, h_saved, h_back, out_done = (sem(n) for n in ("gain_in", "h_ready", "h_saved", "h_back", "out_done"))
        st_out = [sem("st_out0"), sem("st_out1")]
        sh_t, sh_y, shifted, v_out0, v_out1 = (sem(n) for n in ("sh_t", "sh_y", "shifted", "v_out0", "v_out1"))
        lora_act, gd_ready = sem("lora_act"), sem("gd_ready")
        kk_raw, kk_sq, kk_sum, kk_max, kk_sqrt, kk_rec, kk_bc, kk_ready = (
            sem(n) for n in ("kk_raw", "kk_sq", "kk_sum", "kk_max", "kk_sqrt", "kk_rec", "kk_bc", "kk_ready"))
        g_mm, g_st = sem("g_mm"), sem("g_st")
        g_out = [sem("g_out0"), sem("g_out1")]
        za_mm, za_act, ex_in, ex_out, aa_ready, ra_ready, q_ready = (
            sem(n) for n in ("za_mm", "za_act", "ex_in", "ex_out", "aa_ready", "ra_ready", "q_ready"))
        bon_in, bon_mm, bon_st, bon_out, v1_in = (sem(n) for n in ("bon_in", "bon_mm", "bon_st", "bon_out", "v1_in"))
        n_mm, n_st, z_in, z_done, z_out, zs_in = (sem(n) for n in ("n_mm", "n_st", "z_in", "z_done", "z_out", "zs_in"))
        n_out = [sem("n_out0"), sem("n_out1")]
        vb_in = sem("vb_in")
        sv_zero, dd_ready, vt_mm, vt_ready, ab_mm, ab_ready, w_mm, w_ready, gh_mm, gh_ready = (
            sem(n) for n in ("sv_zero", "dd_ready", "vt_mm", "vt_ready", "ab_mm", "ab_ready", "w_mm", "w_ready",
                             "gh_mm", "gh_ready"))
        s_mm, s_ready, o_mm, o_ready = sem("s_mm"), sem("s_ready"), sem("o_mm"), sem("o_ready")
        gn_sum, gn_mean, gn_bc, gn_cent, gn_sq, gn_var, gn_varv, gn_sqrt, gn_rec, gn_bc2, gn_in, ya_y, ya_hi, ya_lo = (
            sem(n) for n in ("gn_sum", "gn_mean", "gn_bc", "gn_cent", "gn_sq", "gn_var", "gn_varv", "gn_sqrt",
                             "gn_rec", "gn_bc2", "gn_in", "ya_y", "ya_hi", "ya_lo"))
        at_in, lam_sum, lam_exp, lam_ready, roped, qt_mm, qt_ready = (
            sem(n) for n in ("at_in", "lam_sum", "lam_exp", "lam_ready", "roped", "qt_mm", "qt_ready"))
        sc_mm, mx_ready, ex_p, am_ready, am_t, amt_ready, pv_mm, pv_sq, pv_ms, pv_rs, yb_ready, yb_t, yb_hi, yb_lo = (
            sem(n) for n in ("sc_mm", "mx_ready", "ex_p", "am_ready", "am_t", "amt_ready", "pv_mm", "pv_sq", "pv_ms",
                             "pv_rs", "yb_ready", "yb_t", "yb_hi", "yb_lo"))
        vr_ready = sem("vr_ready")
        gt_in = [sem("gt_in0"), sem("gt_in1")]
        mg_ready = sem("mg_ready")

        SS = {e: slice(6 * e, 6 * e + 2) for e in range(6)}
        MS = {e: slice(6 * e + 2, 6 * e + 4) for e in range(6)}
        RS = {e: slice(6 * e + 4, 6 * e + 6) for e in range(6)}
        HALF = slice(40, 48)

        def slot_of(p, u, j):
            return (p.n0 + u * p.slots + j) % RING

        def walk(eng, p, slot, hooks=(), carried=(), skip=0):
            def turn(i, first):
                for k in range(p.unroll * p.slots):
                    if not (first and k < skip):
                        slot(p.n0 + i * (p.unroll * p.slots) + k, i, k // p.slots, k % p.slots)
                    for at, fn in carried if first else ():
                        if at == k:
                            fn()
                    for at, lag, fn in hooks:
                        if at == k and not (first and lag):
                            fn(i - lag)
            turn(0, True)
            if p.turns > 1:
                with eng.Fori(1, p.turns) as i:
                    turn(i, False)
            return [(at, (lambda fn=fn: fn(p.turns - 1))) for at, lag, fn in hooks if lag]

        def each_chunk(p, fn):
            if p.unroll == 1:
                return [(3, 1, lambda i: fn(i, 0))]
            return [(3, 1, lambda i: fn(i, 1)), (p.slots + 3, 0, lambda i: fn(i, 0))]

        def ut_base(e):
            return KB * e

        block = ctx.enter_context(nc.Block())

        @block.sync
        def _(sp):
            for p in passes:
                def load(n, i, u, j, p=p):
                    s = slot_of(p, u, j)
                    if not (isinstance(n, int) and n < RING):
                        sp.wait_ge(lo_ready, n - RING + 1)
                    sp.dma_start(raw[:, s, :, 0:p.width], p.source(i, u, j)).then_inc(landed[s], 16)
                walk(sp, p, load)

        @block.scalar
        def _(act):
            links = [0]

            def link(ins):
                links[0] += 1
                ins.then_inc(act_link, 1)
                act.wait_ge(act_link, links[0])

            def split_hi(p):
                def slot(n, i, u, j):
                    s = slot_of(p, u, j)
                    k = p.n0 + u * p.slots + j
                    act.wait_ge(landed[s], i * (16 * p.unroll * p.slots // RING) + 16 * (k // RING + 1))
                    if not (isinstance(n, int) and n < RING):
                        act.wait_ge(slots_used, n - RING + 1)
                    nc.scalar.activation(whi[:, s, :, 0:p.width], raw[:, s, :, 0:p.width], ACT.Copy).then_inc(hi_ready, 1)
                return slot

            def ahead(p):
                for k in range(RING):
                    split_hi(p)(p.n0 + k, 0, 0, k)

            def sum_squares(e, src, junk):
                for t in range(NT):
                    nc.scalar.activation(junk, src[:, t, :], ACT.Square,
                                         accum_out=sm[:, 6 * e + t:6 * e + t + 1]).then_inc(ss_ready, 1)
                    if t + 1 < NT:
                        act.wait_ge(ss_ready, NT * e + t + 1)

            def transposed_hi(e, col):
                for k in range(KB):
                    act.wait_ge(ut_done, ut_base(e) + k + 1)
                    bank = ps[:, 4 + k % 4, 0:T]
                    if col is None:
                        nc.scalar.activation(uhi[:, k, :], bank, ACT.Copy).then_inc(ut_hi, 1)
                    else:
                        nc.scalar.activation(uhi[:, k, :], bank, ACT.Identity,
                                             scale=vec[:, col + k:col + k + 1]).then_inc(ut_hi, 1)

            def feed_forward(w, F, groups, post, pre_split):
                h, f, hthi, htlo, sg, hm, gain = F

                def group(g, gu, dn, carried):
                    f0, f1 = FF_GROUPS[g]
                    fb = w * FFC + f0

                    def silu(i):
                        if not (isinstance(i, int) and gu.uses(i, 1) == 0):
                            act.wait_ge(pair_free[gu.pair(1)], gu.uses(i, 1))
                        act.wait_ge(slots_used, gu.end(i, 0))
                        for t in range(NT):
                            last = nc.scalar.activation(sg[:, t, :], ps[:, 2 * gu.pair(0) + t, :], ACT.Silu)
                        last.then_inc(pair_free[gu.pair(0)], 1)

                    def h_hi(i):
                        for b in range(2):
                            act.wait_ge(hm_t, 2 * (fb + i) + b + 1)
                            nc.scalar.activation(hthi[:, bass.ds(4 * i + 2 * b, 2), :],
                                                 ps[:, 4 + b, :].rearrange("p (k t) -> p k t", k=2),
                                                 ACT.Copy).then_inc(ht_hi, 1)

                    carried = walk(act, gu, split_hi(gu), [(9, 1, h_hi), (11, 0, silu)], carried,
                                   skip=RING if g == 0 and pre_split else 0)
                    carried = walk(act, dn, split_hi(dn), [], carried)
                    return carried

                carried = []
                for g, (gu, dn) in enumerate(groups):
                    carried = group(g, gu, dn, carried)
                last = groups[-1][1]
                act.wait_ge(pair_free[last.pair(1)], last.uses(last.turns - 1, 1) + 1)

            act.dma_start(kc[:, :], consts).then_inc(c_in, 16)
            act.dma_start(F1[0][:, :, :], x[0].rearrange("(t p) d -> p t d", p=P)).then_inc(x_in, 16)
            act.dma_start(seltA[:, :], sel_t).then_inc(sel_in, 16)
            ahead(passes[0])
            act.wait_ge(x_in, 16)
            junk1 = F1[2][:, 0:8, :].rearrange("p k t -> p (k t)")
            junk2 = F2[2][:, 0:8, :].rearrange("p k t -> p (k t)")
            sum_squares(0, F1[0], junk1)
            act.wait_ge(vec_t, 1)
            nc.scalar.activation(vec[:, :], ps[:, 4, 0:256], ACT.Copy).then_inc(vec_copied, 1)
            act.wait_ge(vec_copied, 1)
            transposed_hi(0, R_F1)
            feed_forward(0, F1, ffn1, 1, True)
            ahead(p_rw)
            sum_squares(1, F1[1], junk1)
            act.wait_ge(h_ready, NT)
            act.wait_ge(ss_ready, NT * 2)
            sum_squares(2, F1[0], junk1)
            transposed_hi(1, R_MIX)

            def to_proj(p, c0):
                def fn(i, u):
                    act.wait_ge(slots_used, p.end(i, u))
                    for t in range(NT):
                        last = nc.scalar.activation(proj[:, t, bass.ds((p.unroll * i + u) * CW + c0, p.width)],
                                                    ps[:, 2 * p.pair(u) + t, 0:p.width], ACT.Copy)
                    last.then_inc(pair_free[p.pair(u)], 1)
                return fn

            def to_stage(p, tile, func, before):
                def fn(i, u):
                    act.wait_ge(slots_used, p.end(i, u))
                    b = p.pair(u)
                    if not (isinstance(i, int) and i + before == 0):
                        act.wait_ge(st_out[b], 16 * i + 16 * before)
                    for t in range(NT):
                        last = nc.scalar.activation(tile[:, b, t, :], ps[:, 2 * b + t, :], func)
                    last.then_inc(pair_free[b], 1)
                return fn

            act.wait_ge(h_saved, 16)
            carried = walk(act, p_rw, split_hi(p_rw), each_chunk(p_rw, to_proj(p_rw, 0)), (), skip=RING)
            carried = walk(act, p_rw7, split_hi(p_rw7), each_chunk(p_rw7, to_proj(p_rw7, 6 * CW)), carried)
            carried = walk(act, p_dif, split_hi(p_dif), each_chunk(p_dif, to_stage(p_dif, dst_a, ACT.Copy, 0)), carried)
            for _, fn in carried:
                fn()
            ahead(p_gate)

            for n in range(NBLK):
                w = 32 if BLOCKS[n] == NBLK - 1 else P
                act.wait_ge(sh_t, n + 1)
                if n >= 2:
                    act.wait_ge(shifted, n - 1)
                nc.scalar.activation(ybuf[0:w, n % 2, 1:T + 1], ps[0:w, 4 + n % 4, 0:T], ACT.Copy).then_inc(sh_y, 1)
            act.wait_ge(shifted, 4)
            nc.scalar.activation(lwa[:, 0, :], lwa[:, 0, :], ACT.Tanh).then_inc(lora_act, 1)
            act.wait_ge(shifted, NBLK)
            nc.scalar.activation(lgd[:, 0, :], lgd[:, 0, :], ACT.Tanh, scale=0.5)
            nc.scalar.activation(lgd[0:32, 1, :], lgd[0:32, 1, :], ACT.Tanh, scale=0.5).then_inc(lora_act, 1)
            for b in range(NPAIR):
                nc.scalar.activation(kkn[:, b, :], kr[:, b, :], ACT.Identity,
                                     scale=vec[:, R_KK + b:R_KK + b + 1]).then_inc(kk_raw, 1)
                act.wait_ge(kk_raw, b + 1)
                if b >= 2:
                    act.wait_ge(kk_sum, b - 1)
                nc.scalar.activation(sqb[:, b % 2, :], kkn[:, b, :], ACT.Square).then_inc(kk_sq, 1)
            act.wait_ge(kk_max, 1)
            nc.scalar.activation(s16[:, 1, :], s16[:, 0, :], ACT.Sqrt).then_inc(kk_sqrt, 1)
            for b in range(NPAIR):
                act.wait_ge(g_mm, b + 1)
                if b >= 2:
                    act.wait_ge(g_out[b % 2], 16 * (b // 2))
                nc.scalar.activation(gst[:, b % 2, :], ps[:, 4 + b % 2, 0:T], ACT.Copy).then_inc(g_st, 1)
            act.wait_ge(kk_ready, NPAIR)
            act.wait_ge(g_out[0], 16 * (NPAIR // 2))
            act.wait_ge(g_out[1], 16 * (NPAIR // 2))
            for m in range(NM):
                b, d = m // 2, m % 2
                act.wait_ge(za_mm, m + 1)
                if m:
                    act.wait_ge(aa_ready, m)
                for w, col in ((0, D_W0), (1, D_A0)):
                    last = nc.scalar.activation(tz[:, w, :], ps[:, 4 + m % 2, w * T:(w + 1) * T], ACT.Tanh, scale=0.5,
                                                bias=vecd[:, col + 8 * d + b:col + 8 * d + b + 1])
                last.then_inc(za_act, 1)
                act.wait_ge(ex_in, m + 1)
                if m:
                    act.wait_ge(q_ready, m)
                    act.wait_ge(ra_ready, 2 * m)
                nc.scalar.activation(eie[:, 0:2, :], ie[:, :, :], ACT.Exp)
                nc.scalar.activation(eie[:, 2, :], ie[:, 0, :], ACT.Exp, scale=-1.0).then_inc(ex_out, 1)

            carried = walk(act, p_gate, split_hi(p_gate), each_chunk(p_gate, to_stage(p_gate, gst_g, ACT.Sigmoid, 3)), (), skip=RING)
            for _, fn in carried:
                fn()
            ahead(p_br)

            act.wait_ge(zs_in, 32)
            for b in range(2):
                act.wait_ge(st_out[b], 16 * 7)

            def values(m):
                act.wait_ge(vt_mm, m + 1)
                if m >= 2:
                    act.wait_ge(o_mm, m - 1)
                nc.scalar.activation(sv[C:P, m % 2, :, :], ps[C:P, 2, :].rearrange("p (c v) -> p c v", c=NC_),
                                     ACT.Copy).then_inc(vt_ready, 1)

            def minus_w(m):
                act.wait_ge(w_mm, m + 1)
                nc.scalar.activation(wt[:, m % 2, :, :], ps[:, 3, :].rearrange("p (c v) -> p c v", c=NC_),
                                     ACT.Copy, scale=-1.0).then_inc(w_ready, 1)

            values(0)
            minus_w(0)
            for m in range(NM):
                for c in range(NC_ - 1):
                    act.wait_ge(s_mm, 3 * m + c + 1)
                    nc.scalar.activation(sv[0:C, m % 2, c + 1, :], ps[0:C, 6, 0:2 * C], ACT.Copy).then_inc(s_ready, 1)
                if m + 1 < NM:
                    values(m + 1)
                    minus_w(m + 1)
            for b in range(NPAIR):
                act.wait_ge(gn_cent, b + 1)
                if b >= 2:
                    act.wait_ge(gn_var, b - 1)
                nc.scalar.activation(osq[:, b % 2, :], oc[:, b, :], ACT.Square).then_inc(gn_sq, 1)
            act.wait_ge(gn_varv, 1)
            nc.scalar.activation(o16[:, 2, :], o16[:, 1, :], ACT.Sqrt).then_inc(gn_sqrt, 1)
            for b in range(NPAIR):
                act.wait_ge(ya_y, b + 1)
                nc.scalar.activation(ythi[:, b, :], oc[:, b, :], ACT.Copy).then_inc(ya_hi, 1)

            act.wait_ge(lam_sum, 1)
            nc.scalar.activation(lamb[:, 2:4], lamb[:, 0:2], ACT.Exp).then_inc(lam_exp, 1)
            for n in range(16):
                act.wait_ge(qt_mm, n + 1)
                dst = (qt_, kt_)[n // 8][:, n % 8, :]
                nc.scalar.activation(dst, ps[:, 4 + n % 4, 0:T], ACT.Copy).then_inc(qt_ready, 1)
            for g in range(4):
                for v in range(4):
                    w = 4 * g + v
                    act.wait_ge(mx_ready, 2 * g + v // 2 + 1)
                    if g:
                        act.wait_ge(am_ready, w - 3)
                    for s in range(2):
                        last = nc.scalar.activation(pex[:, v, s, :], ps[:, 2 * (v // 2) + s, (v % 2) * T:(v % 2 + 1) * T], ACT.Exp, scale=0.125,
                                                    bias=mx[:, v, s:s + 1], accum_out=su[:, v, s:s + 1])
                    last.then_inc(ex_p, 1)
                for v2 in range(2):
                    act.wait_ge(am_t, 2 * g + v2 + 1)
                    if g:
                        act.wait_ge(pv_mm, g)
                    nc.scalar.activation(amt[:, 2 * v2:2 * v2 + 2, :], ps[:, 4 + v2, :].rearrange("p (v t) -> p v t", v=2),
                                         ACT.Copy).then_inc(amt_ready, 1)
                act.wait_ge(pv_mm, g + 1)
                if g:
                    act.wait_ge(pv_ms, g)
                    act.wait_ge(pv_sq, g)
                for v in range(4):
                    last = nc.scalar.activation(oj[:, v, :], ps[:, 6, v * P:(v + 1) * P], ACT.Square,
                                                accum_out=os_[:, v:v + 1])
                last.then_inc(pv_sq, 1)
                act.wait_ge(yb_t, g + 1)
                hs, t = 4 * (g % 2), g // 2
                nc.scalar.activation(ythi[:, 8 + hs:12 + hs, t * P:(t + 1) * P],
                                     ps[:, 7, :].rearrange("p (v t) -> p v t", v=4), ACT.Identity,
                                     scale=vecd[:, D_SUB:D_SUB + 1]).then_inc(yb_hi, 1)

            walk(act, p_br, split_hi(p_br), [], (), skip=RING)
            ahead(p_out)
            transposed_hi(2, None)
            walk(act, p_out, split_hi(p_out), [], (), skip=RING)
            ahead(ffn2[0][0])
            act.wait_ge(pair_free[p_out.pair(1)], p_out.uses(1, 1) + 1)
            sum_squares(3, F2[1], junk2)
            act.wait_ge(h_ready, NT * 2)
            act.wait_ge(ss_ready, NT * 4)
            sum_squares(4, F2[0], junk2)
            transposed_hi(3, R_F2)
            feed_forward(1, F2, ffn2, 5, True)
            sum_squares(5, F2[1], junk2)

        @block.vector
        def _(dve):
            links = [0]

            def link(ins):
                links[0] += 1
                ins.then_inc(dve_link, 1)
                dve.wait_ge(dve_link, links[0])

            V = nc.vector

            def split_lo(p):
                def slot(n, i, u, j):
                    s = slot_of(p, u, j)
                    dve.wait_ge(hi_ready, n + 1)
                    V.tensor_tensor(wlo[:, s, :, 0:p.width], raw[:, s, :, 0:p.width],
                                    whi[:, s, :, 0:p.width].bitcast(F32), ALU.subtract).then_inc(lo_ready, 1)
                return slot

            def ahead(p):
                for k in range(RING):
                    split_lo(p)(p.n0 + k, 0, 0, k)

            def mean_square(e, eps):
                dve.wait_ge(ss_ready, NT * (e + 1))
                V.tensor_scalar(sm[:, MS[e]], sm[:, SS[e]], 1.0 / D, eps, ALU.mult, ALU.add).then_inc(ms_ready, 1)

            def diagonal(e, k):
                dve.wait_ge(rstd_ready, e + 1)
                dve.wait_ge(c_in, 16)
                for t in range(NT):
                    last = V.tensor_scalar(dg[:, t, :], ident, sm[:, 6 * e + 4 + t:6 * e + 5 + t], None, ALU.mult)
                last.then_inc(diag_ready, 1)

            def transposed_lo(e, col):
                for k in range(KB):
                    dve.wait_ge(ut_hi, ut_base(e) + k + 1)
                    bank, hi = ps[:, 4 + k % 4, 0:T], uhi[:, k, :].bitcast(F32)
                    if col is None:
                        V.tensor_tensor(ulo[:, k, :], bank, hi, ALU.subtract).then_inc(ut_lo, 1)
                    else:
                        V.scalar_tensor_tensor(out=ulo[:, k, :], in0=bank, scalar=vec[:, col + k:col + k + 1], in1=hi,
                                               op0=ALU.mult, op1=ALU.subtract).then_inc(ut_lo, 1)

            def post_norm(e, nth, F, weight):
                h, f, gain = F[0], F[1], F[6]
                dve.wait_ge(rstd_ready, e + 1)
                dve.wait_ge(gain_in, 16 * (nth + 1))
                for t in range(NT):
                    link(V.scalar_tensor_tensor(out=f[:, t, :], in0=f[:, t, :], scalar=sm[:, 6 * e + 4 + t:6 * e + 5 + t],
                                                in1=gain[:, :], op0=ALU.mult, op1=ALU.mult))
                    V.scalar_tensor_tensor(out=h[:, t, :], in0=f[:, t, :], scalar=weight, in1=h[:, t, :],
                                           op0=ALU.mult, op1=ALU.add).then_inc(h_ready, 1)

            def feed_forward(w, F, groups):
                h, f, hthi, htlo, sg, hm, gain = F

                def group(g, gu, dn, carried):
                    f0, f1 = FF_GROUPS[g]
                    fb = w * FFC + f0

                    def times_up(i):
                        dve.wait_ge(pair_free[gu.pair(0)], gu.uses(i, 0) + 1)
                        dve.wait_ge(slots_used, gu.end(i, 1))
                        for t in range(NT):
                            last = V.tensor_tensor(hm[:, t, :], sg[:, t, :], ps[:, 2 * gu.pair(1) + t, :], ALU.mult)
                        last.then_inc(pair_free[gu.pair(1)], 1)

                    def h_lo(i):
                        for b in range(2):
                            dve.wait_ge(ht_hi, 2 * (fb + i) + b + 1)
                            V.tensor_tensor(htlo[:, bass.ds(4 * i + 2 * b, 2), :],
                                            ps[:, 4 + b, :].rearrange("p (k t) -> p k t", k=2),
                                            hthi[:, bass.ds(4 * i + 2 * b, 2), :].bitcast(F32),
                                            ALU.subtract).then_inc(ht_lo, 1)

                    def to_f(i, u):
                        dve.wait_ge(slots_used, dn.end(i, u))
                        for t in range(NT):
                            dst, src = f[:, t, bass.ds((2 * i + u) * CW, CW)], ps[:, 2 * dn.pair(u) + t, :]
                            last = V.tensor_tensor(dst, dst, src, ALU.add) if g else V.tensor_copy(dst, src)
                        last.then_inc(pair_free[dn.pair(u)], 1)

                    carried = walk(dve, gu, split_lo(gu), [(3, 1, times_up), (9, 1, h_lo)], carried,
                                   skip=RING if g == 0 else 0)
                    carried = walk(dve, dn, split_lo(dn), each_chunk(dn, to_f), carried)
                    return carried

                carried = []
                for g, (gu, dn) in enumerate(groups):
                    carried = group(g, gu, dn, carried)
                for _, fn in carried:
                    fn()
                dve.wait_ge(pair_free[dn.pair(1)], dn.uses(1, 1) + 1)

            V.memset(vrows[:, 0, 0:256], 0.0).then_inc(vr_zero, 1)
            ahead(passes[0])
            mean_square(0, EPS)
            diagonal(0, 0)
            dve.wait_ge(vec_copied, 1)
            link(V.tensor_tensor(vecd[:, 0:28], vec[:, R_MUP:R_MUP + 28], vec[:, R_MUN:R_MUN + 28], ALU.add))
            link(V.tensor_scalar(vecd[:, 0:28], vecd[:, 0:28], -1.0, 1.0, ALU.mult, ALU.add))
            V.tensor_scalar(vecd[:, 28:44], vec[:, R_W0:R_W0 + 16], 0.5, None, ALU.mult)
            V.tensor_scalar(vecd[:, 44:60], vec[:, R_A0:R_A0 + 16], 0.5, None, ALU.mult)
            V.tensor_scalar(vecd[:, 60:68], vec[:, R_KA:R_KA + 8], 0.5, None, ALU.mult)
            V.tensor_scalar(vecd[:, 68:76], vec[:, R_KA:R_KA + 8], -0.5, 1.0, ALU.mult, ALU.add)
            V.tensor_scalar(vecd[:, 76:77], vec[:, R_SUB:R_SUB + 1], 1.0 - LAM_INIT, None, ALU.mult).then_inc(vec_ready, 1)
            transposed_lo(0, R_F1)
            feed_forward(0, F1, ffn1)
            ahead(p_rw)
            mean_square(1, EPS)
            post_norm(1, 0, F1, 0.5)
            mean_square(2, EPS)
            diagonal(2, 1)
            transposed_lo(1, R_MIX)
            for p in (p_rw, p_rw7, p_dif):
                walk(dve, p, split_lo(p), [], (), skip=RING if p is p_rw else 0)
            ahead(p_gate)

            dve.wait_ge(pair_free[p_dif.pair(1)], p_dif.uses(2, 1) + 1)
            for i in range(2):
                V.memset(ybuf[:, i, 0:1], 0.0)
                link(V.memset(ybuf[:, i, T + 1:T + 2], 0.0))
            for n, j in enumerate(BLOCKS):
                w = 32 if j == NBLK - 1 else P
                kind, b = j // 8, j % 8
                if kind == 2 and b >= 2:
                    dve.wait_ge((v_out0, v_out1)[b % 2], 16 * (b // 2))
                tile, at = ((rr, b), (kr, b), (vst, b % 2), (lwa, b) if b < 2 else (lgd, b - 2))[kind]
                dst = tile[0:w, at, :]
                y = ybuf[0:w, n % 2, :]
                dve.wait_ge(sh_y, n + 1)
                link(V.tensor_scalar(dst, y[:, 1:T + 1], vecd[0:w, j:j + 1], None, ALU.mult))
                link(V.scalar_tensor_tensor(out=dst, in0=y[:, 0:T], scalar=vec[0:w, R_MUP + j:R_MUP + j + 1], in1=dst,
                                            op0=ALU.mult, op1=ALU.add))
                V.scalar_tensor_tensor(out=dst, in0=y[:, 2:T + 2], scalar=vec[0:w, R_MUN + j:R_MUN + j + 1], in1=dst,
                                       op0=ALU.mult, op1=ALU.add).then_inc(shifted, 1)
            dve.wait_ge(lora_act, 2)
            link(V.tensor_scalar(lgd[0:32, 1, :], lgd[0:32, 1, :], 0.5, 0.5, ALU.mult, ALU.add))
            V.tensor_scalar(lgd[:, 0, :], lgd[:, 0, :], 0.5, 0.5, ALU.mult, ALU.add).then_inc(gd_ready, 1)
            dve.wait_ge(kk_sum, NPAIR)
            V.tensor_scalar(s16[:, 0, :], ps[0:NH, 6, 0:T], 1e-24, None, ALU.max).then_inc(kk_max, 1)
            dve.wait_ge(kk_sqrt, 1)
            V.reciprocal(s16[:, 0, :], s16[:, 1, :]).then_inc(kk_rec, 1)
            for b in range(NPAIR):
                dve.wait_ge(kk_bc, b + 1)
                V.tensor_tensor(kkn[:, b, :], kkn[:, b, :], ps[:, 6 + b % 2, 0:T], ALU.mult).then_inc(kk_ready, 1)
            dve.wait_ge(v_out0, 16 * 4)
            dve.wait_ge(v_out1, 16 * 4)
            V.tensor_copy(q[0:C, 0, :], ident[0:C, 0:C])
            link(V.tensor_copy(q[C:P, 0, :], ident[C:P, C:P]))
            dve.wait_ge(g_out[0], 16 * (NPAIR // 2))
            dve.wait_ge(g_out[1], 16 * (NPAIR // 2))
            dve.wait_ge(kk_ready, NPAIR)

            def n_evac(m):
                dve.wait_ge(n_mm, m + 1)
                if m >= 2:
                    dve.wait_ge(n_out[m % 2], 32 * (m // 2))
                V.tensor_tensor(nst[:, m % 2, :, :], ps[:, 6 + m % 2, 0:T].rearrange("p (c t) -> p c t", c=NC_),
                                kc[:, K_MN:K_M1].unsqueeze(1).broadcast_to((P, NC_, C)), ALU.mult).then_inc(n_st, 1)

            def bonus(b):
                dve.wait_ge(bon_mm, b + 1)
                dve.wait_ge(v1_in, 16 * (b + 1))
                if b:
                    dve.wait_ge(bon_out, 16 * b)
                V.tensor_tensor(bst[:, :], ps[:, 5, 0:T], vb1[:, :], ALU.mult).then_inc(bon_st, 1)

            for m in range(NM):
                b, d = m // 2, m % 2
                sgn = slice(None, None, -1) if d else slice(None)
                r_, k_, kk_ = rr[:, b, sgn], kr[:, b, sgn], kkn[:, b, sgn]
                dve.wait_ge(za_act, m + 1)
                link(V.tensor_scalar(ld[:, :], tz[:, 0, :], -0.5 * DECAY, -0.5 * DECAY, ALU.mult, ALU.add))
                if m:
                    dve.wait_ge(ex_out, m)
                link(V.tensor_tensor_scan(ie[:, 0, :], kc[:, K_RESET:K_COS], ld[:, :], 0.0, ALU.mult, ALU.add))
                V.tensor_tensor(ie[:, 1, :], ie[:, 0, :], ld[:, :], ALU.subtract).then_inc(ex_in, 1)
                if d == 0 and b:
                    dve.wait_ge(bon_in, b)
                link(V.tensor_scalar(kd[:, :], tz[:, 1, :], vecd[:, 60 + b:61 + b], vecd[:, 68 + b:69 + b],
                                     ALU.mult, ALU.add))
                V.tensor_scalar(aa[:, :], tz[:, 1, :], 0.5, 0.5, ALU.mult, ALU.add).then_inc(aa_ready, 1)
                dve.wait_ge(aa_ready, m + 1)
                link(V.tensor_tensor(kd[:, :], kd[:, :], k_, ALU.mult))
                link(V.tensor_tensor(aa[:, :], aa[:, :], kk_, ALU.mult))
                if d == 0:
                    if b:
                        dve.wait_ge(bon_mm, b)
                    link(V.tensor_copy(kds[:, :], kd[:, :]))
                else:
                    link(V.tensor_tensor(kds[:, :], kds[:, :], kd[:, ::-1], ALU.add))
                    V.scalar_tensor_tensor(out=kds[:, :], in0=kds[:, :], scalar=vec[:, R_RK + b:R_RK + b + 1],
                                           in1=rr[:, b, :], op0=ALU.mult, op1=ALU.mult).then_inc(bon_in, 1)
                dve.wait_ge(ex_out, m + 1)
                s0 = 1 + 3 * NC_ * m
                qv = q[:, s0:s0 + 3 * NC_, :].rearrange("p (c w) t -> p c w t", w=3)
                ch = lambda a: a.rearrange("p (c t) -> p c t", c=NC_)
                V.tensor_tensor(qv[:, :, 1, :], ch(kd[:, :]), ch(eie[:, 2, :]), ALU.mult)
                V.tensor_tensor(beta[:, m, :], aa[:, :], eie[:, 2, :], ALU.mult)
                V.tensor_copy(pend[:, m, :], ch(eie[:, 0, :])[:, :, C - 1]).then_inc(q_ready, 1)
                if m:
                    n_evac(m - 1)
                if d == 0 and b:
                    bonus(b - 1)
            n_evac(NM - 1)
            bonus(NPAIR - 1)

            ones = z[:, :, :].rearrange("p c t -> p (c t)")[:, 0:C * C:C + 1]

            def step(s):
                if s == 0:
                    dve.wait_ge(z_in, 16)
                    link(V.memset(ones, 1.0))
                    return
                if s >= C - 1:
                    return
                n = C - 1 - s
                prod = zt[:, 0:s * n].rearrange("p (c t) -> p c t", c=s)
                rest = z[:, 0:s, s + 1:C]
                link(V.tensor_tensor(prod, z[:, 0:s, s:s + 1].broadcast_to((P, s, n)),
                                     z[:, s:s + 1, s + 1:C].broadcast_to((P, s, n)), ALU.mult))
                if s == C - 2:
                    V.tensor_tensor(rest, rest, prod, ALU.add).then_inc(z_done, 1)
                else:
                    link(V.tensor_tensor(rest, rest, prod, ALU.add))

            for k in range(p_gate.chunks * p_gate.slots):
                if k >= RING:
                    split_lo(p_gate)(p_gate.n0 + k, 0, k // p_gate.slots, k % p_gate.slots)
                step(k)
            ahead(p_br)

            dve.wait_ge(zs_in, 32)
            V.memset(sv[0:C, 0, 0, :], 0.0)
            V.memset(sv[0:C, 1, 0, :], 0.0).then_inc(sv_zero, 1)

            def ends(m):
                if m >= 2:
                    dve.wait_ge(gh_mm, 2 * (m - 1))
                at = 1 + 3 * NC_ * NM + NC_ * (m % 2)
                V.tensor_tensor(q[:, at:at + NC_, :], q[:, 0:1, :].broadcast_to((P, NC_, C)),
                                pend[:, m, :].unsqueeze(2).broadcast_to((P, NC_, C)), ALU.mult).then_inc(dd_ready, 1)

            def masked_ab(m):
                for h in range(2):
                    dve.wait_ge(ab_mm, 2 * m + h + 1)
                    if m >= 2 and h == 0:
                        dve.wait_ge(gh_mm, 2 * (m - 1))
                    V.tensor_tensor(mb[:, m % 2, 2 * h:2 * h + 2, :],
                                    ps[:, h, :].rearrange("p (c v) -> p c v", c=2),
                                    kc[:, K_M1:K_MG].unsqueeze(1).broadcast_to((P, 2, 4 * C)), ALU.mult).then_inc(ab_ready, 1)

            def masked_gh(m):
                for h in range(2):
                    dve.wait_ge(gh_mm, 2 * m + h + 1)
                    if m >= 2 and h == 0:
                        dve.wait_ge(o_mm, m - 1)
                    V.tensor_tensor(gh[:, m % 2, 4 * h:4 * h + 4, :],
                                    ps[:, 4 + h, :].rearrange("p (c v) -> p c v", c=4),
                                    kc[:, K_MG:K_RESET].unsqueeze(1).broadcast_to((P, 4, 2 * C)), ALU.mult).then_inc(gh_ready, 1)

            def to_oc(m):
                b = m // 2
                dve.wait_ge(o_mm, m + 1)
                src = ps[:, 7, 0:T]
                if m % 2:
                    V.tensor_tensor(oc[:, b, :], oc[:, b, :], src[:, ::-1], ALU.add).then_inc(o_ready, 1)
                else:
                    V.tensor_copy(oc[:, b, :], src).then_inc(o_ready, 1)

            ends(0)
            masked_ab(0)
            masked_gh(0)
            for m in range(NM):
                if m + 1 < NM:
                    ends(m + 1)
                    masked_ab(m + 1)
                to_oc(m)
                dve.wait_ge(o_ready, m + 1)
                if m + 1 < NM:
                    masked_gh(m + 1)
            dve.wait_ge(gn_sum, 1)
            V.tensor_scalar(o16[:, 0, :], ps[0:NH, 0, 0:T], 1.0 / 64, None, ALU.mult).then_inc(gn_mean, 1)
            for b in range(NPAIR):
                dve.wait_ge(gn_bc, b + 1)
                V.tensor_tensor(oc[:, b, :], oc[:, b, :], ps[:, 4 + b % 4, 0:T], ALU.subtract).then_inc(gn_cent, 1)
            dve.wait_ge(gn_var, NPAIR)
            V.tensor_scalar(o16[:, 1, :], ps[0:NH, 1, 0:T], 1.0 / 64, GN_EPS, ALU.mult, ALU.add).then_inc(gn_varv, 1)
            dve.wait_ge(gn_sqrt, 1)
            V.reciprocal(o16[:, 3, :], o16[:, 2, :]).then_inc(gn_rec, 1)
            dve.wait_ge(gn_in, 32)
            for b in range(NPAIR):
                dve.wait_ge(gn_bc2, b + 1)
                y = oc[:, b, :]
                link(V.tensor_tensor(y, y, ps[:, 4 + b % 4, 0:T], ALU.mult))
                link(V.tensor_scalar(y, y, vec[:, R_GNW + b:R_GNW + b + 1], vec[:, R_GNB + b:R_GNB + b + 1],
                                     ALU.mult, ALU.add))
                link(V.tensor_tensor(y, y, bo[:, b, :], ALU.add))
                V.tensor_tensor(y, y, gg[:, b, :], ALU.mult).then_inc(ya_y, 1)
            for b in range(NPAIR):
                dve.wait_ge(ya_hi, b + 1)
                V.tensor_tensor(ytlo[:, b, :], oc[:, b, :], ythi[:, b, :].bitcast(F32), ALU.subtract).then_inc(ya_lo, 1)

            dve.wait_ge(ya_lo, NPAIR)
            dve.wait_ge(at_in, 16 * 6)
            for t in range(NT):
                cos = kc[:, K_COS + 32 * t:K_COS + 32 * t + 32].unsqueeze(1).unsqueeze(1).broadcast_to((P, 16, 2, 32))
                sin = kc[:, K_SIN + 32 * t:K_SIN + 32 * t + 32].unsqueeze(1).unsqueeze(1).broadcast_to((P, 16, 2, 32))
                for w in range(2):
                    xv = qk[:, t, w * RW:(w + 1) * RW].rearrange("p (h s f) -> p h s f", h=16, s=2)
                    a_ = ra[:, :].rearrange("p (h s f) -> p h s f", h=16, s=2)
                    b_ = rb[:, :].rearrange("p (h s f) -> p h s f", h=16, s=2)
                    V.tensor_tensor(a_, xv, cos, ALU.mult)
                    link(V.tensor_tensor(b_, xv[:, :, ::-1, :], sin, ALU.mult))
                    V.tensor_tensor(xv[:, :, 0, :], a_[:, :, 0, :], b_[:, :, 0, :], ALU.subtract)
                    V.tensor_tensor(xv[:, :, 1, :], a_[:, :, 1, :], b_[:, :, 1, :], ALU.add).then_inc(roped, 1)
                    dve.wait_ge(roped, 2 * t + w + 1)
            for i in range(2):
                link(V.tensor_tensor(lamv[:, 2 * i, :], lamv[:, 2 * i, :], lamv[:, 2 * i + 1, :], ALU.mult))
                last = V.tensor_reduce(lamb[:, i:i + 1], lamv[:, 2 * i, :], AX.X, ALU.add)
            last.then_inc(lam_sum, 1)
            dve.wait_ge(lam_exp, 1)
            link(V.tensor_tensor(lamb[:, 4:5], lamb[:, 3:4], lamb[:, 2:3], ALU.subtract))
            link(V.tensor_scalar(lamb[:, 5:6], lamb[:, 4:5], -LAM_INIT, None, ALU.add))
            for g in range(4):
                for v2 in range(2):
                    dve.wait_ge(sc_mm, 2 * g + v2 + 1)
                    if g:
                        dve.wait_ge(ex_p, 4 * (g - 1) + 2 * v2 + 2)
                    for s in range(2):
                        last = V.tensor_reduce(mx[:, 2 * v2:2 * v2 + 2, s], ps[:, 2 * v2 + s, :].rearrange("p (v t) -> p v t", v=2),
                                               AX.X, ALU.max)
                    link(last)
                    pair = mx[:, 2 * v2:2 * v2 + 2, :]
                    V.tensor_scalar(pair, pair, -0.125, None, ALU.mult).then_inc(mx_ready, 1)
                for v in range(4):
                    w = 4 * g + v
                    dve.wait_ge(ex_p, w + 1)
                    if g:
                        dve.wait_ge(am_t, 2 * g)
                    link(V.reciprocal(su[:, v, :], su[:, v, :]))
                    link(V.tensor_tensor(su[:, v, 1:2], su[:, v, 1:2], lamb[:, 5:6], ALU.mult))
                    link(V.tensor_scalar(am[:, v, :], pex[:, v, 1, :], su[:, v, 1:2], None, ALU.mult))
                    V.scalar_tensor_tensor(out=am[:, v, :], in0=pex[:, v, 0, :], scalar=su[:, v, 0:1], in1=am[:, v, :],
                                           op0=ALU.mult, op1=ALU.add).then_inc(am_ready, 1)
                dve.wait_ge(pv_sq, g + 1)
                V.tensor_scalar(os_[:, 4:8], os_[:, 0:4], 1.0 / P, SUBLN_EPS, ALU.mult, ALU.add).then_inc(pv_ms, 1)
                dve.wait_ge(pv_rs, g + 1)
                if g:
                    dve.wait_ge(yb_t, g)
                V.tensor_tensor(ov[:, :, :], ps[:, 6, :].rearrange("p (v i) -> p v i", v=4),
                                os_[:, 8:12].unsqueeze(2).broadcast_to((P, 4, P)), ALU.mult).then_inc(yb_ready, 1)
                hs, t = 4 * (g % 2), g // 2
                dve.wait_ge(yb_hi, g + 1)
                V.scalar_tensor_tensor(out=ytlo[:, 8 + hs:12 + hs, t * P:(t + 1) * P],
                                       in0=ps[:, 7, :].rearrange("p (v t) -> p v t", v=4), scalar=vecd[:, 76:77],
                                       in1=ythi[:, 8 + hs:12 + hs, t * P:(t + 1) * P].bitcast(F32),
                                       op0=ALU.mult, op1=ALU.subtract).then_inc(yb_lo, 1)

            def merge_a(i, u=0):
                dve.wait_ge(slots_used, p_br.end(i, 0))
                dve.wait_ge(gt_in[i % 2], 32 * (i // 2 + 1))
                for t in range(NT):
                    last = V.tensor_tensor(mg[:, t, i * CW:(i + 1) * CW], ps[:, 2 * p_br.pair(0) + t, :],
                                           gbuf[:, i % 2, 0, t, :], ALU.mult)
                last.then_inc(pair_free[p_br.pair(0)], 1)

            def merge_b(i, u=1):
                dve.wait_ge(slots_used, p_br.end(i, 1))
                for t in range(NT):
                    last = V.tensor_tensor(mt[:, t, :], ps[:, 2 * p_br.pair(1) + t, :], gbuf[:, i % 2, 1, t, :], ALU.mult)
                last.then_inc(pair_free[p_br.pair(1)], 1)
                dve.wait_ge(pair_free[p_br.pair(1)], p_br.uses(i, 1) + 1)
                dst = mg[:, :, i * CW:(i + 1) * CW]
                V.tensor_tensor(dst, dst, mt[:, :, :], ALU.add).then_inc(mg_ready, 1)
                dve.wait_ge(mg_ready, i + 1)

            for i in range(4):
                for k in range(8):
                    if i or k >= RING:
                        split_lo(p_br)(p_br.n0 + 8 * i + k, 0, 2 * i + k // 4, k % 4)
                    if k == 3 and i:
                        merge_b(i - 1)
                    if k == 7:
                        merge_a(i)
            merge_b(3)
            ahead(p_out)
            transposed_lo(2, None)

            def out_to_f(i, u):
                dve.wait_ge(slots_used, p_out.end(i, u))
                for t in range(NT):
                    last = V.tensor_copy(F2[1][:, t, bass.ds((2 * i + u) * CW, CW)], ps[:, 2 * p_out.pair(u) + t, :])
                last.then_inc(pair_free[p_out.pair(u)], 1)

            for _, fn in walk(dve, p_out, split_lo(p_out), each_chunk(p_out, out_to_f), (), skip=RING):
                fn()
            ahead(ffn2[0][0])
            mean_square(3, EPS)
            dve.wait_ge(h_back, 16)
            post_norm(3, 1, F2, 1.0)
            mean_square(4, EPS)
            diagonal(4, 2)
            transposed_lo(3, R_F2)
            feed_forward(1, F2, ffn2)
            mean_square(5, EPS)
            post_norm(5, 2, F2, 0.5)

        @block.tensor
        def _(pe):
            mm = nc.tensor.matmul

            def product(p, hi, lo, ready=None):
                def slot(n, i, u, j):
                    s = slot_of(p, u, j)
                    first = isinstance(i, int) and i == 0 and u == 0
                    if first and ready is not None:
                        ready(j)
                    if j == 0 and not (isinstance(i, int) and p.uses(i, u) == 0):
                        pe.wait_ge(pair_free[p.pair(u)], p.uses(i, u))
                    pe.wait_ge(lo_ready, n + 1)
                    for k in range(SB):
                        a, b = hi(u, SB * j + k), lo(u, SB * j + k)
                        for t in range(NT):
                            o = ps[:, 2 * p.pair(u) + t, 0:p.width]
                            at, bt = a[:, t * P:(t + 1) * P], b[:, t * P:(t + 1) * P]
                            w_, l_ = whi[:, s, k, 0:p.width], wlo[:, s, k, 0:p.width]
                            mm(o, at, w_, start=(j == 0 and k == 0), stop=False)
                            mm(o, at, l_, start=False, stop=False)
                            last = mm(o, bt, w_, start=False, stop=(j == p.slots - 1 and k == SB - 1))
                    last.then_inc(slots_used, 1)
                return slot

            def from_u(p, e):
                return product(p, lambda u, k: uhi[:, k, :], lambda u, k: ulo[:, k, :],
                               (lambda j: pe.wait_ge(ut_lo, ut_base(e) + SB * (j + 1))) if e is not None else None)

            def transpose_u(e, src, nth_diag):
                if nth_diag is not None:
                    pe.wait_ge(diag_ready, nth_diag + 1)
                for k in range(KB):
                    if k >= 4:
                        pe.wait_ge(ut_lo, ut_base(e) + k - 3)
                    for t in range(NT):
                        o, a = ps[:, 4 + k % 4, t * P:(t + 1) * P], src[:, t, k * P:(k + 1) * P]
                        if nth_diag is None:
                            last = nc.tensor.transpose(o, a, ident)
                        else:
                            last = mm(o, a, dg[:, t, :], start=True, stop=True)
                    last.then_inc(ut_done, 1)

            def feed_forward(w, F, groups, e):
                h, f, hthi, htlo, sg, hm, gain = F

                def group(g, gu, dn, carried):
                    f0, f1 = FF_GROUPS[g]
                    fb = w * FFC + f0

                    def turn_h(i):
                        pe.wait_ge(pair_free[gu.pair(1)], gu.uses(i, 1) + 1)
                        if not (isinstance(i, int) and fb + i == 0):
                            pe.wait_ge(ht_lo, 2 * (fb + i))
                        for b in range(2):
                            for k in range(2):
                                for t in range(NT):
                                    kk = 2 * b + k
                                    last = nc.tensor.transpose(ps[:, 4 + b, (2 * k + t) * P:(2 * k + t + 1) * P],
                                                               hm[:, t, kk * P:(kk + 1) * P], ident)
                            last.then_inc(hm_t, 1)

                    def h_ready_(j):
                        if j == 0:
                            pe.wait_ge(ht_lo, 2 * (fb + f1 - f0 - 1))
                        if j == dn.slots - 2:
                            pe.wait_ge(ht_lo, 2 * (fb + f1 - f0))

                    carried = walk(pe, gu, from_u(gu, e if g == 0 else None), [(3, 1, turn_h)], carried)
                    carried = walk(pe, dn, product(dn, lambda u, k: hthi[:, k, :], lambda u, k: htlo[:, k, :], h_ready_),
                                   [], carried)
                    return carried

                carried = []
                for g, (gu, dn) in enumerate(groups):
                    carried = group(g, gu, dn, carried)
            pe.wait_ge(c_in, 16)
            pe.wait_ge(vr_in, 16 * N_VEC)
            nc.tensor.transpose(ps[:, 4, 0:P], vrows[:, 0, 0:P], ident)
            nc.tensor.transpose(ps[:, 4, P:2 * P], vrows[:, 0, P:2 * P], ident).then_inc(vec_t, 1)
            pe.wait_ge(vec_copied, 1)
            pe.wait_ge(x_in, 16)
            transpose_u(0, F1[0], 0)
            feed_forward(0, F1, ffn1, 0)
            pe.wait_ge(h_ready, NT)
            transpose_u(1, F1[0], 1)
            for p in (p_rw, p_rw7, p_dif):
                walk(pe, p, from_u(p, 1 if p is p_rw else None))

            pe.wait_ge(pair_free[p_rw7.pair(0)], p_rw7.uses(0, 0) + 1)
            pe.wait_ge(pair_free[p_rw.pair(1)], p_rw.uses(2, 1) + 1)
            for n, j in enumerate(BLOCKS):
                w = 32 if j == NBLK - 1 else P
                if n >= 4:
                    pe.wait_ge(sh_y, n - 3)
                for t in range(NT):
                    last = nc.tensor.transpose(ps[0:w, 4 + n % 4, t * P:(t + 1) * P], proj[:, t, j * P:j * P + w], ident)
                last.then_inc(sh_t, 1)
            for b in range(NPAIR):
                pe.wait_ge(kk_sq, b + 1)
                mm(ps[0:NH, 6, 0:T], kc[:, K_SEL + NH * b:K_SEL + NH * (b + 1)], sqb[:, b % 2, :],
                   start=(b == 0), stop=(b == NPAIR - 1)).then_inc(kk_sum, 1)
            pe.wait_ge(gd_ready, 1)
            pe.wait_ge(par_in, 64)
            for b in range(NPAIR):
                if b >= 2:
                    pe.wait_ge(g_st, b - 1)
                o = ps[:, 4 + b % 2, 0:T]
                mm(o, gupa[:, b * P:(b + 1) * P], lgd[:, 0, :], start=True, stop=False)
                mm(o, gupb[:, b * P:(b + 1) * P], lgd[0:32, 1, :], start=False, stop=True).then_inc(g_mm, 1)
            pe.wait_ge(kk_rec, 1)
            pe.wait_ge(sel_in, 16)
            for b in range(NPAIR):
                if b >= 2:
                    pe.wait_ge(kk_ready, b - 1)
                mm(ps[:, 6 + b % 2, 0:T], seltA[:, b * P:(b + 1) * P], s16[:, 0, :], start=True, stop=True).then_inc(kk_bc, 1)

            def low_rank(m):
                b, d = m // 2, m % 2
                if m >= 2:
                    pe.wait_ge(za_act, m - 1)
                if m == 2 * (m // 2) + 1 and b:
                    pe.wait_ge(bon_st, b)
                rows = slice(LORA * d, LORA * (d + 1))
                sgn = slice(None, None, -1) if d else slice(None)
                mm(ps[:, 4 + m % 2, 0:T], wup[rows, b * P:(b + 1) * P], lwa[rows, 0, sgn], start=True, stop=True)
                mm(ps[:, 4 + m % 2, T:2 * T], aup[rows, b * P:(b + 1) * P], lwa[rows, 1, sgn],
                   start=True, stop=True).then_inc(za_mm, 1)

            def n_products(m):
                pe.wait_ge(q_ready, m + 1)
                pe.wait_ge(ra_ready, 2 * m + 2)
                if m >= 2:
                    pe.wait_ge(n_st, m - 1)
                else:
                    pe.wait_ge(kk_ready, NPAIR)
                for c in range(NC_):
                    for h in range(2):
                        r = slice(C * h, C * (h + 1))
                        last = mm(ps[r, 6 + m % 2, c * C:(c + 1) * C], beta[r, m, c * C:(c + 1) * C],
                                  q[r, 1 + 3 * (NC_ * m + c) + 2, :], start=True, stop=True)
                last.then_inc(n_mm, 1)

            pe.wait_ge(g_st, NPAIR)
            pe.wait_ge(lora_act, 1)
            low_rank(0)
            low_rank(1)
            for m in range(NM):
                n_products(m)
                if m % 2:
                    b = m // 2
                    pe.wait_ge(bon_in, b + 1)
                    pe.wait_ge(za_act, m + 1)
                    mm(ps[:, 5, 0:T], headsum[:, :], kds[:, :], start=True, stop=True).then_inc(bon_mm, 1)
                if m + 2 < NM:
                    low_rank(m + 2)

            walk(pe, p_gate, from_u(p_gate, None))

            pe.wait_ge(zs_in, 32)
            for b in range(2):
                pe.wait_ge(pair_free[b], (p_gate.q0 + 8 - b + 1) // 2)

            def alpha_beta(m, c):
                b, d = m // 2, m % 2
                if c == 0:
                    pe.wait_ge(dd_ready, m + 1)
                    if d:
                        pe.wait_ge(vr_ready, b + 1)
                    else:
                        pe.wait_ge(vb_in, 16 * (b + 1))
                    if m:
                        pe.wait_ge(vt_ready, m)
                        pe.wait_ge(ab_ready, 2 * m)
                at = 1 + 3 * (NC_ * m + c)
                dd = 1 + 3 * NC_ * NM + NC_ * (m % 2) + c
                vt = vrev if d else vb
                last_v = mm(ps[C:P, 2, c * P:(c + 1) * P], vt[:, c * C:(c + 1) * C], ident, start=True, stop=True)
                if c == NC_ - 1:
                    last_v.then_inc(vt_mm, 1)
                for h in range(2):
                    r = slice(C * h, C * (h + 1))
                    o = ps[r, c // 2, (c % 2) * 4 * C:(c % 2 + 1) * 4 * C]
                    mm(o[:, 0:2 * C], beta[r, m, c * C:(c + 1) * C], q[r, at:dd + 1:dd - at, :], start=True, stop=True)
                    last = mm(o[:, 2 * C:4 * C], q[r, at + 2, :], q[r, 0:at + 2:at + 1, :], start=True, stop=True)
                if c % 2:
                    last.then_inc(ab_mm, 1)

            def w_products(m):
                pe.wait_ge(ab_ready, 2 * m + 2)
                if m:
                    pe.wait_ge(w_ready, m)
                for c in range(NC_):
                    for h in range(2):
                        r = slice(C * h, C * (h + 1))
                        last = mm(ps[r, 3, c * P:(c + 1) * P], zs[r, NC_ * m + c, :], mb[r, m % 2, c, 2 * C:4 * C],
                                  start=True, stop=True)
                last.then_inc(w_mm, 1)

            def gh_products(m):
                pe.wait_ge(w_ready, m + 1)
                if m:
                    pe.wait_ge(gh_ready, 2 * m)
                for c in range(NC_):
                    at = 1 + 3 * (NC_ * m + c)
                    dd = 1 + 3 * NC_ * NM + NC_ * (m % 2) + c
                    for h in range(2):
                        r = slice(C * h, C * (h + 1))
                        o = ps[:, 4 + h, c * P:(c + 1) * P]
                        rho_end = q[r, at:dd + 1:dd - at, :]
                        mm(o, wt[r, m % 2, c, :], mb[r, m % 2, c, 0:2 * C], start=True, stop=False, skip_group_check=True)
                        mm(o[0:C], q[r, 0, :], rho_end, start=False, stop=False, skip_group_check=True)
                        last = mm(o[C:P], q[r, at + 1, :], rho_end, start=False, stop=True, skip_group_check=True)
                        if c == NC_ - 1:
                            last.then_inc(gh_mm, 1)

            def recur(m, c):
                if c == 0:
                    pe.wait_ge(gh_ready, 2 * m + 2)
                    pe.wait_ge(vt_ready, m + 1)
                    pe.wait_ge(sv_zero, 1)
                    if m:
                        pe.wait_ge(o_ready, m)
                else:
                    pe.wait_ge(s_ready, 3 * m + c)
                if c < NC_ - 1:
                    for h in range(2):
                        last = mm(ps[0:C, 6, h * C:(h + 1) * C], gh[:, m % 2, NC_ * h + c, C:2 * C],
                                  sv[:, m % 2, c, h * C:(h + 1) * C], start=True, stop=True)
                    last.then_inc(s_mm, 1)
                for h in range(2):
                    last = mm(ps[C * h:C * (h + 1), 7, c * C:(c + 1) * C], sv[:, m % 2, c, h * C:(h + 1) * C],
                              gh[:, m % 2, NC_ * h + c, 0:C], start=True, stop=True)
                if c == NC_ - 1:
                    last.then_inc(o_mm, 1)

            for c in range(NC_):
                alpha_beta(0, c)
            w_products(0)
            gh_products(0)
            for m in range(NM):
                for c in range(NC_):
                    recur(m, c)
                    if m + 1 < NM:
                        alpha_beta(m + 1, c)
                if m + 1 < NM:
                    w_products(m + 1)
                    gh_products(m + 1)
            pe.wait_ge(ab_ready, 2 * NM)
            pe.wait_ge(o_ready, NM)
            for b in range(NPAIR):
                last = mm(ps[0:NH, 0, 0:T], kc[:, K_SEL + NH * b:K_SEL + NH * (b + 1)], oc[:, b, :],
                          start=(b == 0), stop=(b == NPAIR - 1))
            last.then_inc(gn_sum, 1)
            pe.wait_ge(gn_mean, 1)
            for b in range(NPAIR):
                if b >= 4:
                    pe.wait_ge(gn_cent, b - 3)
                mm(ps[:, 4 + b % 4, 0:T], seltA[:, b * P:(b + 1) * P], o16[:, 0, :], start=True, stop=True).then_inc(gn_bc, 1)
            for b in range(NPAIR):
                pe.wait_ge(gn_sq, b + 1)
                mm(ps[0:NH, 1, 0:T], kc[:, K_SEL + NH * b:K_SEL + NH * (b + 1)], osq[:, b % 2, :],
                   start=(b == 0), stop=(b == NPAIR - 1)).then_inc(gn_var, 1)
            pe.wait_ge(gn_rec, 1)
            for b in range(NPAIR):
                if b >= 4:
                    pe.wait_ge(ya_y, b - 3)
                mm(ps[:, 4 + b % 4, 0:T], seltA[:, b * P:(b + 1) * P], o16[:, 3, :], start=True, stop=True).then_inc(gn_bc2, 1)

            pe.wait_ge(ya_y, NPAIR)
            pe.wait_ge(roped, 4)
            for n in range(16):
                if n >= 4:
                    pe.wait_ge(qt_ready, n - 3)
                for t in range(NT):
                    last = nc.tensor.transpose(ps[:, 4 + n % 4, t * P:(t + 1) * P],
                                               qk[:, t, n * P:(n + 1) * P], ident)
                last.then_inc(qt_mm, 1)
            pe.wait_ge(qt_ready, 16)

            def scores(g):
                t, hs = g // 2, 4 * (g % 2)
                for v2 in range(2):
                    if g:
                        pe.wait_ge(ex_p, 4 * (g - 1) + 2 * v2 + 2)
                    for v in range(2):
                        hd = hs + 2 * v2 + v
                        for s in range(2):
                            r = slice(C * s, C * (s + 1))
                            last = mm(ps[:, 2 * v2 + s, v * T:(v + 1) * T], qt_[r, hd, t * P:(t + 1) * P], kt_[r, hd, :],
                                      start=True, stop=True)
                    last.then_inc(sc_mm, 1)

            scores(0)
            for g in range(4):
                t, hs = g // 2, 4 * (g % 2)
                for v in range(4):
                    pe.wait_ge(am_ready, 4 * g + v + 1)
                    if g:
                        pe.wait_ge(amt_ready, 2 * g - 1 + v // 2)
                    for k in range(NT):
                        last = nc.tensor.transpose(ps[:, 4 + v // 2, (v % 2) * T + k * P:(v % 2) * T + (k + 1) * P],
                                                   am[:, v, k * P:(k + 1) * P], ident)
                    if v % 2:
                        last.then_inc(am_t, 1)
                if g < 3:
                    scores(g + 1)
                pe.wait_ge(amt_ready, 2 * g + 2)
                if g:
                    pe.wait_ge(yb_ready, g)
                for v in range(4):
                    for k in range(NT):
                        last = mm(ps[:, 6, v * P:(v + 1) * P], amt[:, v, k * P:(k + 1) * P],
                                  va[:, k, (hs + v) * P:(hs + v + 1) * P], start=(k == 0), stop=(k == NT - 1))
                last.then_inc(pv_mm, 1)
                pe.wait_ge(yb_ready, g + 1)
                if g:
                    pe.wait_ge(yb_lo, g)
                for v in range(4):
                    last = nc.tensor.transpose(ps[:, 7, v * P:(v + 1) * P], ov[:, v, :], ident)
                last.then_inc(yb_t, 1)

            pe.wait_ge(ya_lo, NPAIR)
            pe.wait_ge(yb_lo, 4)
            walk(pe, p_br, product(p_br, lambda u, k: ythi[:, 8 * u + k, :], lambda u, k: ytlo[:, 8 * u + k, :]))
            pe.wait_ge(mg_ready, 4)
            transpose_u(2, mg, None)
            walk(pe, p_out, from_u(p_out, 2))
            pe.wait_ge(h_ready, 2 * NT)
            transpose_u(3, F2[0], 2)
            feed_forward(1, F2, ffn2, 3)

        @block.gpsimd
        def _(pool):
            links = [0]
            G = nc.gpsimd

            def link(ins):
                links[0] += 1
                ins.then_inc(pool_link, 1)
                pool.wait_ge(pool_link, links[0])

            def inverse_norm(e):
                pool.wait_ge(ms_ready, e + 1)
                G.tensor_tensor(sm[:, RS[e]], sm[:, MS[e]], sm[:, HALF][:, 0:2], ALU.pow).then_inc(rstd_ready, 1)

            def gain(F, g):
                pool.dma_start(F[6][:, :], g.partition_broadcast(P)).then_inc(gain_in, 16)

            link(G.memset(sm[:, HALF], -0.5))
            pool.wait_ge(vr_zero, 1)
            for v, r, n in VECTORS:
                dst = vrows[r % P:r % P + n, 0, (r // P) * P:(r // P) * P + v.shape[-1]]
                pool.dma_start(dst, v).then_inc(vr_in, 16)
            inverse_norm(0)
            gain(F1, ffn[0][3][0])
            inverse_norm(1)
            inverse_norm(2)
            pool.wait_ge(h_ready, NT)
            pool.dma_start(h_dram.rearrange("(t p) d -> p t d", p=P), F1[0][:, :, :]).then_inc(h_saved, 16)

            def store_stage(p, tile, dram):
                for i in range(p.turns):
                    for u in range(2):
                        b = p.pair(u)
                        pool.wait_ge(pair_free[b], p.uses(i, u) + 1)
                        c0 = (2 * i + u) * CW
                        pool.dma_start(dram[:, c0:c0 + CW].rearrange("(t p) n -> p t n", p=P),
                                       tile[:, b, :, :]).then_inc(st_out[b], 16)

            store_stage(p_dif, dst_a, dif_dram)
            pool.dma_start(wup[:, :], w_up[0].rearrange("d r c -> (d r) c")).then_inc(par_in, 16)
            pool.dma_start(aup[:, :], a_up[0].rearrange("d r c -> (d r) c")).then_inc(par_in, 16)
            pool.dma_start(gupa[:, :], g_up[0, 0:P, :]).then_inc(par_in, 16)
            pool.dma_start(gupb[:, :], g_up[0, P:GLORA, :]).then_inc(par_in, 16)
            for b in range(NPAIR):
                pool.wait_ge(shifted, NBLK - NPAIR + b + 1)
                pool.dma_start(v_dram[b], vst[:, b % 2, :]).then_inc((v_out0, v_out1)[b % 2], 16)
            for b in range(NPAIR):
                pool.wait_ge(g_st, b + 1)
                pool.dma_start(g_dram[b], gst[:, b % 2, :]).then_inc(g_out[b % 2], 16)
            pool.wait_ge(v_out0, 16 * 4)
            pool.wait_ge(v_out1, 16 * 4)
            pool.wait_ge(g_out[0], 16 * 4)
            pool.wait_ge(g_out[1], 16 * 4)
            pool.wait_ge(kk_ready, NPAIR)
            n_out_dst = n_dram.rearrange("h m c s t -> h m s c t")

            def stage_out(m):
                pool.wait_ge(n_st, m + 1)
                for h in range(2):
                    pool.dma_start(n_out_dst[h, m], nst[C * h:C * (h + 1), m % 2, :, :]).then_inc(n_out[m % 2], 16)

            for m in range(NM):
                b, d = m // 2, m % 2
                if d == 0:
                    if b:
                        pool.wait_ge(bon_st, b)
                    pool.dma_start(vb1[:, :], v_dram[b]).then_inc(v1_in, 16)
                sgn = slice(None, None, -1) if d else slice(None)
                s0 = 1 + 3 * NC_ * m
                qv = q[:, s0:s0 + 3 * NC_, :].rearrange("p (c w) t -> p c w t", w=3)
                ch = lambda a: a.rearrange("p (c t) -> p c t", c=NC_)
                pool.wait_ge(ex_out, m + 1)
                G.tensor_tensor(qv[:, :, 0, :], ch(rr[:, b, sgn]), ch(eie[:, 0, :]), ALU.mult).then_inc(ra_ready, 1)
                G.tensor_tensor(qv[:, :, 2, :], ch(kkn[:, b, sgn]), ch(eie[:, 1, :]), ALU.mult).then_inc(ra_ready, 1)
                if m:
                    stage_out(m - 1)
                if d == 0 and b:
                    pool.wait_ge(bon_st, b)
                    pool.dma_start(bonus_dram[b - 1], bst[:, :]).then_inc(bon_out, 16)
            stage_out(NM - 1)
            pool.wait_ge(bon_st, NPAIR)
            pool.dma_start(bonus_dram[NPAIR - 1], bst[:, :]).then_inc(bon_out, 16)
            pool.wait_ge(n_out[0], 32 * (NM // 2))
            pool.wait_ge(n_out[1], 32 * (NM // 2))
            pool.wait_ge(bon_out, 16 * NPAIR)
            pool.dma_start(z[:, :, :].rearrange("p c t -> p (c t)"),
                           n_dram.rearrange("h m c s t -> (h m c) (s t)")).then_inc(z_in, 16)
            for i in range(p_gate.turns):
                for u in range(2):
                    b = p_gate.pair(u)
                    pool.wait_ge(pair_free[b], p_gate.uses(i, u) + 1)
                    c0 = (2 * i + u) * CW
                    pool.dma_start(gate_dram[:, c0:c0 + CW].rearrange("(t p) n -> p t n", p=P),
                                   gst_g[:, b, :, :]).then_inc(st_out[b], 16)
            pool.wait_ge(z_done, 1)
            pool.dma_start(z_dram.rearrange("h m c s t -> (h m c) (s t)"),
                           z[:, :, :].rearrange("p c t -> p (c t)")).then_inc(z_out, 16)
            pool.wait_ge(z_out, 16)
            pool.wait_ge(st_out[0], 16 * 7)
            pool.wait_ge(st_out[1], 16 * 7)
            for h in range(2):
                pool.dma_start(zs[C * h:C * (h + 1), :, :],
                               z_dram[h].rearrange("m c s t -> s (m c) t")).then_inc(zs_in, 16)

            pool.wait_ge(zs_in, 32)
            for b in range(NPAIR):
                if b:
                    pool.wait_ge(vt_mm, 2 * b - 1)
                    pool.wait_ge(vr_ready, b)
                pool.dma_start(vb[:, :], v_dram[b]).then_inc(vb_in, 16)
                pool.wait_ge(vb_in, 16 * (b + 1))
                if b:
                    pool.wait_ge(vt_mm, 2 * b)
                G.tensor_copy(vrev[:, :], vb[:, ::-1]).then_inc(vr_ready, 1)
            pool.wait_ge(gh_mm, 2 * NM)
            pool.dma_start(bo[:, :, :], bonus_dram.rearrange("b p t -> p b t")).then_inc(gn_in, 16)
            pool.dma_start(gg[:, :, :], g_dram.rearrange("b p t -> p b t")).then_inc(gn_in, 16)
            pool.wait_ge(ya_lo, NPAIR)
            dif = dif_dram.rearrange("(t p) c -> p t c", p=P)
            pool.dma_start(qk[:, :, :], dif[:, :, 0:2 * RW]).then_inc(at_in, 16)
            pool.dma_start(va[:, :, :], dif[:, :, 2 * RW:3 * RW]).then_inc(at_in, 16)
            for i, n in enumerate(("lambda_q1", "lambda_k1", "lambda_q2", "lambda_k2")):
                pool.dma_start(lamv[:, i, :], a[n][0].partition_broadcast(P)).then_inc(at_in, 16)
            for g in range(4):
                pool.wait_ge(pv_ms, g + 1)
                if g:
                    pool.wait_ge(yb_ready, g)
                G.tensor_tensor(os_[:, 8:12], os_[:, 4:8], sm[:, HALF][:, 0:4], ALU.pow).then_inc(pv_rs, 1)
            pool.wait_ge(yb_lo, 4)
            gates = gate_dram.rearrange("(t p) (w n) -> p w t n", p=P, w=2)
            for i in range(4):
                if i >= 2:
                    pool.wait_ge(mg_ready, i - 1)
                for w in range(2):
                    pool.dma_start(gbuf[:, i % 2, w, :, :], gates[:, w, :, i * CW:(i + 1) * CW]).then_inc(gt_in[i % 2], 16)
            pool.wait_ge(mg_ready, 4)
            pool.wait_ge(slots_used, p_br.end(3, 1))
            pool.dma_start(F2[0][:, :, :], h_dram.rearrange("(t p) d -> p t d", p=P)).then_inc(h_back, 16)
            gain(F2, mix_post_g[0])
            inverse_norm(3)
            inverse_norm(4)
            pool.wait_ge(h_ready, 2 * NT)
            gain(F2, ffn[1][3][0])
            inverse_norm(5)
            pool.wait_ge(h_ready, 3 * NT)
            pool.dma_start(out[0].rearrange("(t p) d -> p t d", p=P), F2[0][:, :, :]).then_inc(out_done, 16)
            pool.wait_ge(out_done, 16)
            pool.wait_ge(h_saved, 16)


_NAMES = ['x', 'ffn1_pre_g', 'ffn1_w_gu', 'ffn1_w_down', 'ffn1_post_g', 'mix_pre_g', 'w_in', 'mu_prev', 'mu_next',
          'w0', 'w_up', 'a0', 'a_up', 'g_up', 'k_k', 'k_a', 'r_k', 'gn_w', 'gn_b', 'lambda_q1', 'lambda_k1',
          'lambda_q2', 'lambda_k2', 'subln_g', 'w_branch_a', 'w_branch_b', 'w_out', 'mix_post_g', 'ffn2_pre_g',
          'ffn2_w_gu', 'ffn2_w_down', 'ffn2_post_g']


def kernel(**inputs):
    import concourse.bacc as bacc
    from concourse.bass_utils import run_bass_kernel_spmd

    nc = bacc.Bacc("TRN2", target_bir_lowering=False, num_devices=1)
    arrays, a = {}, {}
    consts, sel_t = constants()
    for name, array in [(n, np.ascontiguousarray(inputs[n])) for n in _NAMES] + [("consts", consts), ("sel_t", sel_t)]:
        arrays["in_" + name] = array
        a[name] = nc.dram_tensor("in_" + name, array.shape, F32, kind="ExternalInput").ap()
    out = nc.dram_tensor("out_0", (1, T, D), F32, kind="ExternalOutput").ap()
    layer(nc, a, out)
    r = run_bass_kernel_spmd(nc, [arrays], core_ids=[0])
    return r.results[0]["out_0"]
```

```python
import math
from contextlib import ExitStack

import numpy as np

import concourse.bass as bass
from concourse import mybir

F32 = mybir.dt.float32
F32R = mybir.dt.float32r
ALU = mybir.AluOpType
ACT = mybir.ActivationFunctionType
AX = mybir.AxisListType

P = 128
D = 2048
T = 256
NT = T // P
KB = D // P
FF = ((8 * D // 3 + 255) // 256) * 256
CW = 512
RING = 4
SB = 2
FFC = FF // CW
FF_GROUPS = ((0, 6), (6, FFC))
NPAIR = 8
NH = 16
RW = 1024
LORA = 64
GLORA = 160
RCOLS = 3 * RW + 4 * LORA + GLORA
DCOLS = 3 * 1024
NBLK = -(-RCOLS // P)
C = 64
NC_ = T // C
NM = 2 * NPAIR
EPS = 1e-6
GN_EPS = 64e-5
SUBLN_EPS = 1e-5
LAM_INIT = 0.8 - 0.6 * math.exp(-0.3 * 0)
DECAY = math.exp(-0.5)
QSLOTS = 1 + NM * 3 * NC_ + 2 * NC_
BEFORE_SHIFT, IN_SHIFT, IN_KK, IN_G, IN_CHUNKS = 2, (0, 1), (0, 1), (0, 1), (2, 1)
assert BEFORE_SHIFT + NBLK // 2 * sum(IN_SHIFT) + NPAIR // 2 * (sum(IN_KK) + sum(IN_G)) + NPAIR * sum(IN_CHUNKS) == 48
K_ID, K_SEL, K_HEAD, K_MN, K_M1, K_MG, K_RESET, K_COS, K_SIN, K_END = np.cumsum(
    [0, P, P, P, C, 4 * C, P, T, 2 * 32, 2 * 32]).tolist()
BLOCKS = list(range(24, NBLK)) + list(range(24))
D_MU, D_W0, D_A0, D_KA, D_KA1, D_SUB = 0, 28, 44, 60, 68, 76
R_F1, R_MIX, R_F2, R_MUP, R_MUN, R_W0 = 0, 16, 32, 48, 76, 104
R_A0, R_KK, R_KA, R_RK, R_GNW, R_GNB, R_SUB = 128, 144, 152, 160, 168, 176, 184


def constants():
    k = np.zeros((P, K_END), np.float32)
    p = np.arange(P)[:, None]
    t = np.arange(C)[None, :]
    k[:, K_ID:K_SEL] = np.eye(P)
    bh = np.arange(P)[None, :]
    k[:, K_SEL:K_HEAD] = (bh % NH == 2 * (bh // NH) + p // C)
    k[:, K_HEAD:K_MN] = (p // C == bh // C)
    s = p % C
    k[:, K_MN:K_M1] = -1.0 * (s < t)
    k[:, K_M1:K_MG] = np.concatenate([s <= t, s >= -1 + 0 * t, s >= -1 + 0 * t, t < s], 1)
    k[:, K_MG:K_RESET] = np.concatenate([(p < C) | (s <= t), s >= -1 + 0 * t], 1)
    k[:, K_RESET:K_COS] = (np.arange(T) % C != 0)[None, :]
    inv = np.float32(10000.0) ** (-np.arange(32, dtype=np.float32) / np.float32(32))
    ang = np.arange(T, dtype=np.float32)[:, None] * inv.astype(np.float32)[None, :]
    for i in range(NT):
        k[:, K_COS + 32 * i:K_COS + 32 * (i + 1)] = np.cos(ang[i * P:(i + 1) * P])
        k[:, K_SIN + 32 * i:K_SIN + 32 * (i + 1)] = np.sin(ang[i * P:(i + 1) * P])
    sel_t = (np.arange(NH)[:, None] == (2 * np.arange(NPAIR)[:, None] + np.arange(P)[None, :] // C).reshape(1, -1))
    return k, sel_t.astype(np.float32)


def layer(nc, a, out):
    x, w_in, mix_post_g, w_up, a_up, g_up, w_branch_a, w_branch_b, w_out, consts, sel_t = (
        a[n] for n in ("x", "w_in", "mix_post_g", "w_up", "a_up", "g_up", "w_branch_a", "w_branch_b", "w_out",
                       "consts", "sel_t"))
    ffn = [(a[f"ffn{i}_pre_g"], a[f"ffn{i}_w_gu"], a[f"ffn{i}_w_down"], a[f"ffn{i}_post_g"]) for i in (1, 2)]

    def rows(v):
        return v.rearrange("(b p) -> b p", p=P)

    def by_direction(v):
        return v.rearrange("d (b p) -> (d b) p", p=P)

    whole = (NBLK - 1) * P
    VECTORS = [(rows(ffn[0][0][0]), R_F1, 16), (rows(a["mix_pre_g"][0]), R_MIX, 16), (rows(ffn[1][0][0]), R_F2, 16),
               (rows(a["mu_prev"][0, 0:whole]), R_MUP, NBLK - 1), (a["mu_prev"][0:1, whole:RCOLS], R_MUP + NBLK - 1, 1),
               (rows(a["mu_next"][0, 0:whole]), R_MUN, NBLK - 1), (a["mu_next"][0:1, whole:RCOLS], R_MUN + NBLK - 1, 1),
               (by_direction(a["w0"][0]), R_W0, 16), (by_direction(a["a0"][0]), R_A0, 16), (rows(a["k_k"][0]), R_KK, 8),
               (rows(a["k_a"][0]), R_KA, 8), (a["r_k"][0].rearrange("(b h) p -> b (h p)", h=2), R_RK, 8),
               (rows(a["gn_w"][0]), R_GNW, 8), (rows(a["gn_b"][0]), R_GNB, 8), (a["subln_g"], R_SUB, 1)]
    N_VEC = len(VECTORS)

    class Pass:

        def __init__(self, chunks, slots, unroll, width, source):
            self.n0, self.q0 = Pass.n, Pass.q
            self.chunks, self.slots, self.unroll, self.width, self.source = chunks, slots, unroll, width, source
            self.turns = chunks // unroll
            assert chunks % unroll == 0
            Pass.n += chunks * slots
            Pass.q += chunks
            assert self.turns == 1 or (unroll * slots % RING == 0 and unroll % 2 == 0)

        def end(self, i, u):
            return self.n0 + (i * self.unroll + u + 1) * self.slots

        def uses(self, i, u):
            return (self.q0 + i * self.unroll + u) // 2 if isinstance(i, int) else \
                i * (self.unroll // 2) + (self.q0 + u) // 2

        def pair(self, u):
            return (self.q0 + u) % 2

    Pass.n = Pass.q = 0

    def rows_cols(w, r0, j, c0, width):
        return w[r0 + j * SB * P:r0 + (j + 1) * SB * P, bass.ds(c0, width)].rearrange("(k p) n -> p k n", p=P)

    def gate_up(wgu, f0):
        return lambda i, u, j: rows_cols(wgu, 0, j, u * FF + (f0 + i) * CW, CW)

    def down(wd, f0):
        return lambda i, u, j: rows_cols(wd, f0 * CW, j, (2 * i + u) * CW, CW)

    def make_ffn(w):
        ps = []
        for f0, f1 in FF_GROUPS:
            ps.append((Pass(2 * (f1 - f0), KB // SB, 2, CW, gate_up(w[1][0], f0)),
                       Pass(D // CW, (f1 - f0) * CW // (SB * P), 2, CW, down(w[2][0], f0))))
        return ps

    wi = w_in[0]
    ffn1 = make_ffn(ffn[0])
    p_rw = Pass(6, 8, 2, CW, lambda i, u, j: rows_cols(wi, 0, j, (2 * i + u) * CW, CW))
    p_rw7 = Pass(1, 8, 1, RCOLS - 6 * CW, lambda i, u, j: rows_cols(wi, 0, j, 6 * CW, RCOLS - 6 * CW))
    p_dif = Pass(6, 8, 2, CW, lambda i, u, j: rows_cols(wi, 0, j, RCOLS + (2 * i + u) * CW, CW))
    p_gate = Pass(8, 8, 2, CW, lambda i, u, j: rows_cols(wi, 0, j, RCOLS + DCOLS + (2 * i + u) * CW, CW))
    p_br = Pass(8, 4, 2, CW, lambda i, u, j: rows_cols((w_branch_a[0], w_branch_b[0])[u], 0, j, i * CW, CW))
    p_out = Pass(4, 8, 2, CW, lambda i, u, j: rows_cols(w_out[0], 0, j, (2 * i + u) * CW, CW))
    ffn2 = make_ffn(ffn[1])
    passes = [p for g in ffn1 for p in g] + [p_rw, p_rw7, p_dif, p_gate, p_br, p_out] + [p for g in ffn2 for p in g]

    def scratch(name, shape):
        return nc.dram_tensor(name, shape, F32).ap()

    h_dram = scratch("h_dram", (T, D))
    dif_dram = scratch("dif_dram", (T, DCOLS))
    gate_dram = scratch("gate_dram", (T, 2 * D))
    v_dram = scratch("v_dram", (NPAIR, P, T))
    g_dram = scratch("g_dram", (NPAIR, P, T))
    bonus_dram = scratch("bonus_dram", (NPAIR, P, T))
    n_dram = scratch("n_dram", (2, NM, NC_, C, C))
    z_dram = scratch("z_dram", (2, NM, NC_, C, C))

    ctx = ExitStack()
    with ctx:
        def sem(name):
            return ctx.enter_context(nc.semaphore(name))

        def sb(scope, name, shape, dt=F32):
            return scope.enter_context(nc.sbuf_tensor(name, shape, dt))

        ps = ctx.enter_context(nc.psum_tensor("ps", [P, 8, 512], F32))

        kc = sb(ctx, "kc", [P, K_END])
        vec = sb(ctx, "vec", [P, 256])
        sm = sb(ctx, "sm", [P, 64])
        vecd = sb(ctx, "vecd", [P, 80])
        raw = sb(ctx, "raw", [P, RING, SB, CW])
        whi = sb(ctx, "whi", [P, RING, SB, CW], F32R)
        wlo = sb(ctx, "wlo", [P, RING, SB, CW], F32R)
        uhi = sb(ctx, "uhi", [P, KB, T], F32R)
        ulo = sb(ctx, "ulo", [P, KB, T], F32R)
        ident = kc[:, K_ID:K_SEL]
        headsum = kc[:, K_HEAD:K_MN]

        def room(*names):
            scope = ExitStack()
            tiles = [sb(scope, *n) for n in names]
            return scope, tiles

        def ffn_room(tag):
            return room(("h" + tag, [P, NT, D]), ("f" + tag, [P, NT, D]),
                        ("hthi" + tag, [P, 24, T], F32R), ("htlo" + tag, [P, 24, T], F32R),
                        ("sg" + tag, [P, NT, CW]), ("hm" + tag, [P, NT, CW]), ("gain" + tag, [P, D]))

        s1, F1 = ffn_room("1")
        vrows = F1[1]
        s1.close()
        s_proj, (proj, ybuf, vst, lgd, gupa, gupb, sqb, s16, gst, selt1) = room(
            ("proj", [P, NT, NBLK * P]), ("ybuf", [P, 2, T + 2]), ("vst", [P, 2, T]),
            ("lgd", [P, 2, T]), ("gupa", [P, RW]), ("gupb", [GLORA - P, RW]), ("sqb", [P, 2, T]),
            ("s16", [NH, 2, T]), ("gst", [P, 2, T]), ("selt1", [NH, NPAIR * P]))
        s_proj.close()
        s_q, (q, beta, pend) = room(("q", [P, QSLOTS, C]), ("beta", [P, NM, T]), ("pend", [P, NM, NC_]))
        s_rk, (rr, kr, kkn, wup, aup, lwa) = room(
            ("rr", [P, NPAIR, T]), ("kr", [P, NPAIR, T]), ("kkn", [P, NPAIR, T]),
            ("wup", [P, RW]), ("aup", [P, RW]), ("lwa", [P, 2, T]))
        bst, vb1 = (q[:, QSLOTS - 8 + 4 * i:QSLOTS - 4 + 4 * i, :].rearrange("p c t -> p (c t)") for i in range(2))
        s_e, (dst_a, tz, ie, eie, ld, aa, kd, kds, nst) = room(
            ("dst_a", [P, 2, NT, CW]), ("tz", [P, 2, T]), ("ie", [P, 2, T]), ("eie", [P, 3, T]), ("ld", [P, T]), ("aa", [P, T]), ("kd", [P, T]),
            ("kds", [P, T]), ("nst", [P, 2, NC_, C]))
        s_e.close()
        s_rk.close()
        s_z, (z, zt, _, gst_g) = room(("z", [P, C, C]), ("zt", [P, 32 * 32]), ("z_gap", [P, 24 * 256]),
                                      ("gst_g", [P, 2, NT, CW]))
        s_z.close()
        s_r, (zs, vb, vrev, mb, wt, gh, sv, ik, oc) = room(
            ("zs", [P, NM * NC_, C]), ("vb", [P, T]), ("vrev", [P, T]), ("mb", [P, 2, NC_, 4 * C]),
            ("wt", [P, 2, NC_, 2 * C]), ("gh", [P, 2, 2 * NC_, 2 * C]), ("sv", [P, 2, NC_, 2 * C]), ("ik", [P, NC_, 2 * C]), ("oc", [P, NPAIR, T]))
        s_r.close()
        s_q.close()
        s_y, (ythi, ytlo) = room(("ythi", [P, 16, T], F32R), ("ytlo", [P, 16, T], F32R))
        s_qkv, (qk, va, pa, pb) = room(("qk", [P, NT, 2 * RW]), ("va", [P, NT, RW]), ("pa", [P, RW]), ("pb", [P, RW]))
        s_n, (osq, o16, selt2, bo, gg) = room(
            ("osq", [P, 2, T]), ("o16", [NH, 4, T]), ("selt2", [NH, NPAIR * P]), ("bo", [P, NPAIR, T]), ("gg", [P, NPAIR, T]))
        s_n.close()
        s_t, (ra, rb, qt_, kt_, lamv, lamb, mx, su, pex, am, amt, ov, oj, os_) = room(
            ("ra", [P, RW]), ("rb", [P, RW]), ("qt_", [P, 8, T]),
            ("kt_", [P, 8, T]), ("lamv", [P, 4, 64]), ("lamb", [P, 8]), ("mx", [P, 4, 2]), ("su", [P, 4, 2]),
            ("pex", [P, 4, 2, T]), ("am", [P, 4, T]), ("amt", [P, 4, T]), ("ov", [P, 4, P]), ("oj", [P, 4, P]),
            ("os_", [P, 16]))
        s_t.close()
        s_qkv.close()
        s_m, (gbuf, mg, mt) = room(("gbuf", [P, 2, 2, NT, CW]), ("mg", [P, NT, D]), ("mt", [P, NT, CW]))
        s_m.close()
        s_y.close()
        s2, F2 = ffn_room("2")
        s2.close()

        landed = [sem(f"landed{s}") for s in range(RING)]
        hi_ready = sem("hi_ready")
        lo_ready = sem("lo_ready")
        slots_used = sem("slots_used")
        pair_free = [sem("pair_free0"), sem("pair_free1")]
        act_link, dve_link, pool_link = sem("act_link"), sem("dve_link"), sem("pool_link")
        c_in, x_in, vr_in, par_in = (sem(n) for n in ("c_in", "x_in", "vr_in", "par_in"))
        vr_zero, vec_t, vec_copied, vec_ready = (sem(n) for n in ("vr_zero", "vec_t", "vec_copied", "vec_ready"))
        ss_ready, ms_ready, rstd_ready = (sem(n) for n in ("ss_ready", "ms_ready", "rstd_ready"))
        fs_ready, fg_ready = sem("fs_ready"), sem("fg_ready")
        ut_done, ut_hi, ut_lo = sem("ut_done"), sem("ut_hi"), sem("ut_lo")
        hm_t, ht_hi, ht_lo = sem("hm_t"), sem("ht_hi"), sem("ht_lo")
        gain_in, h_ready, h_saved, h_back, out_done = (sem(n) for n in ("gain_in", "h_ready", "h_saved", "h_back", "out_done"))
        st_out = [sem("st_out0"), sem("st_out1")]
        sh_t, sh_y, shifted, v_out0, v_out1 = (sem(n) for n in ("sh_t", "sh_y", "shifted", "v_out0", "v_out1"))
        lora_act, gd_ready = sem("lora_act"), sem("gd_ready")
        kk_raw, kk_sq, kk_sum, kk_max, kk_sqrt, kk_rec, kk_bc, kk_ready = (
            sem(n) for n in ("kk_raw", "kk_sq", "kk_sum", "kk_max", "kk_sqrt", "kk_rec", "kk_bc", "kk_ready"))
        g_mm, g_st = sem("g_mm"), sem("g_st")
        g_out = [sem("g_out0"), sem("g_out1")]
        za_mm, za_act, ex_in, ex_out, aa_ready, ra_ready, q_ready = (
            sem(n) for n in ("za_mm", "za_act", "ex_in", "ex_out", "aa_ready", "ra_ready", "q_ready"))
        bon_in, bon_mm, bon_st, bon_out, v1_in = (sem(n) for n in ("bon_in", "bon_mm", "bon_st", "bon_out", "v1_in"))
        n_mm, n_st, z_in, z_done, z_out, zs_in = (sem(n) for n in ("n_mm", "n_st", "z_in", "z_done", "z_out", "zs_in"))
        n_out = [sem("n_out0"), sem("n_out1")]
        vb_in = sem("vb_in")
        sv_zero, dd_ready, vt_mm, vt_ready, ab_mm, ab_ready, w_mm, w_ready, gh_mm, gh_ready = (
            sem(n) for n in ("sv_zero", "dd_ready", "vt_mm", "vt_ready", "ab_mm", "ab_ready", "w_mm", "w_ready",
                             "gh_mm", "gh_ready"))
        s_mm, s_ready, o_mm, o_ready = sem("s_mm"), sem("s_ready"), sem("o_mm"), sem("o_ready")
        gn_sum, gn_mean, gn_bc, gn_cent, gn_sq, gn_var, gn_varv, gn_sqrt, gn_rec, gn_bc2, gn_in, ya_y, ya_hi, ya_lo = (
            sem(n) for n in ("gn_sum", "gn_mean", "gn_bc", "gn_cent", "gn_sq", "gn_var", "gn_varv", "gn_sqrt",
                             "gn_rec", "gn_bc2", "gn_in", "ya_y", "ya_hi", "ya_lo"))
        at_in, lam_sum, lam_exp, lam_ready, roped, qt_mm, qt_ready = (
            sem(n) for n in ("at_in", "lam_sum", "lam_exp", "lam_ready", "roped", "qt_mm", "qt_ready"))
        sc_mm, mx_ready, ex_p, am_ready, am_t, amt_ready, pv_mm, pv_sq, pv_ms, pv_rs, yb_ready, yb_t, yb_hi, yb_lo = (
            sem(n) for n in ("sc_mm", "mx_ready", "ex_p", "am_ready", "am_t", "amt_ready", "pv_mm", "pv_sq", "pv_ms",
                             "pv_rs", "yb_ready", "yb_t", "yb_hi", "yb_lo"))
        vr_ready, ik_ready = sem("vr_ready"), sem("ik_ready")
        k_in, k_roped = sem("k_in"), sem("k_roped")
        gt_in = [sem("gt_in0"), sem("gt_in1")]
        mg_ready = sem("mg_ready")

        SS = {e: slice(6 * e, 6 * e + 2) for e in range(6)}
        MS = {e: slice(6 * e + 2, 6 * e + 4) for e in range(6)}
        RS = {e: slice(6 * e + 4, 6 * e + 6) for e in range(6)}
        HALF = slice(40, 48)
        QS = slice(48, 56)

        def slot_of(p, u, j):
            return (p.n0 + u * p.slots + j) % RING

        def walk(eng, p, slot, hooks=(), carried=(), skip=0):
            def turn(i, first):
                for k in range(p.unroll * p.slots):
                    if not (first and k < skip):
                        slot(p.n0 + i * (p.unroll * p.slots) + k, i, k // p.slots, k % p.slots)
                    for at, fn in carried if first else ():
                        if at == k:
                            fn()
                    for at, lag, fn in hooks:
                        if at == k and not (first and lag):
                            fn(i - lag)
            turn(0, True)
            if p.turns > 1:
                with eng.Fori(1, p.turns) as i:
                    turn(i, False)
            return [(at, (lambda fn=fn: fn(p.turns - 1))) for at, lag, fn in hooks if lag]

        def in_steps(p, slot, hooks, then):
            for n in range(p.chunks * p.slots):
                i, k = divmod(n, p.unroll * p.slots)
                slot(p.n0 + n, i, k // p.slots, k % p.slots)
                for at, lag, fn in hooks:
                    if at == k and i >= lag:
                        fn(i - lag)
                yield
            for fn in then:
                fn()
                yield

        def filler(steps):
            def fill(k):
                for _ in range(k):
                    next(steps, None)
            return fill

        LEAD = RING - 1

        def each_chunk(p, fn):
            if p.unroll == 1:
                return [(3, 1, lambda i: fn(i, 0))]
            return [(3, 1, lambda i: fn(i, 1)), (p.slots + 3, 0, lambda i: fn(i, 0))]

        def ut_base(e):
            return KB * e

        def rstd(e, t):
            return sm[:, 6 * e + 4 + t:6 * e + 5 + t]

        H_PARTS = NT * (D // CW)

        block = ctx.enter_context(nc.Block())

        @block.sync
        def _(sp):
            for p in passes:
                def load(n, i, u, j, p=p):
                    s = slot_of(p, u, j)
                    if not (isinstance(n, int) and n < RING):
                        sp.wait_ge(lo_ready, n - RING + 1)
                    sp.dma_start(raw[:, s, :, 0:p.width], p.source(i, u, j)).then_inc(landed[s], 16)
                walk(sp, p, load)

        def rope(engine, x_, t, a_, b_, done, before, queue):
            cos = kc[:, K_COS + 32 * t:K_COS + 32 * t + 32].unsqueeze(1).unsqueeze(1).broadcast_to((P, 16, 2, 32))
            sin = kc[:, K_SIN + 32 * t:K_SIN + 32 * t + 32].unsqueeze(1).unsqueeze(1).broadcast_to((P, 16, 2, 32))
            xv, av, bv = (w[:, :].rearrange("p (h s f) -> p h s f", h=16, s=2) for w in (x_, a_, b_))
            engine.tensor_tensor(av, xv, cos, ALU.mult)
            engine.tensor_tensor(bv, xv[:, :, ::-1, :], sin, ALU.mult).then_inc(done, 1)
            queue.wait_ge(done, 2 * before + 1)
            engine.tensor_tensor(xv[:, :, 0, :], av[:, :, 0, :], bv[:, :, 0, :], ALU.subtract)
            engine.tensor_tensor(xv[:, :, 1, :], av[:, :, 1, :], bv[:, :, 1, :], ALU.add).then_inc(done, 1)
            queue.wait_ge(done, 2 * before + 2)

        @block.scalar
        def _(act):
            links = [0]

            def link(ins):
                links[0] += 1
                ins.then_inc(act_link, 1)
                act.wait_ge(act_link, links[0])

            def split_hi(p):
                def slot(n, i, u, j):
                    s = slot_of(p, u, j)
                    k = p.n0 + u * p.slots + j
                    act.wait_ge(landed[s], i * (16 * p.unroll * p.slots // RING) + 16 * (k // RING + 1))
                    if not (isinstance(n, int) and n < RING):
                        act.wait_ge(slots_used, n - RING + 1)
                    nc.scalar.activation(whi[:, s, :, 0:p.width], raw[:, s, :, 0:p.width], ACT.Copy).then_inc(hi_ready, 1)
                return slot

            def ahead(p):
                for k in range(RING):
                    split_hi(p)(p.n0 + k, 0, 0, k)

            def sum_squares(nth, e, src, junk):
                for t in range(NT):
                    nc.scalar.activation(junk, src[:, t, :], ACT.Square,
                                         accum_out=sm[:, 6 * e + t:6 * e + t + 1]).then_inc(ss_ready, 1)
                    if t + 1 < NT:
                        act.wait_ge(ss_ready, NT * nth + t + 1)

            def transposed_hi(e, col):
                for k in range(KB):
                    act.wait_ge(ut_done, ut_base(e) + k + 1)
                    bank = ps[:, 4 + k % 4, 0:T]
                    if col is None:
                        nc.scalar.activation(uhi[:, k, :], bank, ACT.Copy).then_inc(ut_hi, 1)
                    else:
                        nc.scalar.activation(uhi[:, k, :], bank, ACT.Identity,
                                             scale=vec[:, col + k:col + k + 1]).then_inc(ut_hi, 1)

            def chunk_squares(p, nth, F):
                def fn(i, u):
                    c = 2 * i + u
                    act.wait_ge(pair_free[p.pair(u)], p.uses(i, u) + 1)
                    if not (isinstance(c, int) and 4 * nth + c == 0):
                        act.wait_ge(fs_ready, 4 * nth + c)
                    for t in range(NT):
                        last = nc.scalar.activation(F[4][:, t, :], F[1][:, t, bass.ds(c * CW, CW)], ACT.Square,
                                                    accum_out=sm[:, bass.ds(QS.start + 4 * t + c, 1)])
                    last.then_inc(fs_ready, 1)
                return fn

            def feed_forward(w, F, groups, e, pre_split):
                h, f, hthi, htlo, sg, hm, gain = F

                def group(g, gu, dn, carried):
                    f0, f1 = FF_GROUPS[g]
                    fb = w * FFC + f0

                    def silu(i):
                        if not (isinstance(i, int) and gu.uses(i, 1) == 0):
                            act.wait_ge(pair_free[gu.pair(1)], gu.uses(i, 1))
                        act.wait_ge(slots_used, gu.end(i, 0))
                        for t in range(NT):
                            last = nc.scalar.activation(sg[:, t, :], ps[:, 2 * gu.pair(0) + t, :], ACT.Silu,
                                                        scale=rstd(e, t))
                        last.then_inc(pair_free[gu.pair(0)], 1)

                    def h_hi(i):
                        for b in range(2):
                            act.wait_ge(hm_t, 2 * (fb + i) + b + 1)
                            nc.scalar.activation(hthi[:, bass.ds(4 * i + 2 * b, 2), :],
                                                 ps[:, 4 + b, :].rearrange("p (k t) -> p k t", k=2),
                                                 ACT.Copy).then_inc(ht_hi, 1)

                    carried = walk(act, gu, split_hi(gu), [(9, 1, h_hi), (11, 0, silu)], carried,
                                   skip=RING if g == 0 and pre_split else 0)
                    carried = walk(act, dn, split_hi(dn), each_chunk(dn, chunk_squares(dn, 2 * w, F)) if g else [], carried)
                    return carried

                carried = []
                for g, (gu, dn) in enumerate(groups):
                    carried = group(g, gu, dn, carried)
                for _, fn in carried:
                    fn()

            act.dma_start(kc[:, :], consts).then_inc(c_in, 16)
            act.dma_start(F1[0][:, :, :], x[0].rearrange("(t p) d -> p t d", p=P)).then_inc(x_in, 16)
            ahead(passes[0])
            act.wait_ge(x_in, 16)
            junk1 = F1[2][:, 0:8, :].rearrange("p k t -> p (k t)")
            junk2 = F2[2][:, 0:8, :].rearrange("p k t -> p (k t)")
            act.wait_ge(vec_t, 1)
            nc.scalar.activation(vec[:, :], ps[:, 4, 0:256], ACT.Copy).then_inc(vec_copied, 1)
            act.wait_ge(vec_copied, 1)
            transposed_hi(0, R_F1)
            sum_squares(0, 0, F1[0], junk1)
            act.wait_ge(rstd_ready, 1)
            feed_forward(0, F1, ffn1, 0, True)
            ahead(p_rw)
            transposed_hi(1, R_MIX)
            sum_squares(1, 2, F1[0], junk1)
            act.wait_ge(rstd_ready, 3)

            def to_proj(p, c0):
                def fn(i, u):
                    act.wait_ge(slots_used, p.end(i, u))
                    for t in range(NT):
                        last = nc.scalar.activation(proj[:, t, bass.ds((p.unroll * i + u) * CW + c0, p.width)],
                                                    ps[:, 2 * p.pair(u) + t, 0:p.width], ACT.Identity, scale=rstd(2, t))
                    last.then_inc(pair_free[p.pair(u)], 1)
                return fn

            def to_stage(p, tile, func, before):
                def fn(i, u):
                    act.wait_ge(slots_used, p.end(i, u))
                    b = p.pair(u)
                    if not (isinstance(i, int) and i + before == 0):
                        act.wait_ge(st_out[b], 16 * i + 16 * before)
                    for t in range(NT):
                        last = nc.scalar.activation(tile[:, b, t, :], ps[:, 2 * b + t, :], func, scale=rstd(2, t))
                    last.then_inc(pair_free[b], 1)
                return fn

            act.wait_ge(h_saved, 16)
            carried = walk(act, p_rw, split_hi(p_rw), each_chunk(p_rw, to_proj(p_rw, 0)), (), skip=RING)
            carried = walk(act, p_rw7, split_hi(p_rw7), each_chunk(p_rw7, to_proj(p_rw7, 6 * CW)), carried)
            for _, fn in carried:
                fn()
            dif_out = to_stage(p_dif, dst_a, ACT.Identity, 0)
            first_gates = [lambda k=k: split_hi(p_gate)(p_gate.n0 + k, 0, 0, k) for k in range(RING)]
            fill = filler(in_steps(p_dif, split_hi(p_dif), each_chunk(p_dif, dif_out),
                                   first_gates[:-1] + [lambda: (first_gates[-1](), dif_out(2, 1))]))
            fill(LEAD + BEFORE_SHIFT)

            for n in range(NBLK):
                w = 32 if BLOCKS[n] == NBLK - 1 else P
                act.wait_ge(sh_t, n + 1)
                if n >= 2:
                    act.wait_ge(shifted, n - 1)
                nc.scalar.activation(ybuf[0:w, n % 2, 1:T + 1], ps[0:w, 4 + n % 4, 0:T], ACT.Copy).then_inc(sh_y, 1)
                fill(IN_SHIFT[n % 2])
            act.wait_ge(shifted, 4)
            nc.scalar.activation(lwa[:, 0, :], lwa[:, 0, :], ACT.Tanh).then_inc(lora_act, 1)
            act.wait_ge(shifted, NBLK)
            nc.scalar.activation(lgd[:, 0, :], lgd[:, 0, :], ACT.Tanh, scale=0.5)
            nc.scalar.activation(lgd[0:32, 1, :], lgd[0:32, 1, :], ACT.Tanh, scale=0.5).then_inc(lora_act, 1)
            for b in range(NPAIR):
                nc.scalar.activation(kkn[:, b, :], kr[:, b, :], ACT.Identity,
                                     scale=vec[:, R_KK + b:R_KK + b + 1]).then_inc(kk_raw, 1)
                act.wait_ge(kk_raw, b + 1)
                if b >= 2:
                    act.wait_ge(kk_sum, b - 1)
                nc.scalar.activation(sqb[:, b % 2, :], kkn[:, b, :], ACT.Square).then_inc(kk_sq, 1)
                fill(IN_KK[b % 2])
            act.wait_ge(kk_max, 1)
            nc.scalar.activation(s16[:, 1, :], s16[:, 0, :], ACT.Sqrt).then_inc(kk_sqrt, 1)
            for b in range(NPAIR):
                act.wait_ge(g_mm, b + 1)
                if b >= 2:
                    act.wait_ge(g_out[b % 2], 16 * (b // 2))
                nc.scalar.activation(gst[:, b % 2, :], ps[:, 4 + b % 2, 0:T], ACT.Copy).then_inc(g_st, 1)
                fill(IN_G[b % 2])
            act.wait_ge(kk_ready, NPAIR)
            act.wait_ge(g_out[0], 16 * (NPAIR // 2))
            act.wait_ge(g_out[1], 16 * (NPAIR // 2))
            n_out_dst = n_dram.rearrange("h m c s t -> h m s c t")

            def stage_out(m):
                act.wait_ge(n_st, m + 1)
                for h in range(2):
                    act.dma_start(n_out_dst[h, m], nst[C * h:C * (h + 1), m % 2, :, :]).then_inc(n_out[m % 2], 16)

            for m in range(NM):
                b, d = m // 2, m % 2
                act.wait_ge(za_mm, m + 1)
                if m:
                    act.wait_ge(aa_ready, m)
                for w, col in ((0, D_W0), (1, D_A0)):
                    last = nc.scalar.activation(tz[:, w, :], ps[:, 4 + m % 2, w * T:(w + 1) * T], ACT.Tanh, scale=0.5,
                                                bias=vecd[:, col + 8 * d + b:col + 8 * d + b + 1])
                last.then_inc(za_act, 1)
                act.wait_ge(ex_in, m + 1)
                if m:
                    act.wait_ge(q_ready, m)
                    act.wait_ge(ra_ready, 2 * m)
                nc.scalar.activation(eie[:, 0:2, :], ie[:, :, :], ACT.Exp)
                nc.scalar.activation(eie[:, 2, :], ie[:, 0, :], ACT.Exp, scale=-1.0).then_inc(ex_out, 1)
                fill(IN_CHUNKS[m % 2])
                if m >= 2:
                    stage_out(m - 2)
            stage_out(NM - 2)
            stage_out(NM - 1)
            fill(1)

            carried = walk(act, p_gate, split_hi(p_gate), each_chunk(p_gate, to_stage(p_gate, gst_g, ACT.Sigmoid, 3)), (), skip=RING)
            for _, fn in carried:
                fn()
            ahead(p_br)

            act.wait_ge(zs_in, 32)
            for b in range(2):
                act.wait_ge(st_out[b], 16 * 7)

            def values(m):
                act.wait_ge(vt_mm, m + 1)
                if m >= 2:
                    act.wait_ge(o_mm, m - 1)
                nc.scalar.activation(sv[C:P, m % 2, :, :], ps[C:P, 2, :].rearrange("p (c v) -> p c v", c=NC_),
                                     ACT.Copy).then_inc(vt_ready, 1)

            def minus_w(m):
                act.wait_ge(w_mm, m + 1)
                nc.scalar.activation(wt[:, m % 2, :, :], ps[:, 3, :].rearrange("p (c v) -> p c v", c=NC_),
                                     ACT.Copy, scale=-1.0).then_inc(w_ready, 1)

            minus_w(0)
            values(0)
            for m in range(NM):
                if m + 1 < NM:
                    minus_w(m + 1)
                    values(m + 1)
                for c in range(NC_ - 1):
                    act.wait_ge(s_mm, 3 * m + c + 1)
                    nc.scalar.activation(sv[0:C, m % 2, c + 1, :], ps[0:C, 6, 0:2 * C], ACT.Copy).then_inc(s_ready, 1)
            for b in range(NPAIR):
                act.wait_ge(gn_cent, b + 1)
                if b >= 2:
                    act.wait_ge(gn_var, b - 1)
                nc.scalar.activation(osq[:, b % 2, :], oc[:, b, :], ACT.Square).then_inc(gn_sq, 1)
            act.wait_ge(gn_varv, 1)
            nc.scalar.activation(o16[:, 2, :], o16[:, 1, :], ACT.Sqrt).then_inc(gn_sqrt, 1)
            for b in range(NPAIR):
                act.wait_ge(ya_y, b + 1)
                nc.scalar.activation(ythi[:, b, :], oc[:, b, :], ACT.Copy).then_inc(ya_hi, 1)

            act.wait_ge(lam_sum, 1)
            nc.scalar.activation(lamb[:, 2:4], lamb[:, 0:2], ACT.Exp).then_inc(lam_exp, 1)
            for n in range(16):
                act.wait_ge(qt_mm, n + 1)
                dst = (qt_, kt_)[n // 8][:, n % 8, :]
                nc.scalar.activation(dst, ps[:, 4 + n % 4, 0:T], ACT.Copy).then_inc(qt_ready, 1)

            def exps(g):
                for v in range(4):
                    act.wait_ge(mx_ready, 2 * g + v // 2 + 1)
                    if g:
                        act.wait_ge(am_ready, 4 * (g - 1) + v + 1)
                    for s in range(2):
                        last = nc.scalar.activation(pex[:, v, s, :], ps[:, 2 * (v // 2) + s, (v % 2) * T:(v % 2 + 1) * T],
                                                    ACT.Exp, scale=0.125, bias=mx[:, v, s:s + 1], accum_out=su[:, v, s:s + 1])
                    last.then_inc(ex_p, 1)
                for v2 in range(2):
                    act.wait_ge(am_t, 2 * g + v2 + 1)
                    if g:
                        act.wait_ge(pv_mm, g)
                    nc.scalar.activation(amt[:, 2 * v2:2 * v2 + 2, :], ps[:, 4 + v2, :].rearrange("p (v t) -> p v t", v=2),
                                         ACT.Copy).then_inc(amt_ready, 1)

            exps(0)
            for g in range(4):
                act.wait_ge(pv_mm, g + 1)
                if g:
                    act.wait_ge(pv_ms, g)
                for v in range(4):
                    last = nc.scalar.activation(oj[:, v, :], ps[:, 6, v * P:(v + 1) * P], ACT.Square,
                                                accum_out=os_[:, v:v + 1])
                last.then_inc(pv_sq, 1)
                if g + 1 < 4:
                    exps(g + 1)
                act.wait_ge(yb_t, g + 1)
                hs, t = 4 * (g % 2), g // 2
                nc.scalar.activation(ythi[:, 8 + hs:12 + hs, t * P:(t + 1) * P],
                                     ps[:, 7, :].rearrange("p (v t) -> p v t", v=4), ACT.Identity,
                                     scale=vecd[:, D_SUB:D_SUB + 1]).then_inc(yb_hi, 1)

            walk(act, p_br, split_hi(p_br), [], (), skip=RING)
            ahead(p_out)
            transposed_hi(2, None)
            for _, fn in walk(act, p_out, split_hi(p_out), each_chunk(p_out, chunk_squares(p_out, 1, F2)), (), skip=RING):
                fn()
            ahead(ffn2[0][0])
            transposed_hi(3, R_F2)
            sum_squares(2, 4, F2[0], junk2)
            act.wait_ge(rstd_ready, 5)
            feed_forward(1, F2, ffn2, 4, True)

        @block.vector
        def _(dve):
            links = [0]

            def link(ins):
                links[0] += 1
                ins.then_inc(dve_link, 1)
                dve.wait_ge(dve_link, links[0])

            V = nc.vector

            def split_lo(p):
                def slot(n, i, u, j):
                    s = slot_of(p, u, j)
                    dve.wait_ge(hi_ready, n + 1)
                    V.tensor_tensor(wlo[:, s, :, 0:p.width], raw[:, s, :, 0:p.width],
                                    whi[:, s, :, 0:p.width].bitcast(F32), ALU.subtract).then_inc(lo_ready, 1)
                return slot

            def ahead(p):
                for k in range(RING):
                    split_lo(p)(p.n0 + k, 0, 0, k)

            def mean_square(nth, e):
                dve.wait_ge(ss_ready, NT * (nth + 1))
                V.tensor_scalar(sm[:, MS[e]], sm[:, SS[e]], 1.0 / D, EPS, ALU.mult, ALU.add).then_inc(ms_ready, 1)

            def times_gain(p, nth, F):
                def fn(i, u):
                    c = 2 * i + u
                    dve.wait_ge(fs_ready, 4 * nth + c + 1)
                    dve.wait_ge(gain_in, 16 * (nth + 1))
                    f = F[1][:, :, bass.ds(c * CW, CW)]
                    V.tensor_tensor(f, f, F[6][:, bass.ds(c * CW, CW)].unsqueeze(1).broadcast_to((P, NT, CW)),
                                    ALU.mult).then_inc(fg_ready, 1)
                return fn

            def gain_hooks(p, nth, F):
                fn = times_gain(p, nth, F)
                return [(5, 1, lambda i: fn(i, 1)), (p.slots + 5, 0, lambda i: fn(i, 0))]

            def transposed_lo(e, col, first=None):
                for k in range(KB):
                    if first is not None and k in (6, 10):
                        split_lo(first)(first.n0 + (2 if k == 6 else 3), 0, 0, 2 if k == 6 else 3)
                    dve.wait_ge(ut_hi, ut_base(e) + k + 1)
                    bank, hi = ps[:, 4 + k % 4, 0:T], uhi[:, k, :].bitcast(F32)
                    if col is None:
                        V.tensor_tensor(ulo[:, k, :], bank, hi, ALU.subtract).then_inc(ut_lo, 1)
                    else:
                        V.scalar_tensor_tensor(out=ulo[:, k, :], in0=bank, scalar=vec[:, col + k:col + k + 1], in1=hi,
                                               op0=ALU.mult, op1=ALU.subtract).then_inc(ut_lo, 1)

            def post_norm(e, nth, F, weight, first=None):
                h, f = F[0], F[1]
                dve.wait_ge(fs_ready, 4 * (nth + 1))
                link(V.tensor_reduce(sm[:, SS[e]], sm[:, QS].rearrange("p (t c) -> p t c", t=NT), AX.X, ALU.add))
                V.tensor_scalar(sm[:, MS[e]], sm[:, SS[e]], 1.0 / D / weight ** 2, EPS / weight ** 2,
                                ALU.mult, ALU.add).then_inc(ms_ready, 1)
                times_gain(None, nth, F)(1, 1)
                if first is not None:
                    for k in range(2):
                        split_lo(first)(first.n0 + k, 0, 0, k)
                dve.wait_ge(rstd_ready, e + 1)
                dve.wait_ge(fg_ready, 4 * (nth + 1))
                for c in range(D // CW):
                    for t in range(NT):
                        hc = h[:, t, c * CW:(c + 1) * CW]
                        V.scalar_tensor_tensor(out=hc, in0=f[:, t, c * CW:(c + 1) * CW], scalar=rstd(e, t), in1=hc,
                                               op0=ALU.mult, op1=ALU.add).then_inc(h_ready, 1)

            def feed_forward(w, F, groups, e):
                h, f, hthi, htlo, sg, hm, gain = F

                def group(g, gu, dn, carried):
                    f0, f1 = FF_GROUPS[g]
                    fb = w * FFC + f0

                    def times_up(i):
                        dve.wait_ge(pair_free[gu.pair(0)], gu.uses(i, 0) + 1)
                        dve.wait_ge(slots_used, gu.end(i, 1))
                        for t in range(NT):
                            last = V.scalar_tensor_tensor(out=hm[:, t, :], in0=ps[:, 2 * gu.pair(1) + t, :],
                                                          scalar=rstd(e, t), in1=sg[:, t, :], op0=ALU.mult, op1=ALU.mult)
                        last.then_inc(pair_free[gu.pair(1)], 1)

                    def h_lo(i):
                        for b in range(2):
                            dve.wait_ge(ht_hi, 2 * (fb + i) + b + 1)
                            V.tensor_tensor(htlo[:, bass.ds(4 * i + 2 * b, 2), :],
                                            ps[:, 4 + b, :].rearrange("p (k t) -> p k t", k=2),
                                            hthi[:, bass.ds(4 * i + 2 * b, 2), :].bitcast(F32),
                                            ALU.subtract).then_inc(ht_lo, 1)

                    def to_f(i, u):
                        dve.wait_ge(slots_used, dn.end(i, u))
                        for t in range(NT):
                            dst, src = f[:, t, bass.ds((2 * i + u) * CW, CW)], ps[:, 2 * dn.pair(u) + t, :]
                            last = V.tensor_tensor(dst, dst, src, ALU.add) if g else V.tensor_copy(dst, src)
                        last.then_inc(pair_free[dn.pair(u)], 1)

                    carried = walk(dve, gu, split_lo(gu), [(3, 1, times_up), (9, 1, h_lo)], carried,
                                   skip=RING if g == 0 else 0)
                    carried = walk(dve, dn, split_lo(dn), each_chunk(dn, to_f) + (gain_hooks(dn, 2 * w, F) if g else []), carried)
                    return carried

                carried = []
                for g, (gu, dn) in enumerate(groups):
                    carried = group(g, gu, dn, carried)
                carried[0][1]()

            V.memset(vrows[:, 0, 0:256], 0.0).then_inc(vr_zero, 1)
            ahead(passes[0])
            dve.wait_ge(c_in, 16)
            transposed_lo(0, R_F1)
            dve.wait_ge(vec_copied, 1)
            link(V.tensor_tensor(vecd[:, 0:28], vec[:, R_MUP:R_MUP + 28], vec[:, R_MUN:R_MUN + 28], ALU.add))
            link(V.tensor_scalar(vecd[:, 0:28], vecd[:, 0:28], -1.0, 1.0, ALU.mult, ALU.add))
            V.tensor_scalar(vecd[:, 28:44], vec[:, R_W0:R_W0 + 16], 0.5, None, ALU.mult)
            V.tensor_scalar(vecd[:, 44:60], vec[:, R_A0:R_A0 + 16], 0.5, None, ALU.mult)
            V.tensor_scalar(vecd[:, 60:68], vec[:, R_KA:R_KA + 8], 0.5, None, ALU.mult)
            V.tensor_scalar(vecd[:, 68:76], vec[:, R_KA:R_KA + 8], -0.5, 1.0, ALU.mult, ALU.add)
            V.tensor_scalar(vecd[:, 76:77], vec[:, R_SUB:R_SUB + 1], 1.0 - LAM_INIT, None, ALU.mult).then_inc(vec_ready, 1)
            mean_square(0, 0)
            dve.wait_ge(rstd_ready, 1)
            feed_forward(0, F1, ffn1, 0)
            post_norm(1, 0, F1, 0.5, p_rw)
            transposed_lo(1, R_MIX, p_rw)
            mean_square(1, 2)
            for p in (p_rw, p_rw7):
                walk(dve, p, split_lo(p), [], (), skip=RING if p is p_rw else 0)
            fill = filler(in_steps(p_dif, split_lo(p_dif), [],
                                   [lambda k=k: split_lo(p_gate)(p_gate.n0 + k, 0, 0, k) for k in range(RING)]))
            fill(LEAD + BEFORE_SHIFT)

            dve.wait_ge(h_saved, 16)
            for i in range(2):
                V.memset(ybuf[:, i, 0:1], 0.0)
                link(V.memset(ybuf[:, i, T + 1:T + 2], 0.0))
            for n, j in enumerate(BLOCKS):
                w = 32 if j == NBLK - 1 else P
                kind, b = j // 8, j % 8
                if kind == 2 and b >= 2:
                    dve.wait_ge((v_out0, v_out1)[b % 2], 16 * (b // 2))
                tile, at = ((rr, b), (kr, b), (vst, b % 2), (lwa, b) if b < 2 else (lgd, b - 2))[kind]
                dst = tile[0:w, at, :]
                y = ybuf[0:w, n % 2, :]
                dve.wait_ge(sh_y, n + 1)
                link(V.tensor_scalar(dst, y[:, 1:T + 1], vecd[0:w, j:j + 1], None, ALU.mult))
                link(V.scalar_tensor_tensor(out=dst, in0=y[:, 0:T], scalar=vec[0:w, R_MUP + j:R_MUP + j + 1], in1=dst,
                                            op0=ALU.mult, op1=ALU.add))
                V.scalar_tensor_tensor(out=dst, in0=y[:, 2:T + 2], scalar=vec[0:w, R_MUN + j:R_MUN + j + 1], in1=dst,
                                       op0=ALU.mult, op1=ALU.add).then_inc(shifted, 1)
                fill(IN_SHIFT[n % 2])
            dve.wait_ge(lora_act, 2)
            link(V.tensor_scalar(lgd[0:32, 1, :], lgd[0:32, 1, :], 0.5, 0.5, ALU.mult, ALU.add))
            V.tensor_scalar(lgd[:, 0, :], lgd[:, 0, :], 0.5, 0.5, ALU.mult, ALU.add).then_inc(gd_ready, 1)
            fill(sum(IN_KK) * NPAIR // 2)
            dve.wait_ge(kk_sum, NPAIR)
            V.tensor_scalar(s16[:, 0, :], ps[0:NH, 6, 0:T], 1e-24, None, ALU.max).then_inc(kk_max, 1)
            dve.wait_ge(kk_sqrt, 1)
            V.reciprocal(s16[:, 0, :], s16[:, 1, :]).then_inc(kk_rec, 1)
            fill(sum(IN_G) * NPAIR // 2)
            for b in range(NPAIR):
                dve.wait_ge(kk_bc, b + 1)
                V.tensor_tensor(kkn[:, b, :], kkn[:, b, :], ps[:, 6 + b % 2, 0:T], ALU.mult).then_inc(kk_ready, 1)
            dve.wait_ge(v_out0, 16 * 4)
            dve.wait_ge(v_out1, 16 * 4)
            V.tensor_copy(q[0:C, 0, :], ident[0:C, 0:C])
            link(V.tensor_copy(q[C:P, 0, :], ident[C:P, C:P]))
            dve.wait_ge(g_out[0], 16 * (NPAIR // 2))
            dve.wait_ge(g_out[1], 16 * (NPAIR // 2))
            dve.wait_ge(kk_ready, NPAIR)

            def n_evac(m):
                dve.wait_ge(n_mm, m + 1)
                if m >= 2:
                    dve.wait_ge(n_out[m % 2], 32 * (m // 2))
                V.tensor_tensor(nst[:, m % 2, :, :], ps[:, 6 + m % 2, 0:T].rearrange("p (c t) -> p c t", c=NC_),
                                kc[:, K_MN:K_M1].unsqueeze(1).broadcast_to((P, NC_, C)), ALU.mult).then_inc(n_st, 1)

            def bonus(b):
                dve.wait_ge(bon_mm, b + 1)
                dve.wait_ge(v1_in, 16 * (b + 1))
                if b:
                    dve.wait_ge(bon_out, 16 * b)
                V.tensor_tensor(bst[:, :], ps[:, 6, T:2 * T], vb1[:, :], ALU.mult).then_inc(bon_st, 1)

            for m in range(NM):
                b, d = m // 2, m % 2
                sgn = slice(None, None, -1) if d else slice(None)
                r_, k_, kk_ = rr[:, b, sgn], kr[:, b, sgn], kkn[:, b, sgn]
                dve.wait_ge(za_act, m + 1)
                link(V.tensor_scalar(ld[:, :], tz[:, 0, :], -0.5 * DECAY, -0.5 * DECAY, ALU.mult, ALU.add))
                if m:
                    dve.wait_ge(ex_out, m)
                link(V.tensor_tensor_scan(ie[:, 0, :], kc[:, K_RESET:K_COS], ld[:, :], 0.0, ALU.mult, ALU.add))
                V.tensor_tensor(ie[:, 1, :], ie[:, 0, :], ld[:, :], ALU.subtract).then_inc(ex_in, 1)
                if d == 0 and b:
                    dve.wait_ge(bon_in, b)
                link(V.tensor_scalar(kd[:, :], tz[:, 1, :], vecd[:, 60 + b:61 + b], vecd[:, 68 + b:69 + b],
                                     ALU.mult, ALU.add))
                V.tensor_scalar(aa[:, :], tz[:, 1, :], 0.5, 0.5, ALU.mult, ALU.add).then_inc(aa_ready, 1)
                dve.wait_ge(aa_ready, m + 1)
                link(V.tensor_tensor(kd[:, :], kd[:, :], k_, ALU.mult))
                link(V.tensor_tensor(aa[:, :], aa[:, :], kk_, ALU.mult))
                if d == 0:
                    if b:
                        dve.wait_ge(bon_mm, b)
                    link(V.tensor_copy(kds[:, :], kd[:, :]))
                else:
                    link(V.tensor_tensor(kds[:, :], kds[:, :], kd[:, ::-1], ALU.add))
                    V.scalar_tensor_tensor(out=kds[:, :], in0=kds[:, :], scalar=vec[:, R_RK + b:R_RK + b + 1],
                                           in1=rr[:, b, :], op0=ALU.mult, op1=ALU.mult).then_inc(bon_in, 1)
                dve.wait_ge(ex_out, m + 1)
                s0 = 1 + 3 * NC_ * m
                qv = q[:, s0:s0 + 3 * NC_, :].rearrange("p (c w) t -> p c w t", w=3)
                ch = lambda a: a.rearrange("p (c t) -> p c t", c=NC_)
                V.tensor_tensor(qv[:, :, 1, :], ch(kd[:, :]), ch(eie[:, 2, :]), ALU.mult)
                V.tensor_tensor(beta[:, m, :], aa[:, :], eie[:, 2, :], ALU.mult)
                V.tensor_copy(pend[:, m, :], ch(eie[:, 0, :])[:, :, C - 1]).then_inc(q_ready, 1)
                if m:
                    n_evac(m - 1)
                if d == 0 and b:
                    bonus(b - 1)
                fill(IN_CHUNKS[d])
            n_evac(NM - 1)
            bonus(NPAIR - 1)
            fill(1)

            ones = z[:, :, :].rearrange("p c t -> p (c t)")[:, 0:C * C:C + 1]

            def steps_before(k):
                first, last = 8, slots - 11
                return min(max(k - first, 0) * (C - 1) // (last - first), C - 1)

            def step(s):
                if s == 0:
                    dve.wait_ge(z_in, 16)
                    link(V.memset(ones, 1.0))
                    return
                if s >= C - 1:
                    return
                n = C - 1 - s
                prod = zt[:, 0:s * n].rearrange("p (c t) -> p c t", c=s)
                rest = z[:, 0:s, s + 1:C]
                link(V.tensor_tensor(prod, z[:, 0:s, s:s + 1].broadcast_to((P, s, n)),
                                     z[:, s:s + 1, s + 1:C].broadcast_to((P, s, n)), ALU.mult))
                if s == C - 2:
                    V.tensor_tensor(rest, rest, prod, ALU.add).then_inc(z_done, 1)
                else:
                    link(V.tensor_tensor(rest, rest, prod, ALU.add))

            slots = p_gate.chunks * p_gate.slots
            for k in range(slots):
                if k >= RING:
                    split_lo(p_gate)(p_gate.n0 + k, 0, k // p_gate.slots, k % p_gate.slots)
                for s in range(steps_before(k), steps_before(k + 1)):
                    step(s)
            ahead(p_br)

            dve.wait_ge(zs_in, 32)
            V.memset(sv[0:C, 0, 0, :], 0.0)
            V.memset(sv[0:C, 1, 0, :], 0.0).then_inc(sv_zero, 1)

            def ends(m):
                if m >= 2:
                    dve.wait_ge(gh_mm, 2 * (m - 1))
                at = 1 + 3 * NC_ * NM + NC_ * (m % 2)
                V.tensor_tensor(q[:, at:at + NC_, :], q[:, 0:1, :].broadcast_to((P, NC_, C)),
                                pend[:, m, :].unsqueeze(2).broadcast_to((P, NC_, C)), ALU.mult).then_inc(dd_ready, 1)

            def masked_ab(m):
                for h in range(2):
                    dve.wait_ge(ab_mm, 2 * m + h + 1)
                    if m >= 2 and h == 0:
                        dve.wait_ge(gh_mm, 2 * (m - 1))
                    V.tensor_tensor(mb[:, m % 2, 2 * h:2 * h + 2, :],
                                    ps[:, h, :].rearrange("p (c v) -> p c v", c=2),
                                    kc[:, K_M1:K_MG].unsqueeze(1).broadcast_to((P, 2, 4 * C)), ALU.mult).then_inc(ab_ready, 1)

            def masked_gh(m):
                for h in range(2):
                    dve.wait_ge(gh_mm, 2 * m + h + 1)
                    if m >= 2 and h == 0:
                        dve.wait_ge(o_mm, m - 1)
                    V.tensor_tensor(gh[:, m % 2, 4 * h:4 * h + 4, :],
                                    ps[:, 4 + h, :].rearrange("p (c v) -> p c v", c=4),
                                    kc[:, K_MG:K_RESET].unsqueeze(1).broadcast_to((P, 4, 2 * C)), ALU.mult).then_inc(gh_ready, 1)

            def to_oc(m):
                b = m // 2
                dve.wait_ge(o_mm, m + 1)
                src = ps[:, 7, 0:T]
                if m % 2:
                    V.tensor_tensor(oc[:, b, :], oc[:, b, :], src[:, ::-1], ALU.add).then_inc(o_ready, 1)
                else:
                    V.tensor_copy(oc[:, b, :], src).then_inc(o_ready, 1)

            for m in range(2):
                ends(m)
                masked_ab(m)
            masked_gh(0)
            dve.wait_ge(st_out[0], 16 * 7)
            dve.wait_ge(st_out[1], 16 * 7)
            for m in range(NM):
                if m + 2 < NM:
                    ends(m + 2)
                    masked_ab(m + 2)
                to_oc(m)
                dve.wait_ge(o_ready, m + 1)
                if m + 1 < NM:
                    masked_gh(m + 1)
            dve.wait_ge(gn_sum, 1)
            V.tensor_scalar(o16[:, 0, :], ps[0:NH, 0, 0:T], 1.0 / 64, None, ALU.mult).then_inc(gn_mean, 1)
            for b in range(NPAIR):
                dve.wait_ge(gn_bc, b + 1)
                V.tensor_tensor(oc[:, b, :], oc[:, b, :], ps[:, 4 + b % 4, 0:T], ALU.subtract).then_inc(gn_cent, 1)
            dve.wait_ge(gn_var, NPAIR)
            V.tensor_scalar(o16[:, 1, :], ps[0:NH, 1, 0:T], 1.0 / 64, GN_EPS, ALU.mult, ALU.add).then_inc(gn_varv, 1)
            dve.wait_ge(gn_sqrt, 1)
            V.reciprocal(o16[:, 3, :], o16[:, 2, :]).then_inc(gn_rec, 1)
            dve.wait_ge(gn_in, 16 * 3)
            for b in range(NPAIR):
                dve.wait_ge(gn_bc2, b + 1)
                y = oc[:, b, :]
                link(V.scalar_tensor_tensor(out=y, in0=y, scalar=vec[:, R_GNW + b:R_GNW + b + 1],
                                            in1=ps[:, 4 + b % 4, 0:T], op0=ALU.mult, op1=ALU.mult))
                link(V.scalar_tensor_tensor(out=y, in0=y, scalar=vec[:, R_GNB + b:R_GNB + b + 1], in1=bo[:, b, :],
                                            op0=ALU.add, op1=ALU.add))
                V.tensor_tensor(y, y, gg[:, b, :], ALU.mult).then_inc(ya_y, 1)
            for b in range(NPAIR):
                dve.wait_ge(ya_hi, b + 1)
                V.tensor_tensor(ytlo[:, b, :], oc[:, b, :], ythi[:, b, :].bitcast(F32), ALU.subtract).then_inc(ya_lo, 1)

            dve.wait_ge(ya_lo, NPAIR)
            dve.wait_ge(k_in, 16)
            for t in range(NT):
                rope(V, qk[:, t, 0:RW], t, ra, rb, roped, t, dve)
            dve.wait_ge(at_in, 16 * 5)
            for i in range(2):
                link(V.tensor_tensor(lamv[:, 2 * i, :], lamv[:, 2 * i, :], lamv[:, 2 * i + 1, :], ALU.mult))
                last = V.tensor_reduce(lamb[:, i:i + 1], lamv[:, 2 * i, :], AX.X, ALU.add)
            last.then_inc(lam_sum, 1)
            dve.wait_ge(lam_exp, 1)
            link(V.tensor_tensor(lamb[:, 4:5], lamb[:, 3:4], lamb[:, 2:3], ALU.subtract))
            link(V.tensor_scalar(lamb[:, 5:6], lamb[:, 4:5], -LAM_INIT, None, ALU.add))

            def maps(g):
                for v2 in range(2):
                    dve.wait_ge(sc_mm, 2 * g + v2 + 1)
                    if g:
                        dve.wait_ge(ex_p, 4 * (g - 1) + 2 * v2 + 2)
                    for s in range(2):
                        last = V.tensor_reduce(mx[:, 2 * v2:2 * v2 + 2, s],
                                               ps[:, 2 * v2 + s, :].rearrange("p (v t) -> p v t", v=2), AX.X, ALU.max)
                    link(last)
                    pair = mx[:, 2 * v2:2 * v2 + 2, :]
                    V.tensor_scalar(pair, pair, -0.125, None, ALU.mult).then_inc(mx_ready, 1)
                for v2 in range(2):
                    dve.wait_ge(ex_p, 4 * g + 2 * v2 + 2)
                    if g:
                        dve.wait_ge(am_t, 2 * (g - 1) + v2 + 1)
                    pair = su[:, 2 * v2:2 * v2 + 2, :]
                    link(V.reciprocal(pair, pair))
                    link(V.tensor_tensor(pair[:, :, 1], pair[:, :, 1], lamb[:, 5:6].broadcast_to((P, 2)), ALU.mult))
                    for v in (2 * v2, 2 * v2 + 1):
                        last = V.tensor_scalar(am[:, v, :], pex[:, v, 1, :], su[:, v, 1:2], None, ALU.mult)
                    link(last)
                    for v in (2 * v2, 2 * v2 + 1):
                        V.scalar_tensor_tensor(out=am[:, v, :], in0=pex[:, v, 0, :], scalar=su[:, v, 0:1],
                                               in1=am[:, v, :], op0=ALU.mult, op1=ALU.add).then_inc(am_ready, 1)

            maps(0)
            for g in range(4):
                dve.wait_ge(pv_sq, g + 1)
                V.tensor_scalar(os_[:, 4:8], os_[:, 0:4], 1.0 / P, SUBLN_EPS, ALU.mult, ALU.add).then_inc(pv_ms, 1)
                if g + 1 < 4:
                    maps(g + 1)
                dve.wait_ge(pv_rs, g + 1)
                if g:
                    dve.wait_ge(yb_t, g)
                V.tensor_tensor(ov[:, :, :], ps[:, 6, :].rearrange("p (v i) -> p v i", v=4),
                                os_[:, 8:12].unsqueeze(2).broadcast_to((P, 4, P)), ALU.mult).then_inc(yb_ready, 1)
                hs, t = 4 * (g % 2), g // 2
                dve.wait_ge(yb_hi, g + 1)
                V.scalar_tensor_tensor(out=ytlo[:, 8 + hs:12 + hs, t * P:(t + 1) * P],
                                       in0=ps[:, 7, :].rearrange("p (v t) -> p v t", v=4), scalar=vecd[:, D_SUB:D_SUB + 1],
                                       in1=ythi[:, 8 + hs:12 + hs, t * P:(t + 1) * P].bitcast(F32),
                                       op0=ALU.mult, op1=ALU.subtract).then_inc(yb_lo, 1)

            def merge_a(i, u=0):
                dve.wait_ge(slots_used, p_br.end(i, 0))
                dve.wait_ge(gt_in[i % 2], 32 * (i // 2 + 1))
                for t in range(NT):
                    last = V.tensor_tensor(mg[:, t, i * CW:(i + 1) * CW], ps[:, 2 * p_br.pair(0) + t, :],
                                           gbuf[:, i % 2, 0, t, :], ALU.mult)
                last.then_inc(pair_free[p_br.pair(0)], 1)

            def merge_b(i, u=1):
                dve.wait_ge(slots_used, p_br.end(i, 1))
                for t in range(NT):
                    last = V.tensor_tensor(mt[:, t, :], ps[:, 2 * p_br.pair(1) + t, :], gbuf[:, i % 2, 1, t, :], ALU.mult)
                last.then_inc(pair_free[p_br.pair(1)], 1)
                dve.wait_ge(pair_free[p_br.pair(1)], p_br.uses(i, 1) + 1)
                dst = mg[:, :, i * CW:(i + 1) * CW]
                V.tensor_tensor(dst, dst, mt[:, :, :], ALU.add).then_inc(mg_ready, 1)
                dve.wait_ge(mg_ready, i + 1)

            for i in range(4):
                for k in range(8):
                    if i or k >= RING:
                        split_lo(p_br)(p_br.n0 + 8 * i + k, 0, 2 * i + k // 4, k % 4)
                    if k == 3 and i:
                        merge_b(i - 1)
                    if k == 7:
                        merge_a(i)
            merge_b(3)
            ahead(p_out)
            transposed_lo(2, None)

            def out_to_f(i, u):
                dve.wait_ge(slots_used, p_out.end(i, u))
                for t in range(NT):
                    last = V.tensor_copy(F2[1][:, t, bass.ds((2 * i + u) * CW, CW)], ps[:, 2 * p_out.pair(u) + t, :])
                last.then_inc(pair_free[p_out.pair(u)], 1)

            carried = walk(dve, p_out, split_lo(p_out), each_chunk(p_out, out_to_f) + gain_hooks(p_out, 1, F2), (), skip=RING)
            carried[0][1]()
            dve.wait_ge(h_back, 16)
            post_norm(3, 1, F2, 1.0, ffn2[0][0])
            transposed_lo(3, R_F2, ffn2[0][0])
            mean_square(2, 4)
            dve.wait_ge(rstd_ready, 5)
            feed_forward(1, F2, ffn2, 4)
            post_norm(5, 2, F2, 0.5)

        @block.tensor
        def _(pe):
            mm = nc.tensor.matmul

            def product(p, hi, lo, ready=None):
                def slot(n, i, u, j):
                    s = slot_of(p, u, j)
                    first = isinstance(i, int) and i == 0 and u == 0
                    if first and ready is not None:
                        ready(j)
                    if j == 0 and not (isinstance(i, int) and p.uses(i, u) == 0):
                        pe.wait_ge(pair_free[p.pair(u)], p.uses(i, u))
                    pe.wait_ge(lo_ready, n + 1)
                    for k in range(SB):
                        a, b = hi(u, SB * j + k), lo(u, SB * j + k)
                        for t in range(NT):
                            o = ps[:, 2 * p.pair(u) + t, 0:p.width]
                            at, bt = a[:, t * P:(t + 1) * P], b[:, t * P:(t + 1) * P]
                            w_, l_ = whi[:, s, k, 0:p.width], wlo[:, s, k, 0:p.width]
                            mm(o, at, w_, start=(j == 0 and k == 0), stop=False)
                            mm(o, at, l_, start=False, stop=False)
                            last = mm(o, bt, w_, start=False, stop=(j == p.slots - 1 and k == SB - 1))
                    last.then_inc(slots_used, 1)
                return slot

            def from_u(p, e):
                return product(p, lambda u, k: uhi[:, k, :], lambda u, k: ulo[:, k, :],
                               (lambda j: pe.wait_ge(ut_lo, ut_base(e) + SB * (j + 1))) if e is not None else None)

            def transpose_u(e, src, nth):
                for k in range(KB):
                    if nth and k % (CW // P) == 0:
                        pe.wait_ge(h_ready, H_PARTS * (nth - 1) + NT * (k // (CW // P) + 1))
                    if k >= 4:
                        pe.wait_ge(ut_lo, ut_base(e) + k - 3)
                    for t in range(NT):
                        last = nc.tensor.transpose(ps[:, 4 + k % 4, t * P:(t + 1) * P], src[:, t, k * P:(k + 1) * P], ident)
                    last.then_inc(ut_done, 1)

            def feed_forward(w, F, groups, e):
                h, f, hthi, htlo, sg, hm, gain = F

                def group(g, gu, dn, carried):
                    f0, f1 = FF_GROUPS[g]
                    fb = w * FFC + f0

                    def turn_h(i):
                        pe.wait_ge(pair_free[gu.pair(1)], gu.uses(i, 1) + 1)
                        if not (isinstance(i, int) and fb + i == 0):
                            pe.wait_ge(ht_lo, 2 * (fb + i))
                        for b in range(2):
                            for k in range(2):
                                for t in range(NT):
                                    kk = 2 * b + k
                                    last = nc.tensor.transpose(ps[:, 4 + b, (2 * k + t) * P:(2 * k + t + 1) * P],
                                                               hm[:, t, kk * P:(kk + 1) * P], ident)
                            last.then_inc(hm_t, 1)

                    def h_ready_(j):
                        if j == 0:
                            pe.wait_ge(ht_lo, 2 * (fb + f1 - f0 - 1))
                        if j == dn.slots - 2:
                            pe.wait_ge(ht_lo, 2 * (fb + f1 - f0))

                    carried = walk(pe, gu, from_u(gu, e if g == 0 else None), [(3, 1, turn_h)], carried)
                    carried = walk(pe, dn, product(dn, lambda u, k: hthi[:, k, :], lambda u, k: htlo[:, k, :], h_ready_),
                                   [], carried)
                    return carried

                carried = []
                for g, (gu, dn) in enumerate(groups):
                    carried = group(g, gu, dn, carried)
            pe.wait_ge(c_in, 16)
            pe.wait_ge(vr_in, 16 * N_VEC)
            nc.tensor.transpose(ps[:, 4, 0:P], vrows[:, 0, 0:P], ident)
            nc.tensor.transpose(ps[:, 4, P:2 * P], vrows[:, 0, P:2 * P], ident).then_inc(vec_t, 1)
            pe.wait_ge(vec_copied, 1)
            pe.wait_ge(x_in, 16)
            transpose_u(0, F1[0], 0)
            feed_forward(0, F1, ffn1, 0)
            transpose_u(1, F1[0], 1)
            for p in (p_rw, p_rw7):
                walk(pe, p, from_u(p, 1 if p is p_rw else None))
            fill = filler(in_steps(p_dif, from_u(p_dif, None), [], []))
            fill(BEFORE_SHIFT)

            pe.wait_ge(pair_free[p_rw7.pair(0)], p_rw7.uses(0, 0) + 1)
            pe.wait_ge(pair_free[p_rw.pair(1)], p_rw.uses(2, 1) + 1)
            for n, j in enumerate(BLOCKS):
                w = 32 if j == NBLK - 1 else P
                if n >= 4:
                    pe.wait_ge(sh_y, n - 3)
                for t in range(NT):
                    last = nc.tensor.transpose(ps[0:w, 4 + n % 4, t * P:(t + 1) * P], proj[:, t, j * P:j * P + w], ident)
                last.then_inc(sh_t, 1)
                fill(IN_SHIFT[n % 2])
            for b in range(NPAIR):
                pe.wait_ge(kk_sq, b + 1)
                mm(ps[0:NH, 6, 0:T], kc[:, K_SEL + NH * b:K_SEL + NH * (b + 1)], sqb[:, b % 2, :],
                   start=(b == 0), stop=(b == NPAIR - 1)).then_inc(kk_sum, 1)
                fill(IN_KK[b % 2])
            pe.wait_ge(gd_ready, 1)
            pe.wait_ge(par_in, 16 * 5)
            for b in range(NPAIR):
                if b >= 2:
                    pe.wait_ge(g_st, b - 1)
                o = ps[:, 4 + b % 2, 0:T]
                mm(o, gupa[:, b * P:(b + 1) * P], lgd[:, 0, :], start=True, stop=False)
                mm(o, gupb[:, b * P:(b + 1) * P], lgd[0:32, 1, :], start=False, stop=True).then_inc(g_mm, 1)
                fill(IN_G[b % 2])
            pe.wait_ge(kk_rec, 1)
            for b in range(NPAIR):
                if b >= 2:
                    pe.wait_ge(kk_ready, b - 1)
                mm(ps[:, 6 + b % 2, 0:T], selt1[:, b * P:(b + 1) * P], s16[:, 0, :], start=True, stop=True).then_inc(kk_bc, 1)

            def low_rank(m):
                b, d = m // 2, m % 2
                if m >= 2:
                    pe.wait_ge(za_act, m - 1)
                rows = slice(LORA * d, LORA * (d + 1))
                sgn = slice(None, None, -1) if d else slice(None)
                mm(ps[:, 4 + m % 2, 0:T], wup[rows, b * P:(b + 1) * P], lwa[rows, 0, sgn], start=True, stop=True)
                mm(ps[:, 4 + m % 2, T:2 * T], aup[rows, b * P:(b + 1) * P], lwa[rows, 1, sgn],
                   start=True, stop=True).then_inc(za_mm, 1)

            def n_products(m):
                pe.wait_ge(q_ready, m + 1)
                pe.wait_ge(ra_ready, 2 * m + 2)
                if m >= 2:
                    pe.wait_ge(n_st, m - 1)
                    if m % 2 == 0:
                        pe.wait_ge(bon_st, m // 2)
                else:
                    pe.wait_ge(kk_ready, NPAIR)
                for c in range(NC_):
                    for h in range(2):
                        r = slice(C * h, C * (h + 1))
                        last = mm(ps[r, 6 + m % 2, c * C:(c + 1) * C], beta[r, m, c * C:(c + 1) * C],
                                  q[r, 1 + 3 * (NC_ * m + c) + 2, :], start=True, stop=True)
                last.then_inc(n_mm, 1)

            pe.wait_ge(g_st, NPAIR)
            pe.wait_ge(lora_act, 1)
            low_rank(0)
            low_rank(1)
            for m in range(NM):
                fill(IN_CHUNKS[m % 2])
                n_products(m)
                if m % 2:
                    b = m // 2
                    pe.wait_ge(bon_in, b + 1)
                    pe.wait_ge(n_st, m)
                    mm(ps[:, 6, T:2 * T], headsum[:, :], kds[:, :], start=True, stop=True).then_inc(bon_mm, 1)
                if m + 2 < NM:
                    low_rank(m + 2)

            walk(pe, p_gate, from_u(p_gate, None))

            pe.wait_ge(zs_in, 32)
            for b in range(2):
                pe.wait_ge(pair_free[b], (p_gate.q0 + 8 - b + 1) // 2)

            def alpha_beta(m, c):
                if c == 0:
                    pe.wait_ge(dd_ready, m + 1)
                    if m:
                        pe.wait_ge(ab_ready, 2 * m)
                at = 1 + 3 * (NC_ * m + c)
                dd = 1 + 3 * NC_ * NM + NC_ * (m % 2) + c
                for h in range(2):
                    r = slice(C * h, C * (h + 1))
                    o = ps[r, c // 2, (c % 2) * 4 * C:(c % 2 + 1) * 4 * C]
                    mm(o[:, 0:2 * C], beta[r, m, c * C:(c + 1) * C], q[r, at:dd + 1:dd - at, :], start=True, stop=True)
                    last = mm(o[:, 2 * C:4 * C], q[r, at + 2, :], q[r, 0:at + 2:at + 1, :], start=True, stop=True)
                if c % 2:
                    last.then_inc(ab_mm, 1)

            def values_t(m):
                b, d = m // 2, m % 2
                if d:
                    pe.wait_ge(vr_ready, b + 1)
                else:
                    pe.wait_ge(vb_in, 16 * (b + 1))
                if m:
                    pe.wait_ge(vt_ready, m)
                vt = vrev if d else vb
                for c in range(NC_):
                    last = mm(ps[C:P, 2, c * P:(c + 1) * P], vt[:, c * C:(c + 1) * C], ident, start=True, stop=True)
                last.then_inc(vt_mm, 1)

            def w_products(m):
                pe.wait_ge(ab_ready, 2 * m + 2)
                if m:
                    pe.wait_ge(w_ready, m)
                for c in range(NC_):
                    for h in range(2):
                        r = slice(C * h, C * (h + 1))
                        last = mm(ps[r, 3, c * P:(c + 1) * P], zs[r, NC_ * m + c, :], mb[r, m % 2, c, 2 * C:4 * C],
                                  start=True, stop=True)
                last.then_inc(w_mm, 1)

            def gh_products(m):
                pe.wait_ge(w_ready, m + 1)
                if m:
                    pe.wait_ge(gh_ready, 2 * m)
                pe.wait_ge(ik_ready, m + 1)
                for c in range(NC_):
                    at = 1 + 3 * (NC_ * m + c)
                    dd = 1 + 3 * NC_ * NM + NC_ * (m % 2) + c
                    for h in range(2):
                        r = slice(C * h, C * (h + 1))
                        o = ps[:, 4 + h, c * P:(c + 1) * P]
                        mm(o, wt[r, m % 2, c, :], mb[r, m % 2, c, 0:2 * C], start=True, stop=False)
                        last = mm(o, ik[r, c, :], q[r, at:dd + 1:dd - at, :], start=False, stop=True)
                        if c == NC_ - 1:
                            last.then_inc(gh_mm, 1)

            def recur(m, c):
                if c == 0:
                    pe.wait_ge(gh_ready, 2 * m + 2)
                    pe.wait_ge(vt_ready, m + 1)
                    pe.wait_ge(sv_zero, 1)
                    if m:
                        pe.wait_ge(o_ready, m)
                else:
                    pe.wait_ge(s_ready, 3 * m + c)
                if c < NC_ - 1:
                    for h in range(2):
                        last = mm(ps[0:C, 6, h * C:(h + 1) * C], gh[:, m % 2, NC_ * h + c, C:2 * C],
                                  sv[:, m % 2, c, h * C:(h + 1) * C], start=True, stop=True)
                    last.then_inc(s_mm, 1)
                for h in range(2):
                    last = mm(ps[C * h:C * (h + 1), 7, c * C:(c + 1) * C], sv[:, m % 2, c, h * C:(h + 1) * C],
                              gh[:, m % 2, NC_ * h + c, 0:C], start=True, stop=True)
                if c == NC_ - 1:
                    last.then_inc(o_mm, 1)

            for c in range(NC_):
                alpha_beta(0, c)
            w_products(0)
            values_t(0)
            for c in range(NC_):
                alpha_beta(1, c)
            gh_products(0)
            for m in range(NM):
                if m + 1 < NM:
                    w_products(m + 1)
                    values_t(m + 1)
                for c in range(NC_):
                    recur(m, c)
                    if m + 2 < NM:
                        alpha_beta(m + 2, c)
                if m + 1 < NM:
                    gh_products(m + 1)
            pe.wait_ge(ab_ready, 2 * NM)
            pe.wait_ge(o_ready, NM)
            for b in range(NPAIR):
                last = mm(ps[0:NH, 0, 0:T], kc[:, K_SEL + NH * b:K_SEL + NH * (b + 1)], oc[:, b, :],
                          start=(b == 0), stop=(b == NPAIR - 1))
            last.then_inc(gn_sum, 1)
            pe.wait_ge(gn_mean, 1)
            pe.wait_ge(gn_in, 16 * 3)
            for b in range(NPAIR):
                if b >= 4:
                    pe.wait_ge(gn_cent, b - 3)
                mm(ps[:, 4 + b % 4, 0:T], selt2[:, b * P:(b + 1) * P], o16[:, 0, :], start=True, stop=True).then_inc(gn_bc, 1)
            for b in range(NPAIR):
                pe.wait_ge(gn_sq, b + 1)
                mm(ps[0:NH, 1, 0:T], kc[:, K_SEL + NH * b:K_SEL + NH * (b + 1)], osq[:, b % 2, :],
                   start=(b == 0), stop=(b == NPAIR - 1)).then_inc(gn_var, 1)
            pe.wait_ge(gn_rec, 1)
            for b in range(NPAIR):
                if b >= 4:
                    pe.wait_ge(ya_y, b - 3)
                mm(ps[:, 4 + b % 4, 0:T], selt2[:, b * P:(b + 1) * P], o16[:, 3, :], start=True, stop=True).then_inc(gn_bc2, 1)

            pe.wait_ge(ya_y, NPAIR)
            pe.wait_ge(roped, 2 * NT)
            pe.wait_ge(k_roped, 2 * NT)
            for n in range(16):
                if n >= 4:
                    pe.wait_ge(qt_ready, n - 3)
                for t in range(NT):
                    last = nc.tensor.transpose(ps[:, 4 + n % 4, t * P:(t + 1) * P],
                                               qk[:, t, n * P:(n + 1) * P], ident)
                last.then_inc(qt_mm, 1)
            pe.wait_ge(qt_ready, 16)
            pe.wait_ge(at_in, 16 * 5)

            def scores(g):
                t, hs = g // 2, 4 * (g % 2)
                for v2 in range(2):
                    if g:
                        pe.wait_ge(ex_p, 4 * (g - 1) + 2 * v2 + 2)
                    for v in range(2):
                        hd = hs + 2 * v2 + v
                        for s in range(2):
                            r = slice(C * s, C * (s + 1))
                            last = mm(ps[:, 2 * v2 + s, v * T:(v + 1) * T], qt_[r, hd, t * P:(t + 1) * P], kt_[r, hd, :],
                                      start=True, stop=True)
                    last.then_inc(sc_mm, 1)

            def transpose_maps(g):
                for v in range(4):
                    pe.wait_ge(am_ready, 4 * g + v + 1)
                    if g:
                        pe.wait_ge(amt_ready, 2 * g - 1 + v // 2)
                    for k in range(NT):
                        last = nc.tensor.transpose(ps[:, 4 + v // 2, (v % 2) * T + k * P:(v % 2) * T + (k + 1) * P],
                                                   am[:, v, k * P:(k + 1) * P], ident)
                    if v % 2:
                        last.then_inc(am_t, 1)

            scores(0)
            transpose_maps(0)
            scores(1)
            for g in range(4):
                t, hs = g // 2, 4 * (g % 2)
                pe.wait_ge(amt_ready, 2 * g + 2)
                if g:
                    pe.wait_ge(yb_ready, g)
                for v in range(4):
                    for k in range(NT):
                        last = mm(ps[:, 6, v * P:(v + 1) * P], amt[:, v, k * P:(k + 1) * P],
                                  va[:, k, (hs + v) * P:(hs + v + 1) * P], start=(k == 0), stop=(k == NT - 1))
                last.then_inc(pv_mm, 1)
                if g + 1 < 4:
                    transpose_maps(g + 1)
                if g + 2 < 4:
                    scores(g + 2)
                pe.wait_ge(yb_ready, g + 1)
                if g:
                    pe.wait_ge(yb_lo, g)
                for v in range(4):
                    last = nc.tensor.transpose(ps[:, 7, v * P:(v + 1) * P], ov[:, v, :], ident)
                last.then_inc(yb_t, 1)

            pe.wait_ge(ya_lo, NPAIR)
            pe.wait_ge(yb_lo, 4)
            walk(pe, p_br, product(p_br, lambda u, k: ythi[:, 8 * u + k, :], lambda u, k: ytlo[:, 8 * u + k, :]))
            pe.wait_ge(mg_ready, 4)
            transpose_u(2, mg, None)
            walk(pe, p_out, from_u(p_out, 2))
            transpose_u(3, F2[0], 2)
            feed_forward(1, F2, ffn2, 3)

        @block.gpsimd
        def _(pool):
            links = [0]
            G = nc.gpsimd

            def link(ins):
                links[0] += 1
                ins.then_inc(pool_link, 1)
                pool.wait_ge(pool_link, links[0])

            def inverse_norm(e):
                pool.wait_ge(ms_ready, e + 1)
                G.tensor_tensor(sm[:, RS[e]], sm[:, MS[e]], sm[:, HALF][:, 0:2], ALU.pow).then_inc(rstd_ready, 1)

            def gain(F, g):
                pool.dma_start(F[6][:, :], g.partition_broadcast(P)).then_inc(gain_in, 16)

            link(G.memset(sm[:, HALF], -0.5))
            pool.wait_ge(vr_zero, 1)
            for v, r, n in VECTORS:
                dst = vrows[r % P:r % P + n, 0, (r // P) * P:(r // P) * P + v.shape[-1]]
                pool.dma_start(dst, v).then_inc(vr_in, 16)
            inverse_norm(0)
            gain(F1, ffn[0][3][0])
            inverse_norm(1)
            inverse_norm(2)
            pool.wait_ge(h_ready, H_PARTS)
            pool.dma_start(h_dram.rearrange("(t p) d -> p t d", p=P), F1[0][:, :, :]).then_inc(h_saved, 16)

            pool.dma_start(wup[:, :], w_up[0].rearrange("d r c -> (d r) c")).then_inc(par_in, 16)
            pool.dma_start(aup[:, :], a_up[0].rearrange("d r c -> (d r) c")).then_inc(par_in, 16)
            pool.dma_start(gupa[:, :], g_up[0, 0:P, :]).then_inc(par_in, 16)
            pool.dma_start(gupb[:, :], g_up[0, P:GLORA, :]).then_inc(par_in, 16)
            pool.dma_start(selt1[:, :], sel_t).then_inc(par_in, 16)

            def store_chunk(c):
                b = p_dif.pair(c % 2)
                pool.wait_ge(pair_free[b], p_dif.uses(c // 2, c % 2) + 1)
                pool.dma_start(dif_dram[:, c * CW:(c + 1) * CW].rearrange("(t p) n -> p t n", p=P),
                               dst_a[:, b, :, :]).then_inc(st_out[b], 16)

            def stores():
                for n in range(p_dif.chunks * p_dif.slots):
                    if n and n % p_dif.slots == 0:
                        store_chunk(n // p_dif.slots - 1)
                    yield

            fill = filler(stores())
            fill(BEFORE_SHIFT + (NBLK - NPAIR) // 2 * sum(IN_SHIFT))
            for b in range(NPAIR):
                pool.wait_ge(shifted, NBLK - NPAIR + b + 1)
                pool.dma_start(v_dram[b], vst[:, b % 2, :]).then_inc((v_out0, v_out1)[b % 2], 16)
                fill(IN_SHIFT[b % 2])
            fill(sum(IN_KK) * NPAIR // 2)
            for b in range(NPAIR):
                pool.wait_ge(g_st, b + 1)
                pool.dma_start(g_dram[b], gst[:, b % 2, :]).then_inc(g_out[b % 2], 16)
                fill(IN_G[b % 2])
            pool.wait_ge(v_out0, 16 * 4)
            pool.wait_ge(v_out1, 16 * 4)
            pool.wait_ge(g_out[0], 16 * 4)
            pool.wait_ge(g_out[1], 16 * 4)
            pool.wait_ge(kk_ready, NPAIR)
            for m in range(NM):
                b, d = m // 2, m % 2
                if d == 0:
                    if b:
                        pool.wait_ge(bon_st, b)
                    pool.dma_start(vb1[:, :], v_dram[b]).then_inc(v1_in, 16)
                sgn = slice(None, None, -1) if d else slice(None)
                s0 = 1 + 3 * NC_ * m
                qv = q[:, s0:s0 + 3 * NC_, :].rearrange("p (c w) t -> p c w t", w=3)
                ch = lambda a: a.rearrange("p (c t) -> p c t", c=NC_)
                pool.wait_ge(ex_out, m + 1)
                G.tensor_tensor(qv[:, :, 0, :], ch(rr[:, b, sgn]), ch(eie[:, 0, :]), ALU.mult).then_inc(ra_ready, 1)
                G.tensor_tensor(qv[:, :, 2, :], ch(kkn[:, b, sgn]), ch(eie[:, 1, :]), ALU.mult).then_inc(ra_ready, 1)
                if d == 0 and b:
                    pool.wait_ge(bon_st, b)
                    pool.dma_start(bonus_dram[b - 1], bst[:, :]).then_inc(bon_out, 16)
                fill(IN_CHUNKS[d])
            store_chunk(p_dif.chunks - 1)
            pool.wait_ge(bon_st, NPAIR)
            pool.dma_start(bonus_dram[NPAIR - 1], bst[:, :]).then_inc(bon_out, 16)
            pool.wait_ge(n_out[0], 32 * (NM // 2))
            pool.wait_ge(n_out[1], 32 * (NM // 2))
            pool.wait_ge(bon_out, 16 * NPAIR)
            pool.dma_start(z[:, :, :].rearrange("p c t -> p (c t)"),
                           n_dram.rearrange("h m c s t -> (h m c) (s t)")).then_inc(z_in, 16)
            def store_gates(chunks):
                for c in chunks:
                    b = p_gate.pair(c % 2)
                    pool.wait_ge(pair_free[b], p_gate.uses(c // 2, c % 2) + 1)
                    pool.dma_start(gate_dram[:, c * CW:(c + 1) * CW].rearrange("(t p) n -> p t n", p=P),
                                   gst_g[:, b, :, :]).then_inc(st_out[b], 16)

            store_gates(range(6))
            pool.wait_ge(z_done, 1)
            pool.dma_start(z_dram.rearrange("h m c s t -> (h m c) (s t)"),
                           z[:, :, :].rearrange("p c t -> p (c t)")).then_inc(z_out, 16)
            pool.wait_ge(z_out, 16)
            for h in range(2):
                pool.dma_start(zs[C * h:C * (h + 1), :, :],
                               z_dram[h].rearrange("m c s t -> s (m c) t")).then_inc(zs_in, 16)
            store_gates(range(6, 8))

            pool.wait_ge(zs_in, 32)

            def kappas(m):
                if m:
                    pool.wait_ge(gh_mm, 2 * m)
                at = 1 + 3 * NC_ * m
                G.tensor_copy(ik[:, :, C:2 * C], q[:, at:at + 3 * NC_, :].rearrange("p (c w) t -> p c w t", w=3)[:, :, 1, :]).then_inc(ik_ready, 1)

            link(G.tensor_copy(ik[:, :, 0:C], q[:, 0:1, :].broadcast_to((P, NC_, C))))
            kappas(0)
            for b in range(NPAIR):
                if b:
                    pool.wait_ge(vt_mm, 2 * b - 1)
                    pool.wait_ge(vr_ready, b)
                pool.dma_start(vb[:, :], v_dram[b]).then_inc(vb_in, 16)
                pool.wait_ge(vb_in, 16 * (b + 1))
                if b:
                    pool.wait_ge(vt_mm, 2 * b)
                G.tensor_copy(vrev[:, :], vb[:, ::-1]).then_inc(vr_ready, 1)
                if b:
                    kappas(2 * b - 1)
                    kappas(2 * b)
            kappas(NM - 1)
            pool.wait_ge(gh_mm, 2 * NM)
            pool.dma_start(selt2[:, :], sel_t).then_inc(gn_in, 16)
            pool.dma_start(bo[:, :, :], bonus_dram.rearrange("b p t -> p b t")).then_inc(gn_in, 16)
            pool.dma_start(gg[:, :, :], g_dram.rearrange("b p t -> p b t")).then_inc(gn_in, 16)
            dif = dif_dram.rearrange("(t p) c -> p t c", p=P)
            pool.dma_start(qk[:, :, :], dif[:, :, 0:2 * RW]).then_inc(k_in, 16)
            pool.dma_start(va[:, :, :], dif[:, :, 2 * RW:3 * RW]).then_inc(at_in, 16)
            pool.wait_ge(k_in, 16)
            for t in range(NT):
                rope(G, qk[:, t, RW:2 * RW], t, pa, pb, k_roped, t, pool)
            pool.wait_ge(ya_lo, NPAIR)
            for i, n in enumerate(("lambda_q1", "lambda_k1", "lambda_q2", "lambda_k2")):
                pool.dma_start(lamv[:, i, :], a[n][0].partition_broadcast(P)).then_inc(at_in, 16)
            for g in range(4):
                pool.wait_ge(pv_ms, g + 1)
                if g:
                    pool.wait_ge(yb_ready, g)
                G.tensor_tensor(os_[:, 8:12], os_[:, 4:8], sm[:, HALF][:, 0:4], ALU.pow).then_inc(pv_rs, 1)
            pool.wait_ge(yb_lo, 4)
            gates = gate_dram.rearrange("(t p) (w n) -> p w t n", p=P, w=2)
            for i in range(4):
                if i >= 2:
                    pool.wait_ge(mg_ready, i - 1)
                for w in range(2):
                    pool.dma_start(gbuf[:, i % 2, w, :, :], gates[:, w, :, i * CW:(i + 1) * CW]).then_inc(gt_in[i % 2], 16)
            pool.wait_ge(mg_ready, 4)
            pool.wait_ge(slots_used, p_br.end(3, 1))
            pool.dma_start(F2[0][:, :, :], h_dram.rearrange("(t p) d -> p t d", p=P)).then_inc(h_back, 16)
            gain(F2, mix_post_g[0])
            inverse_norm(3)
            inverse_norm(4)
            pool.wait_ge(h_ready, 2 * H_PARTS)
            gain(F2, ffn[1][3][0])
            inverse_norm(5)
            for c in range(D // CW):
                cols = slice(c * CW, (c + 1) * CW)
                pool.wait_ge(h_ready, 2 * H_PARTS + NT * (c + 1))
                pool.dma_start(out[0].rearrange("(t p) d -> p t d", p=P)[:, :, cols], F2[0][:, :, cols]).then_inc(out_done, 16)
            pool.wait_ge(out_done, 16 * (D // CW))
            pool.wait_ge(h_saved, 16)


_NAMES = ['x', 'ffn1_pre_g', 'ffn1_w_gu', 'ffn1_w_down', 'ffn1_post_g', 'mix_pre_g', 'w_in', 'mu_prev', 'mu_next',
          'w0', 'w_up', 'a0', 'a_up', 'g_up', 'k_k', 'k_a', 'r_k', 'gn_w', 'gn_b', 'lambda_q1', 'lambda_k1',
          'lambda_q2', 'lambda_k2', 'subln_g', 'w_branch_a', 'w_branch_b', 'w_out', 'mix_post_g', 'ffn2_pre_g',
          'ffn2_w_gu', 'ffn2_w_down', 'ffn2_post_g']


def kernel(**inputs):
    import concourse.bacc as bacc
    from concourse.bass_utils import run_bass_kernel_spmd

    nc = bacc.Bacc("TRN2", target_bir_lowering=False, num_devices=1)
    arrays, a = {}, {}
    consts, sel_t = constants()
    for name, array in [(n, np.ascontiguousarray(inputs[n])) for n in _NAMES] + [("consts", consts), ("sel_t", sel_t)]:
        arrays["in_" + name] = array
        a[name] = nc.dram_tensor("in_" + name, array.shape, F32, kind="ExternalInput").ap()
    out = nc.dram_tensor("out_0", (1, T, D), F32, kind="ExternalOutput").ap()
    layer(nc, a, out)
    r = run_bass_kernel_spmd(nc, [arrays], core_ids=[0])
    return r.results[0]["out_0"]
```

```python
import math
from contextlib import ExitStack

import numpy as np

import concourse.bass as bass
from concourse import mybir

F32 = mybir.dt.float32
F32R = mybir.dt.float32r
ALU = mybir.AluOpType
ACT = mybir.ActivationFunctionType
AX = mybir.AxisListType

P = 128
D = 2048
T = 256
NT = T // P
KB = D // P
FF = ((8 * D // 3 + 255) // 256) * 256
CW = 512
RING = 4
SB = 2
FFC = FF // CW
FF_GROUPS = ((0, 6), (6, FFC))
NPAIR = 8
NH = 16
RW = 1024
LORA = 64
GLORA = 160
RCOLS = 3 * RW + 4 * LORA + GLORA
DCOLS = 3 * 1024
NBLK = -(-RCOLS // P)
C = 64
NC_ = T // C
NM = 2 * NPAIR
EPS = 1e-6
GN_EPS = 64e-5
SUBLN_EPS = 1e-5
LAM_INIT = 0.8 - 0.6 * math.exp(-0.3 * 0)
DECAY = math.exp(-0.5)
QSLOTS = 1 + NM * 3 * NC_ + 2 * NC_
BEFORE_SHIFT, IN_SHIFT, IN_KK, IN_G, IN_CHUNKS = 2, (0, 1), (0, 1), (0, 1), (2, 1)
IN_ROPE, IN_HEADS = 4, (2, 2, 0)
assert BEFORE_SHIFT + NBLK // 2 * sum(IN_SHIFT) + NPAIR // 2 * (sum(IN_KK) + sum(IN_G)) + NPAIR * sum(IN_CHUNKS) == 48
K_ID, K_SEL, K_HEAD, K_MN, K_M1, K_MG, K_RESET, K_COS, K_SIN, K_END = np.cumsum(
    [0, P, P, P, C, 4 * C, P, T, 2 * 32, 2 * 32]).tolist()
BLOCKS = list(range(24, NBLK)) + list(range(24))
D_MU, D_W0, D_A0, D_KA, D_KA1, D_SUB = 0, 28, 44, 60, 68, 76
R_F1, R_MIX, R_F2, R_MUP, R_MUN, R_W0 = 0, 16, 32, 48, 76, 104
R_A0, R_KK, R_KA, R_RK, R_GNW, R_GNB, R_SUB = 128, 144, 152, 160, 168, 176, 184


def constants():
    k = np.zeros((P, K_END), np.float32)
    p = np.arange(P)[:, None]
    t = np.arange(C)[None, :]
    k[:, K_ID:K_SEL] = np.eye(P)
    bh = np.arange(P)[None, :]
    k[:, K_SEL:K_HEAD] = (bh % NH == 2 * (bh // NH) + p // C)
    k[:, K_HEAD:K_MN] = (p // C == bh // C)
    s = p % C
    k[:, K_MN:K_M1] = -1.0 * (s < t)
    k[:, K_M1:K_MG] = np.concatenate([s <= t, s >= -1 + 0 * t, s >= -1 + 0 * t, t < s], 1)
    k[:, K_MG:K_RESET] = np.concatenate([(p < C) | (s <= t), s >= -1 + 0 * t], 1)
    k[:, K_RESET:K_COS] = (np.arange(T) % C != 0)[None, :]
    inv = np.float32(10000.0) ** (-np.arange(32, dtype=np.float32) / np.float32(32))
    ang = np.arange(T, dtype=np.float32)[:, None] * inv.astype(np.float32)[None, :]
    for i in range(NT):
        k[:, K_COS + 32 * i:K_COS + 32 * (i + 1)] = np.cos(ang[i * P:(i + 1) * P])
        k[:, K_SIN + 32 * i:K_SIN + 32 * (i + 1)] = np.sin(ang[i * P:(i + 1) * P])
    sel_t = (np.arange(NH)[:, None] == (2 * np.arange(NPAIR)[:, None] + np.arange(P)[None, :] // C).reshape(1, -1))
    return k, sel_t.astype(np.float32)


def layer(nc, a, out):
    x, w_in, mix_post_g, w_up, a_up, g_up, w_branch_a, w_branch_b, w_out, consts, sel_t = (
        a[n] for n in ("x", "w_in", "mix_post_g", "w_up", "a_up", "g_up", "w_branch_a", "w_branch_b", "w_out",
                       "consts", "sel_t"))
    ffn = [(a[f"ffn{i}_pre_g"], a[f"ffn{i}_w_gu"], a[f"ffn{i}_w_down"], a[f"ffn{i}_post_g"]) for i in (1, 2)]

    def rows(v):
        return v.rearrange("(b p) -> b p", p=P)

    def by_direction(v):
        return v.rearrange("d (b p) -> (d b) p", p=P)

    whole = (NBLK - 1) * P
    VECTORS = [(rows(ffn[0][0][0]), R_F1, 16), (rows(a["mix_pre_g"][0]), R_MIX, 16), (rows(ffn[1][0][0]), R_F2, 16),
               (rows(a["mu_prev"][0, 0:whole]), R_MUP, NBLK - 1), (a["mu_prev"][0:1, whole:RCOLS], R_MUP + NBLK - 1, 1),
               (rows(a["mu_next"][0, 0:whole]), R_MUN, NBLK - 1), (a["mu_next"][0:1, whole:RCOLS], R_MUN + NBLK - 1, 1),
               (by_direction(a["w0"][0]), R_W0, 16), (by_direction(a["a0"][0]), R_A0, 16), (rows(a["k_k"][0]), R_KK, 8),
               (rows(a["k_a"][0]), R_KA, 8), (a["r_k"][0].rearrange("(b h) p -> b (h p)", h=2), R_RK, 8),
               (rows(a["gn_w"][0]), R_GNW, 8), (rows(a["gn_b"][0]), R_GNB, 8), (a["subln_g"], R_SUB, 1)]
    N_VEC = len(VECTORS)

    class Pass:

        def __init__(self, chunks, slots, unroll, width, source, pairs=2):
            self.n0, self.q0, self.stride = Pass.n, Pass.q, 2 // pairs
            self.chunks, self.slots, self.unroll, self.width, self.source = chunks, slots, unroll, width, source
            self.turns = chunks // unroll
            assert chunks % unroll == 0
            Pass.n += chunks * slots
            Pass.q += chunks * self.stride
            assert self.turns == 1 or (unroll * slots % RING == 0 and unroll % 2 == 0)

        def end(self, i, u):
            return self.n0 + (i * self.unroll + u + 1) * self.slots

        def uses(self, i, u):
            return (self.q0 + self.stride * (i * self.unroll + u)) // 2 if isinstance(i, int) else \
                i * (self.unroll // 2) + (self.q0 + u) // 2

        def pair(self, u):
            return (self.q0 + self.stride * u) % 2

    Pass.n = Pass.q = 0

    def rows_cols(w, r0, j, c0, width):
        return w[r0 + j * SB * P:r0 + (j + 1) * SB * P, bass.ds(c0, width)].rearrange("(k p) n -> p k n", p=P)

    def gate_up(wgu, f0):
        return lambda i, u, j: rows_cols(wgu, 0, j, u * FF + (f0 + i) * CW, CW)

    def down(wd, f0):
        return lambda i, u, j: rows_cols(wd, f0 * CW, j, (2 * i + u) * CW, CW)

    def make_ffn(w):
        ps = []
        for f0, f1 in FF_GROUPS:
            ps.append((Pass(2 * (f1 - f0), KB // SB, 2, CW, gate_up(w[1][0], f0)),
                       Pass(D // CW, (f1 - f0) * CW // (SB * P), 2, CW, down(w[2][0], f0))))
        return ps

    wi = w_in[0]
    ffn1 = make_ffn(ffn[0])
    p_rw = Pass(6, 8, 2, CW, lambda i, u, j: rows_cols(wi, 0, j, (2 * i + u) * CW, CW))
    p_rw7 = Pass(1, 8, 1, RCOLS - 6 * CW, lambda i, u, j: rows_cols(wi, 0, j, 6 * CW, RCOLS - 6 * CW))
    p_dif = Pass(6, 8, 2, CW, lambda i, u, j: rows_cols(wi, 0, j, RCOLS + (2 * i + u) * CW, CW))
    p_gate = Pass(8, 8, 2, CW, lambda i, u, j: rows_cols(wi, 0, j, RCOLS + DCOLS + (2 * i + u) * CW, CW))
    p_ya, p_yb = (Pass(4, 4, 2, CW, lambda i, u, j, w=w: rows_cols(w[0], 0, j, (2 * i + u) * CW, CW), pairs)
                  for w, pairs in ((w_branch_a, 1), (w_branch_b, 2)))
    p_out = Pass(4, 8, 2, CW, lambda i, u, j: rows_cols(w_out[0], 0, j, (2 * i + u) * CW, CW))
    ffn2 = make_ffn(ffn[1])
    passes = [p for g in ffn1 for p in g] + [p_rw, p_rw7, p_dif, p_gate, p_ya, p_yb, p_out] + [p for g in ffn2 for p in g]

    def scratch(name, shape):
        return nc.dram_tensor(name, shape, F32).ap()

    h_dram = scratch("h_dram", (T, D))
    dif_dram = scratch("dif_dram", (T, DCOLS))
    gate_dram = scratch("gate_dram", (T, 2 * D))
    v_dram = scratch("v_dram", (NPAIR, P, T))
    g_dram = scratch("g_dram", (NPAIR, P, T))
    bonus_dram = scratch("bonus_dram", (NPAIR, P, T))
    n_dram = scratch("n_dram", (2, NM, NC_, C, C))
    z_dram = scratch("z_dram", (2, NM, NC_, C, C))

    ctx = ExitStack()
    with ctx:
        def sem(name):
            return ctx.enter_context(nc.semaphore(name))

        def sb(scope, name, shape, dt=F32):
            return scope.enter_context(nc.sbuf_tensor(name, shape, dt))

        ps = ctx.enter_context(nc.psum_tensor("ps", [P, 8, 512], F32))

        kc = sb(ctx, "kc", [P, K_END])
        vec = sb(ctx, "vec", [P, 256])
        sm = sb(ctx, "sm", [P, 64])
        vecd = sb(ctx, "vecd", [P, 80])
        raw = sb(ctx, "raw", [P, RING, SB, CW])
        whi = sb(ctx, "whi", [P, RING, SB, CW], F32R)
        wlo = sb(ctx, "wlo", [P, RING, SB, CW], F32R)
        uhi = sb(ctx, "uhi", [P, KB, T], F32R)
        ulo = sb(ctx, "ulo", [P, KB, T], F32R)
        ident = kc[:, K_ID:K_SEL]
        headsum = kc[:, K_HEAD:K_MN]

        def room(*names):
            scope = ExitStack()
            tiles = [sb(scope, *n) for n in names]
            return scope, tiles

        def ffn_room(tag):
            return room(("h" + tag, [P, NT, D]), ("f" + tag, [P, NT, D]),
                        ("hthi" + tag, [P, 24, T], F32R), ("htlo" + tag, [P, 24, T], F32R),
                        ("sg" + tag, [P, NT, CW]), ("hm" + tag, [P, NT, CW]), ("gain" + tag, [P, D]))

        s1, F1 = ffn_room("1")
        vrows = F1[1]
        s1.close()
        s_proj, (proj, ybuf, vst, lgd, gupa, gupb, sqb, s16, gst, selt1) = room(
            ("proj", [P, NT, NBLK * P]), ("ybuf", [P, 2, T + 2]), ("vst", [P, 2, T]),
            ("lgd", [P, 2, T]), ("gupa", [P, RW]), ("gupb", [GLORA - P, RW]), ("sqb", [P, 2, T]),
            ("s16", [NH, 2, T]), ("gst", [P, 2, T]), ("selt1", [NH, NPAIR * P]))
        s_proj.close()
        s_q, (q, beta, pend) = room(("q", [P, QSLOTS, C]), ("beta", [P, NM, T]), ("pend", [P, NM, NC_]))
        s_rk, (rr, kr, kkn, wup, aup, lwa) = room(
            ("rr", [P, NPAIR, T]), ("kr", [P, NPAIR, T]), ("kkn", [P, NPAIR, T]),
            ("wup", [P, RW]), ("aup", [P, RW]), ("lwa", [P, 2, T]))
        bst, vb1 = (q[:, QSLOTS - 8 + 4 * i:QSLOTS - 4 + 4 * i, :].rearrange("p c t -> p (c t)") for i in range(2))
        s_e, (dst_a, tz, ie, eie, ld, aa, kd, kds, nst) = room(
            ("dst_a", [P, 2, NT, CW]), ("tz", [P, 2, T]), ("ie", [P, 2, T]), ("eie", [P, 3, T]), ("ld", [P, T]), ("aa", [P, T]), ("kd", [P, T]),
            ("kds", [P, T]), ("nst", [P, 2, NC_, C]))
        s_e.close()
        s_rk.close()
        s_z, (z, zt, _, gst_g) = room(("z", [P, C, C]), ("zt", [P, 32 * 32]), ("z_gap", [P, 24 * 256]),
                                      ("gst_g", [P, 2, NT, CW]))
        s_z.close()
        s_r, (zs, vb, vrev, mb, wt, gh, sv, ik, oc) = room(
            ("zs", [P, NM * NC_, C]), ("vb", [P, T]), ("vrev", [P, T]), ("mb", [P, 2, NC_, 4 * C]),
            ("wt", [P, 2, NC_, 2 * C]), ("gh", [P, 2, 2 * NC_, 2 * C]), ("sv", [P, 2, NC_, 2 * C]), ("ik", [P, NC_, 2 * C]), ("oc", [P, NPAIR, T]))
        s_r.close()
        s_q.close()
        s_y, (ythi, ytlo) = room(("ythi", [P, 16, T], F32R), ("ytlo", [P, 16, T], F32R))
        s_qkv, (qk, va, mg) = room(("qk", [P, NT, 2 * RW]), ("va", [P, NT, RW]), ("mg", [P, D // CW, NT, CW]))
        ra, rb, pa, pb = (mg[:, i, :, :].rearrange("p t c -> p (t c)") for i in range(4))
        s_n, (selt2, bo, gg, osq, o16) = room(
            ("selt2", [NH, NPAIR * P]), ("bo", [P, NPAIR, T]), ("gg", [P, NPAIR, T]), ("osq", [P, 2, T]), ("o16", [NH, 4, T]))
        s_n.close()
        s_t, (qt_, kt_, lamv, lamb, mx, su, pex, am, amt, ov, oj, os_, gbuf, mt) = room(
            ("qt_", [P, 8, T]),
            ("kt_", [P, 8, T]), ("lamv", [P, 4, 64]), ("lamb", [P, 8]), ("mx", [P, 4, 2]), ("su", [P, 4, 2]),
            ("pex", [P, 4, 2, T]), ("am", [P, 4, T]), ("amt", [P, 4, T]), ("ov", [P, 4, P]), ("oj", [P, 4, P]),
            ("os_", [P, 16]), ("gbuf", [P, 2, NT, CW]), ("mt", [P, NT, CW]))
        s_t.close()
        s_qkv.close()
        s_y.close()
        s2, F2 = ffn_room("2")
        s2.close()

        landed = [sem(f"landed{s}") for s in range(RING)]
        hi_ready = sem("hi_ready")
        lo_ready = sem("lo_ready")
        slots_used = sem("slots_used")
        pair_free = [sem("pair_free0"), sem("pair_free1")]
        act_link, dve_link, pool_link = sem("act_link"), sem("dve_link"), sem("pool_link")
        c_in, x_in, vr_in, vr_in_a, par_in = (sem(n) for n in ("c_in", "x_in", "vr_in", "vr_in_a", "par_in"))
        vr_zero, vec_t, vec_copied, vec_ready = (sem(n) for n in ("vr_zero", "vec_t", "vec_copied", "vec_ready"))
        ss_ready, ms_ready, rstd_ready = (sem(n) for n in ("ss_ready", "ms_ready", "rstd_ready"))
        fs_ready, fg_ready = sem("fs_ready"), sem("fg_ready")
        ut_done, ut_hi, ut_lo = sem("ut_done"), sem("ut_hi"), sem("ut_lo")
        hm_t, ht_hi, ht_lo = sem("hm_t"), sem("ht_hi"), sem("ht_lo")
        gain_in, h_ready, h_saved, h_back, out_done = (sem(n) for n in ("gain_in", "h_ready", "h_saved", "h_back", "out_done"))
        st_out = [sem("st_out0"), sem("st_out1")]
        sh_t, sh_y, shifted, v_out0, v_out1 = (sem(n) for n in ("sh_t", "sh_y", "shifted", "v_out0", "v_out1"))
        lora_act, gd_ready = sem("lora_act"), sem("gd_ready")
        kk_raw, kk_sq, kk_sum, kk_max, kk_sqrt, kk_rec, kk_bc, kk_ready = (
            sem(n) for n in ("kk_raw", "kk_sq", "kk_sum", "kk_max", "kk_sqrt", "kk_rec", "kk_bc", "kk_ready"))
        g_mm, g_st = sem("g_mm"), sem("g_st")
        g_out = [sem("g_out0"), sem("g_out1")]
        za_mm, za_act, ex_in, ex_out, aa_ready, ra_ready, q_ready = (
            sem(n) for n in ("za_mm", "za_act", "ex_in", "ex_out", "aa_ready", "ra_ready", "q_ready"))
        bon_in, bon_mm, bon_st, bon_out, v1_in = (sem(n) for n in ("bon_in", "bon_mm", "bon_st", "bon_out", "v1_in"))
        n_mm, n_st, z_in, z_done, z_out, zs_in = (sem(n) for n in ("n_mm", "n_st", "z_in", "z_done", "z_out", "zs_in"))
        n_out = [sem("n_out0"), sem("n_out1")]
        vb_in = sem("vb_in")
        sv_zero, dd_ready, vt_mm, vt_ready, ab_mm, ab_ready, w_mm, w_ready, gh_mm, gh_ready = (
            sem(n) for n in ("sv_zero", "dd_ready", "vt_mm", "vt_ready", "ab_mm", "ab_ready", "w_mm", "w_ready",
                             "gh_mm", "gh_ready"))
        s_mm, s_ready, o_mm, o_ready = sem("s_mm"), sem("s_ready"), sem("o_mm"), sem("o_ready")
        gn_sum, gn_mean, gn_bc, gn_cent, gn_sq, gn_var, gn_varv, gn_sqrt, gn_rec, gn_bc2, gn_in, ya_y, ya_hi, ya_lo = (
            sem(n) for n in ("gn_sum", "gn_mean", "gn_bc", "gn_cent", "gn_sq", "gn_var", "gn_varv", "gn_sqrt",
                             "gn_rec", "gn_bc2", "gn_in", "ya_y", "ya_hi", "ya_lo"))
        at_in, lam_sum, lam_exp, roped, qt_mm, qt_ready = (
            sem(n) for n in ("at_in", "lam_sum", "lam_exp", "roped", "qt_mm", "qt_ready"))
        sc_mm, mx_ready, ex_p, am_ready, am_t, amt_ready, pv_mm, pv_sq, pv_ms, pv_rs, yb_ready, yb_t, yb_hi, yb_lo = (
            sem(n) for n in ("sc_mm", "mx_ready", "ex_p", "am_ready", "am_t", "amt_ready", "pv_mm", "pv_sq", "pv_ms",
                             "pv_rs", "yb_ready", "yb_t", "yb_hi", "yb_lo"))
        vr_ready, ik_ready = sem("vr_ready"), sem("ik_ready")
        k_in, k_roped = sem("k_in"), sem("k_roped")
        gt_in = [sem("gt_in0"), sem("gt_in1")]
        mg_ready = sem("mg_ready")

        SS = {e: slice(6 * e, 6 * e + 2) for e in range(6)}
        MS = {e: slice(6 * e + 2, 6 * e + 4) for e in range(6)}
        RS = {e: slice(6 * e + 4, 6 * e + 6) for e in range(6)}
        HALF = slice(40, 48)
        QS = slice(48, 56)

        def slot_of(p, u, j):
            return (p.n0 + u * p.slots + j) % RING

        def walk(eng, p, slot, hooks=(), carried=(), skip=0):
            def turn(i, first):
                for k in range(p.unroll * p.slots):
                    if not (first and k < skip):
                        slot(p.n0 + i * (p.unroll * p.slots) + k, i, k // p.slots, k % p.slots)
                    for at, fn in carried if first else ():
                        if at == k:
                            fn()
                    for at, lag, fn in hooks:
                        if at == k and not (first and lag):
                            fn(i - lag)
            turn(0, True)
            if p.turns > 1:
                with eng.Fori(1, p.turns) as i:
                    turn(i, False)
            return [(at, (lambda fn=fn: fn(p.turns - 1))) for at, lag, fn in hooks if lag]

        def in_steps(p, slot, hooks, then, skip=0):
            for n in range(p.chunks * p.slots):
                i, k = divmod(n, p.unroll * p.slots)
                if n >= skip:
                    slot(p.n0 + n, i, k // p.slots, k % p.slots)
                for at, lag, fn in hooks:
                    if at == k and i >= lag:
                        fn(i - lag)
                yield
            for fn in then:
                fn()
                yield

        def filler(steps):
            def fill(k):
                for _ in range(k):
                    next(steps, None)
            return fill

        LEAD = RING - 1

        def each_chunk(p, fn):
            if p.unroll == 1:
                return [(3, 1, lambda i: fn(i, 0))]
            return [(3, 1, lambda i: fn(i, 1)), (p.slots + 3, 0, lambda i: fn(i, 0))]

        def ut_base(e):
            return KB * e

        def shift_tile(j):
            kind, b = j // 8, j % 8
            tile, at = ((rr, b), (kr, b), (vst, b % 2), (lwa, b) if b < 2 else (lgd, b - 2))[kind]
            return tile[:, at, :]

        def rstd(e, t):
            return sm[:, 6 * e + 4 + t:6 * e + 5 + t]

        H_PARTS = NT * (D // CW)

        block = ctx.enter_context(nc.Block())

        @block.sync
        def _(sp):
            for p in passes:
                def load(n, i, u, j, p=p):
                    s = slot_of(p, u, j)
                    if not (isinstance(n, int) and n < RING):
                        sp.wait_ge(lo_ready, n - RING + 1)
                    sp.dma_start(raw[:, s, :, 0:p.width], p.source(i, u, j)).then_inc(landed[s], 16)
                walk(sp, p, load)

        def rope(engine, x_, t, a_, b_, done, before, queue):
            cos = kc[:, K_COS + 32 * t:K_COS + 32 * t + 32].unsqueeze(1).unsqueeze(1).broadcast_to((P, 16, 2, 32))
            sin = kc[:, K_SIN + 32 * t:K_SIN + 32 * t + 32].unsqueeze(1).unsqueeze(1).broadcast_to((P, 16, 2, 32))
            xv, av, bv = (w[:, :].rearrange("p (h s f) -> p h s f", h=16, s=2) for w in (x_, a_, b_))
            engine.tensor_tensor(av, xv, cos, ALU.mult)
            engine.tensor_tensor(bv, xv[:, :, ::-1, :], sin, ALU.mult).then_inc(done, 1)
            queue.wait_ge(done, 2 * before + 1)
            engine.tensor_tensor(xv[:, :, 0, :], av[:, :, 0, :], bv[:, :, 0, :], ALU.subtract)
            engine.tensor_tensor(xv[:, :, 1, :], av[:, :, 1, :], bv[:, :, 1, :], ALU.add).then_inc(done, 1)
            queue.wait_ge(done, 2 * before + 2)

        @block.scalar
        def _(act):
            links = [0]

            def link(ins):
                links[0] += 1
                ins.then_inc(act_link, 1)
                act.wait_ge(act_link, links[0])

            def split_hi(p):
                def slot(n, i, u, j):
                    s = slot_of(p, u, j)
                    k = p.n0 + u * p.slots + j
                    act.wait_ge(landed[s], i * (16 * p.unroll * p.slots // RING) + 16 * (k // RING + 1))
                    if not (isinstance(n, int) and n < RING):
                        act.wait_ge(slots_used, n - RING + 1)
                    nc.scalar.activation(whi[:, s, :, 0:p.width], raw[:, s, :, 0:p.width], ACT.Copy).then_inc(hi_ready, 1)
                return slot

            def ahead(p, slots=range(RING)):
                for k in slots:
                    split_hi(p)(p.n0 + k, 0, 0, k)

            def pre_norm(nth, e, F):
                junk = F[2][:, 0:8, :].rearrange("p k t -> p (k t)")

                def squares(t):
                    if t:
                        act.wait_ge(ss_ready, NT * nth + t)
                    nc.scalar.activation(junk, F[0][:, t, :], ACT.Square,
                                         accum_out=sm[:, 6 * e + t:6 * e + t + 1]).then_inc(ss_ready, 1)
                return [(4, lambda: squares(0)), (6, lambda: squares(1)), (10, lambda: act.wait_ge(rstd_ready, e + 1))]

            def transposed_hi(e, col):
                for k in range(KB):
                    act.wait_ge(ut_done, ut_base(e) + k + 1)
                    bank = ps[:, 4 + k % 4, 0:T]
                    if col is None:
                        nc.scalar.activation(uhi[:, k, :], bank, ACT.Copy).then_inc(ut_hi, 1)
                    else:
                        nc.scalar.activation(uhi[:, k, :], bank, ACT.Identity,
                                             scale=vec[:, col + k:col + k + 1]).then_inc(ut_hi, 1)

            def chunk_squares(p, nth, F):
                def fn(i, u):
                    c = 2 * i + u
                    act.wait_ge(pair_free[p.pair(u)], p.uses(i, u) + 1)
                    if not (isinstance(c, int) and 4 * nth + c == 0):
                        act.wait_ge(fs_ready, 4 * nth + c)
                    for t in range(NT):
                        last = nc.scalar.activation(F[4][:, t, :], F[1][:, t, bass.ds(c * CW, CW)], ACT.Square,
                                                    accum_out=sm[:, bass.ds(QS.start + 4 * t + c, 1)])
                    last.then_inc(fs_ready, 1)
                return fn

            def feed_forward(w, F, groups, e, following):
                h, f, hthi, htlo, sg, hm, gain = F

                def group(g, gu, dn, carried):
                    f0, f1 = FF_GROUPS[g]
                    fb = w * FFC + f0

                    def silu(i):
                        if not (isinstance(i, int) and gu.uses(i, 1) == 0):
                            act.wait_ge(pair_free[gu.pair(1)], gu.uses(i, 1))
                        act.wait_ge(slots_used, gu.end(i, 0))
                        for t in range(NT):
                            last = nc.scalar.activation(sg[:, t, :], ps[:, 2 * gu.pair(0) + t, :], ACT.Silu,
                                                        scale=rstd(e, t))
                        last.then_inc(pair_free[gu.pair(0)], 1)

                    def h_hi(i):
                        for b in range(2):
                            act.wait_ge(hm_t, 2 * (fb + i) + b + 1)
                            nc.scalar.activation(hthi[:, bass.ds(4 * i + 2 * b, 2), :],
                                                 ps[:, 4 + b, :].rearrange("p (k t) -> p k t", k=2),
                                                 ACT.Copy).then_inc(ht_hi, 1)

                    carried = walk(act, gu, split_hi(gu), [(9, 1, h_hi), (11, 0, silu)], carried,
                                   skip=RING if g == 0 else 0)
                    carried = walk(act, dn, split_hi(dn), each_chunk(dn, chunk_squares(dn, 2 * w, F)) if g else [], carried)
                    return carried

                carried = pre_norm(2 * w, e, F)
                for g, (gu, dn) in enumerate(groups):
                    carried = group(g, gu, dn, carried)
                if following:
                    ahead(following, range(LEAD))
                for _, fn in carried:
                    fn()

            act.dma_start(kc[:, :], consts).then_inc(c_in, 16)
            act.dma_start(F1[0][:, :, :], x[0].rearrange("(t p) d -> p t d", p=P)).then_inc(x_in, 16)
            act.wait_ge(vr_zero, 1)
            for v, r, n in VECTORS[:N_VEC // 2]:
                dst = vrows[r % P:r % P + n, 0, (r // P) * P:(r // P) * P + v.shape[-1]]
                act.dma_start(dst, v).then_inc(vr_in_a, 16)
            ahead(passes[0])
            act.wait_ge(x_in, 16)
            act.wait_ge(vec_t, 1)
            nc.scalar.activation(vec[:, :], ps[:, 4, 0:256], ACT.Copy).then_inc(vec_copied, 1)
            act.wait_ge(vec_copied, 1)
            transposed_hi(0, R_F1)
            feed_forward(0, F1, ffn1, 0, p_rw)
            ahead(p_rw, [LEAD])
            transposed_hi(1, R_MIX)

            def to_proj(p, c0):
                def fn(i, u):
                    act.wait_ge(slots_used, p.end(i, u))
                    for t in range(NT):
                        last = nc.scalar.activation(proj[:, t, bass.ds((p.unroll * i + u) * CW + c0, p.width)],
                                                    ps[:, 2 * p.pair(u) + t, 0:p.width], ACT.Identity, scale=rstd(2, t))
                    last.then_inc(pair_free[p.pair(u)], 1)
                return fn

            def to_stage(p, tile, func, before):
                def fn(i, u):
                    act.wait_ge(slots_used, p.end(i, u))
                    b = p.pair(u)
                    if not (isinstance(i, int) and i + before == 0):
                        act.wait_ge(st_out[b], 16 * i + 16 * before)
                    for t in range(NT):
                        last = nc.scalar.activation(tile[:, b, t, :], ps[:, 2 * b + t, :], func, scale=rstd(2, t))
                    last.then_inc(pair_free[b], 1)
                return fn

            h_gone = [(10, lambda: act.wait_ge(h_saved, 16))]
            carried = walk(act, p_rw, split_hi(p_rw), each_chunk(p_rw, to_proj(p_rw, 0)), pre_norm(1, 2, F1) + h_gone, skip=RING)
            carried = walk(act, p_rw7, split_hi(p_rw7), each_chunk(p_rw7, to_proj(p_rw7, 6 * CW)), carried)
            dif_out = to_stage(p_dif, dst_a, ACT.Identity, 0)
            first_gates = [lambda k=k: split_hi(p_gate)(p_gate.n0 + k, 0, 0, k) for k in range(RING)]
            fill = filler(in_steps(p_dif, split_hi(p_dif), each_chunk(p_dif, dif_out),
                                   first_gates[:-1] + [lambda: (first_gates[-1](), dif_out(2, 1))]))
            fill(LEAD)
            for _, fn in carried:
                fn()
            fill(BEFORE_SHIFT)

            act.wait_ge(vec_ready, 1)
            for n in range(NBLK):
                w = 32 if BLOCKS[n] == NBLK - 1 else P
                act.wait_ge(sh_t, n + 1)
                if n >= 2:
                    act.wait_ge(shifted, n - 1)
                nc.scalar.activation(ybuf[0:w, n % 2, 1:T + 1], ps[0:w, 4 + n % 4, 0:T], ACT.Copy)
                kind, b = BLOCKS[n] // 8, BLOCKS[n] % 8
                if kind == 2 and b >= 2:
                    act.wait_ge((v_out0, v_out1)[b % 2], 16 * (b // 2))
                nc.scalar.activation(shift_tile(BLOCKS[n])[0:w, :], ps[0:w, 4 + n % 4, 0:T], ACT.Identity,
                                     scale=vecd[0:w, D_MU + BLOCKS[n]:D_MU + BLOCKS[n] + 1]).then_inc(sh_y, 1)
                fill(IN_SHIFT[n % 2])
            act.wait_ge(shifted, 4)
            nc.scalar.activation(lwa[:, 0, :], lwa[:, 0, :], ACT.Tanh).then_inc(lora_act, 1)
            act.wait_ge(shifted, NBLK)
            nc.scalar.activation(lgd[:, 0, :], lgd[:, 0, :], ACT.Tanh, scale=0.5)
            nc.scalar.activation(lgd[0:32, 1, :], lgd[0:32, 1, :], ACT.Tanh, scale=0.5).then_inc(lora_act, 1)
            for b in range(NPAIR):
                nc.scalar.activation(kkn[:, b, :], kr[:, b, :], ACT.Identity,
                                     scale=vec[:, R_KK + b:R_KK + b + 1]).then_inc(kk_raw, 1)
                act.wait_ge(kk_raw, b + 1)
                if b >= 2:
                    act.wait_ge(kk_sum, b - 1)
                nc.scalar.activation(sqb[:, b % 2, :], kkn[:, b, :], ACT.Square).then_inc(kk_sq, 1)
                fill(IN_KK[b % 2])
            act.wait_ge(kk_max, 1)
            nc.scalar.activation(s16[:, 1, :], s16[:, 0, :], ACT.Sqrt).then_inc(kk_sqrt, 1)
            for b in range(NPAIR):
                act.wait_ge(g_mm, b + 1)
                if b >= 2:
                    act.wait_ge(g_out[b % 2], 16 * (b // 2))
                nc.scalar.activation(gst[:, b % 2, :], ps[:, 4 + b % 2, 0:T], ACT.Copy).then_inc(g_st, 1)
                fill(IN_G[b % 2])
            act.wait_ge(kk_ready, NPAIR)
            act.wait_ge(g_out[0], 16 * (NPAIR // 2))
            act.wait_ge(g_out[1], 16 * (NPAIR // 2))
            n_out_dst = n_dram.rearrange("h m c s t -> h m s c t")

            def stage_out(m):
                act.wait_ge(n_st, m + 1)
                for h in range(2):
                    act.dma_start(n_out_dst[h, m], nst[C * h:C * (h + 1), m % 2, :, :]).then_inc(n_out[m % 2], 16)

            for m in range(NM):
                b, d = m // 2, m % 2
                act.wait_ge(za_mm, m + 1)
                if m:
                    act.wait_ge(aa_ready, m)
                for w, col in ((0, D_W0), (1, D_A0)):
                    last = nc.scalar.activation(tz[:, w, :], ps[:, 4 + m % 2, w * T:(w + 1) * T], ACT.Tanh, scale=0.5,
                                                bias=vecd[:, col + 8 * d + b:col + 8 * d + b + 1])
                last.then_inc(za_act, 1)
                act.wait_ge(ex_in, m + 1)
                if m:
                    act.wait_ge(q_ready, m)
                    act.wait_ge(ra_ready, 2 * m)
                nc.scalar.activation(eie[:, 0:2, :], ie[:, :, :], ACT.Exp)
                nc.scalar.activation(eie[:, 2, :], ie[:, 0, :], ACT.Exp, scale=-1.0).then_inc(ex_out, 1)
                fill(IN_CHUNKS[m % 2])
                if m >= 2:
                    stage_out(m - 2)
            stage_out(NM - 2)
            stage_out(NM - 1)
            fill(1)

            carried = walk(act, p_gate, split_hi(p_gate), each_chunk(p_gate, to_stage(p_gate, gst_g, ACT.Sigmoid, 3)), (), skip=RING)
            for _, fn in carried:
                fn()
            ahead(p_ya)

            act.wait_ge(zs_in, 32)
            for b in range(2):
                act.wait_ge(st_out[b], 16 * 7)

            def values(m):
                act.wait_ge(vt_mm, m + 1)
                if m >= 2:
                    act.wait_ge(o_mm, m - 1)
                nc.scalar.activation(sv[C:P, m % 2, :, :], ps[C:P, 2, :].rearrange("p (c v) -> p c v", c=NC_),
                                     ACT.Copy).then_inc(vt_ready, 1)

            def minus_w(m):
                act.wait_ge(w_mm, m + 1)
                nc.scalar.activation(wt[:, m % 2, :, :], ps[:, 3, :].rearrange("p (c v) -> p c v", c=NC_),
                                     ACT.Copy, scale=-1.0).then_inc(w_ready, 1)

            minus_w(0)
            values(0)
            for m in range(NM):
                if m + 1 < NM:
                    minus_w(m + 1)
                    values(m + 1)
                for c in range(NC_ - 1):
                    act.wait_ge(s_mm, 3 * m + c + 1)
                    nc.scalar.activation(sv[0:C, m % 2, c + 1, :], ps[0:C, 6, 0:2 * C], ACT.Copy).then_inc(s_ready, 1)
            for b in range(NPAIR):
                act.wait_ge(gn_cent, b + 1)
                if b >= 2:
                    act.wait_ge(gn_var, b - 1)
                nc.scalar.activation(osq[:, b % 2, :], oc[:, b, :], ACT.Square).then_inc(gn_sq, 1)
            act.wait_ge(gn_varv, 1)
            nc.scalar.activation(o16[:, 2, :], o16[:, 1, :], ACT.Sqrt).then_inc(gn_sqrt, 1)
            for b in range(NPAIR):
                act.wait_ge(ya_y, b + 1)
                nc.scalar.activation(ythi[:, b, :], oc[:, b, :], ACT.Copy).then_inc(ya_hi, 1)

            first_yb = [lambda k=k: split_hi(p_yb)(p_yb.n0 + k, 0, k // 4, k % 4) for k in range(RING)]
            fill = filler(in_steps(p_ya, split_hi(p_ya), [], first_yb, skip=RING))
            fill(LEAD + IN_ROPE)
            act.wait_ge(lam_sum, 1)
            nc.scalar.activation(lamb[:, 2:4], lamb[:, 0:2], ACT.Exp).then_inc(lam_exp, 1)
            for n in range(16):
                act.wait_ge(qt_mm, n + 1)
                dst = (qt_, kt_)[n // 8][:, n % 8, :]
                nc.scalar.activation(dst, ps[:, 4 + n % 4, 0:T], ACT.Copy).then_inc(qt_ready, 1)

            def exps(n):
                act.wait_ge(mx_ready, n + 1)
                if n >= 2:
                    act.wait_ge(am_ready, n - 1)
                for v in range(2):
                    for s in range(2):
                        w = 2 * (n % 2) + v
                        last = nc.scalar.activation(pex[:, w, s, :], ps[:, s, v * T:(v + 1) * T], ACT.Exp, scale=0.125,
                                                    bias=mx[:, w, s:s + 1], accum_out=su[:, w, s:s + 1])
                last.then_inc(ex_p, 1)

            def maps_out(n):
                act.wait_ge(am_t, n + 1)
                if n >= 2:
                    act.wait_ge(pv_mm, n // 2)
                v = 2 * (n % 2)
                nc.scalar.activation(amt[:, v:v + 2, :], ps[:, 4 + n % 2, :].rearrange("p (v t) -> p v t", v=2),
                                     ACT.Copy).then_inc(amt_ready, 1)

            def yb_high(g):
                act.wait_ge(yb_t, g + 1)
                hs, t = 4 * (g % 2), g // 2
                nc.scalar.activation(ythi[:, 8 + hs:12 + hs, t * P:(t + 1) * P],
                                     ps[:, 7, :].rearrange("p (v t) -> p v t", v=4), ACT.Identity,
                                     scale=vecd[:, D_SUB:D_SUB + 1]).then_inc(yb_hi, 1)

            exps(0)
            exps(1)
            for g in range(4):
                maps_out(2 * g)
                if g < 3:
                    exps(2 * g + 2)
                maps_out(2 * g + 1)
                if g:
                    yb_high(g - 1)
                if g < 3:
                    fill(IN_HEADS[0])
                    exps(2 * g + 3)
                    fill(IN_HEADS[1])
                act.wait_ge(pv_mm, g + 1)
                if g:
                    act.wait_ge(pv_ms, g)
                for v in range(4):
                    last = nc.scalar.activation(oj[:, v, :], ps[:, 6, v * P:(v + 1) * P], ACT.Square,
                                                accum_out=os_[:, v:v + 1])
                last.then_inc(pv_sq, 1)
            yb_high(3)

            fill(1)
            walk(act, p_yb, split_hi(p_yb), [], (), skip=RING)
            ahead(p_out)
            transposed_hi(2, None)
            carried = walk(act, p_out, split_hi(p_out), each_chunk(p_out, chunk_squares(p_out, 1, F2)), (), skip=RING)
            ahead(ffn2[0][0], range(LEAD))
            for _, fn in carried:
                fn()
            ahead(ffn2[0][0], [LEAD])
            transposed_hi(3, R_F2)
            feed_forward(1, F2, ffn2, 4, None)

        @block.vector
        def _(dve):
            links = [0]

            def link(ins):
                links[0] += 1
                ins.then_inc(dve_link, 1)
                dve.wait_ge(dve_link, links[0])

            V = nc.vector

            def split_lo(p):
                def slot(n, i, u, j):
                    s = slot_of(p, u, j)
                    dve.wait_ge(hi_ready, n + 1)
                    V.tensor_tensor(wlo[:, s, :, 0:p.width], raw[:, s, :, 0:p.width],
                                    whi[:, s, :, 0:p.width].bitcast(F32), ALU.subtract).then_inc(lo_ready, 1)
                return slot

            def ahead(p, slots=range(RING)):
                for k in slots:
                    split_lo(p)(p.n0 + k, 0, 0, k)

            def pre_norm(nth, e):
                def mean_square():
                    dve.wait_ge(ss_ready, NT * (nth + 1))
                    V.tensor_scalar(sm[:, MS[e]], sm[:, SS[e]], 1.0 / D, EPS, ALU.mult, ALU.add).then_inc(ms_ready, 1)
                return [(8, mean_square), (10, lambda: dve.wait_ge(rstd_ready, e + 1))]

            def times_gain(p, nth, F):
                def fn(i, u):
                    c = 2 * i + u
                    dve.wait_ge(fs_ready, 4 * nth + c + 1)
                    dve.wait_ge(gain_in, 16 * (nth + 1))
                    f = F[1][:, :, bass.ds(c * CW, CW)]
                    V.tensor_tensor(f, f, F[6][:, bass.ds(c * CW, CW)].unsqueeze(1).broadcast_to((P, NT, CW)),
                                    ALU.mult).then_inc(fg_ready, 1)
                return fn

            def gain_hooks(p, nth, F):
                fn = times_gain(p, nth, F)
                return [(5, 1, lambda i: fn(i, 1)), (p.slots + 5, 0, lambda i: fn(i, 0))]

            def transposed_lo(e, col, first=None):
                for k in range(KB):
                    if first is not None and k == KB // 2:
                        ahead(first, [LEAD])
                    dve.wait_ge(ut_hi, ut_base(e) + k + 1)
                    bank, hi = ps[:, 4 + k % 4, 0:T], uhi[:, k, :].bitcast(F32)
                    if col is None:
                        V.tensor_tensor(ulo[:, k, :], bank, hi, ALU.subtract).then_inc(ut_lo, 1)
                    else:
                        V.scalar_tensor_tensor(out=ulo[:, k, :], in0=bank, scalar=vec[:, col + k:col + k + 1], in1=hi,
                                               op0=ALU.mult, op1=ALU.subtract).then_inc(ut_lo, 1)

            def post_norm(e, nth, F, weight):
                h, f = F[0], F[1]
                dve.wait_ge(fs_ready, 4 * (nth + 1))
                link(V.tensor_reduce(sm[:, SS[e]], sm[:, QS].rearrange("p (t c) -> p t c", t=NT), AX.X, ALU.add))
                V.tensor_scalar(sm[:, MS[e]], sm[:, SS[e]], 1.0 / D / weight ** 2, EPS / weight ** 2,
                                ALU.mult, ALU.add).then_inc(ms_ready, 1)
                times_gain(None, nth, F)(1, 1)
                dve.wait_ge(rstd_ready, e + 1)
                dve.wait_ge(fg_ready, 4 * (nth + 1))
                for c in range(D // CW):
                    for t in range(NT):
                        hc = h[:, t, c * CW:(c + 1) * CW]
                        V.scalar_tensor_tensor(out=hc, in0=f[:, t, c * CW:(c + 1) * CW], scalar=rstd(e, t), in1=hc,
                                               op0=ALU.mult, op1=ALU.add).then_inc(h_ready, 1)

            def feed_forward(w, F, groups, e, following):
                h, f, hthi, htlo, sg, hm, gain = F

                def group(g, gu, dn, carried):
                    f0, f1 = FF_GROUPS[g]
                    fb = w * FFC + f0

                    def times_up(i):
                        dve.wait_ge(pair_free[gu.pair(0)], gu.uses(i, 0) + 1)
                        dve.wait_ge(slots_used, gu.end(i, 1))
                        for t in range(NT):
                            last = V.scalar_tensor_tensor(out=hm[:, t, :], in0=ps[:, 2 * gu.pair(1) + t, :],
                                                          scalar=rstd(e, t), in1=sg[:, t, :], op0=ALU.mult, op1=ALU.mult)
                        last.then_inc(pair_free[gu.pair(1)], 1)

                    def h_lo(i):
                        for b in range(2):
                            dve.wait_ge(ht_hi, 2 * (fb + i) + b + 1)
                            V.tensor_tensor(htlo[:, bass.ds(4 * i + 2 * b, 2), :],
                                            ps[:, 4 + b, :].rearrange("p (k t) -> p k t", k=2),
                                            hthi[:, bass.ds(4 * i + 2 * b, 2), :].bitcast(F32),
                                            ALU.subtract).then_inc(ht_lo, 1)

                    def to_f(i, u):
                        dve.wait_ge(slots_used, dn.end(i, u))
                        for t in range(NT):
                            dst, src = f[:, t, bass.ds((2 * i + u) * CW, CW)], ps[:, 2 * dn.pair(u) + t, :]
                            last = V.tensor_tensor(dst, dst, src, ALU.add) if g else V.tensor_copy(dst, src)
                        last.then_inc(pair_free[dn.pair(u)], 1)

                    carried = walk(dve, gu, split_lo(gu), [(3, 1, times_up), (9, 1, h_lo)], carried,
                                   skip=RING if g == 0 else 0)
                    carried = walk(dve, dn, split_lo(dn), each_chunk(dn, to_f) + (gain_hooks(dn, 2 * w, F) if g else []), carried)
                    return carried

                carried = pre_norm(2 * w, e)
                for g, (gu, dn) in enumerate(groups):
                    carried = group(g, gu, dn, carried)
                if following:
                    ahead(following, range(LEAD))
                carried[0][1]()

            V.memset(vrows[:, 0, 0:256], 0.0).then_inc(vr_zero, 1)
            V.memset(sm[:, QS], 0.0).then_inc(ht_lo, 2)
            ahead(passes[0])
            dve.wait_ge(c_in, 16)
            transposed_lo(0, R_F1)
            dve.wait_ge(vec_copied, 1)
            link(V.tensor_tensor(vecd[:, 0:28], vec[:, R_MUP:R_MUP + 28], vec[:, R_MUN:R_MUN + 28], ALU.add))
            link(V.tensor_scalar(vecd[:, 0:28], vecd[:, 0:28], -1.0, 1.0, ALU.mult, ALU.add))
            V.tensor_scalar(vecd[:, D_W0:D_A0], vec[:, R_W0:R_W0 + 16], 0.5, None, ALU.mult)
            V.tensor_scalar(vecd[:, D_A0:D_KA], vec[:, R_A0:R_A0 + 16], 0.5, None, ALU.mult)
            V.tensor_scalar(vecd[:, D_KA:D_KA1], vec[:, R_KA:R_KA + 8], 0.5, None, ALU.mult)
            V.tensor_scalar(vecd[:, D_KA1:D_SUB], vec[:, R_KA:R_KA + 8], -0.5, 1.0, ALU.mult, ALU.add)
            V.tensor_scalar(vecd[:, D_SUB:D_SUB + 1], vec[:, R_SUB:R_SUB + 1], 1.0 - LAM_INIT, None, ALU.mult).then_inc(vec_ready, 1)
            feed_forward(0, F1, ffn1, 0, p_rw)
            post_norm(1, 0, F1, 0.5)
            transposed_lo(1, R_MIX, p_rw)
            for p in (p_rw, p_rw7):
                walk(dve, p, split_lo(p), [], pre_norm(1, 2) if p is p_rw else (), skip=RING if p is p_rw else 0)
            fill = filler(in_steps(p_dif, split_lo(p_dif), [],
                                   [lambda k=k: split_lo(p_gate)(p_gate.n0 + k, 0, 0, k) for k in range(RING)]))
            fill(LEAD + BEFORE_SHIFT)

            dve.wait_ge(h_saved, 16)
            for i in range(2):
                V.memset(ybuf[:, i, 0:1], 0.0)
                link(V.memset(ybuf[:, i, T + 1:T + 2], 0.0))
            for n, j in enumerate(BLOCKS):
                w = 32 if j == NBLK - 1 else P
                dst = shift_tile(j)[0:w, :]
                y = ybuf[0:w, n % 2, :]
                dve.wait_ge(sh_y, n + 1)
                link(V.scalar_tensor_tensor(out=dst, in0=y[:, 0:T], scalar=vec[0:w, R_MUP + j:R_MUP + j + 1], in1=dst,
                                            op0=ALU.mult, op1=ALU.add))
                V.scalar_tensor_tensor(out=dst, in0=y[:, 2:T + 2], scalar=vec[0:w, R_MUN + j:R_MUN + j + 1], in1=dst,
                                       op0=ALU.mult, op1=ALU.add).then_inc(shifted, 1)
                fill(IN_SHIFT[n % 2])
            dve.wait_ge(lora_act, 2)
            link(V.tensor_scalar(lgd[0:32, 1, :], lgd[0:32, 1, :], 0.5, 0.5, ALU.mult, ALU.add))
            V.tensor_scalar(lgd[:, 0, :], lgd[:, 0, :], 0.5, 0.5, ALU.mult, ALU.add).then_inc(gd_ready, 1)
            fill(sum(IN_KK) * NPAIR // 2)
            dve.wait_ge(kk_sum, NPAIR)
            V.tensor_scalar(s16[:, 0, :], ps[0:NH, 6, 0:T], 1e-24, None, ALU.max).then_inc(kk_max, 1)
            dve.wait_ge(kk_sqrt, 1)
            V.reciprocal(s16[:, 0, :], s16[:, 1, :]).then_inc(kk_rec, 1)
            fill(sum(IN_G) * NPAIR // 2)
            for b in range(NPAIR):
                dve.wait_ge(kk_bc, b + 1)
                V.tensor_tensor(kkn[:, b, :], kkn[:, b, :], ps[:, 6 + b % 2, 0:T], ALU.mult).then_inc(kk_ready, 1)
            dve.wait_ge(v_out0, 16 * 4)
            dve.wait_ge(v_out1, 16 * 4)
            V.tensor_copy(q[0:C, 0, :], ident[0:C, 0:C])
            link(V.tensor_copy(q[C:P, 0, :], ident[C:P, C:P]))
            dve.wait_ge(g_out[0], 16 * (NPAIR // 2))
            dve.wait_ge(g_out[1], 16 * (NPAIR // 2))
            dve.wait_ge(kk_ready, NPAIR)

            def n_evac(m):
                dve.wait_ge(n_mm, m + 1)
                if m >= 2:
                    dve.wait_ge(n_out[m % 2], 32 * (m // 2))
                V.tensor_tensor(nst[:, m % 2, :, :], ps[:, 6 + m % 2, 0:T].rearrange("p (c t) -> p c t", c=NC_),
                                kc[:, K_MN:K_M1].unsqueeze(1).broadcast_to((P, NC_, C)), ALU.mult).then_inc(n_st, 1)

            def bonus(b):
                dve.wait_ge(bon_mm, b + 1)
                dve.wait_ge(v1_in, 16 * (b + 1))
                if b:
                    dve.wait_ge(bon_out, 16 * b)
                V.tensor_tensor(bst[:, :], ps[:, 6, T:2 * T], vb1[:, :], ALU.mult).then_inc(bon_st, 1)

            for m in range(NM):
                b, d = m // 2, m % 2
                sgn = slice(None, None, -1) if d else slice(None)
                r_, k_, kk_ = rr[:, b, sgn], kr[:, b, sgn], kkn[:, b, sgn]
                dve.wait_ge(za_act, m + 1)
                link(V.tensor_scalar(ld[:, :], tz[:, 0, :], -0.5 * DECAY, -0.5 * DECAY, ALU.mult, ALU.add))
                if m:
                    dve.wait_ge(ex_out, m)
                link(V.tensor_tensor_scan(ie[:, 0, :], kc[:, K_RESET:K_COS], ld[:, :], 0.0, ALU.mult, ALU.add))
                V.tensor_tensor(ie[:, 1, :], ie[:, 0, :], ld[:, :], ALU.subtract).then_inc(ex_in, 1)
                if d == 0 and b:
                    dve.wait_ge(bon_in, b)
                link(V.tensor_scalar(kd[:, :], tz[:, 1, :], vecd[:, D_KA + b:D_KA + b + 1], vecd[:, D_KA1 + b:D_KA1 + b + 1],
                                     ALU.mult, ALU.add))
                V.tensor_scalar(aa[:, :], tz[:, 1, :], 0.5, 0.5, ALU.mult, ALU.add).then_inc(aa_ready, 1)
                dve.wait_ge(aa_ready, m + 1)
                link(V.tensor_tensor(kd[:, :], kd[:, :], k_, ALU.mult))
                link(V.tensor_tensor(aa[:, :], aa[:, :], kk_, ALU.mult))
                if d == 0:
                    if b:
                        dve.wait_ge(bon_mm, b)
                    link(V.tensor_copy(kds[:, :], kd[:, :]))
                else:
                    link(V.tensor_tensor(kds[:, :], kds[:, :], kd[:, ::-1], ALU.add))
                    V.scalar_tensor_tensor(out=kds[:, :], in0=kds[:, :], scalar=vec[:, R_RK + b:R_RK + b + 1],
                                           in1=rr[:, b, :], op0=ALU.mult, op1=ALU.mult).then_inc(bon_in, 1)
                dve.wait_ge(ex_out, m + 1)
                s0 = 1 + 3 * NC_ * m
                qv = q[:, s0:s0 + 3 * NC_, :].rearrange("p (c w) t -> p c w t", w=3)
                ch = lambda a: a.rearrange("p (c t) -> p c t", c=NC_)
                V.tensor_tensor(qv[:, :, 1, :], ch(kd[:, :]), ch(eie[:, 2, :]), ALU.mult)
                V.tensor_tensor(beta[:, m, :], aa[:, :], eie[:, 2, :], ALU.mult)
                V.tensor_copy(pend[:, m, :], ch(eie[:, 0, :])[:, :, C - 1]).then_inc(q_ready, 1)
                if m:
                    n_evac(m - 1)
                if d == 0 and b:
                    bonus(b - 1)
                fill(IN_CHUNKS[d])
            n_evac(NM - 1)
            bonus(NPAIR - 1)
            fill(1)

            ones = z[:, :, :].rearrange("p c t -> p (c t)")[:, 0:C * C:C + 1]

            def steps_before(k):
                first, last = 8, slots - 9
                return min(max(k - first, 0) * (C - 1) // (last - first), C - 1)

            def step(s):
                if s == 0:
                    dve.wait_ge(z_in, 16)
                    link(V.memset(ones, 1.0))
                    return
                if s >= C - 1:
                    return
                n = C - 1 - s
                prod = zt[:, 0:s * n].rearrange("p (c t) -> p c t", c=s)
                rest = z[:, 0:s, s + 1:C]
                link(V.tensor_tensor(prod, z[:, 0:s, s:s + 1].broadcast_to((P, s, n)),
                                     z[:, s:s + 1, s + 1:C].broadcast_to((P, s, n)), ALU.mult))
                if s == C - 2:
                    V.tensor_tensor(rest, rest, prod, ALU.add).then_inc(z_done, 1)
                else:
                    link(V.tensor_tensor(rest, rest, prod, ALU.add))

            slots = p_gate.chunks * p_gate.slots
            for k in range(slots):
                if k >= RING:
                    split_lo(p_gate)(p_gate.n0 + k, 0, k // p_gate.slots, k % p_gate.slots)
                for s in range(steps_before(k), steps_before(k + 1)):
                    step(s)
            ahead(p_ya)

            dve.wait_ge(zs_in, 32)
            V.memset(sv[0:C, 0, 0, :], 0.0)
            V.memset(sv[0:C, 1, 0, :], 0.0).then_inc(sv_zero, 1)

            def ends(m):
                if m >= 2:
                    dve.wait_ge(gh_mm, 2 * (m - 1))
                at = 1 + 3 * NC_ * NM + NC_ * (m % 2)
                V.tensor_tensor(q[:, at:at + NC_, :], q[:, 0:1, :].broadcast_to((P, NC_, C)),
                                pend[:, m, :].unsqueeze(2).broadcast_to((P, NC_, C)), ALU.mult).then_inc(dd_ready, 1)

            def masked_ab(m):
                for h in range(2):
                    dve.wait_ge(ab_mm, 2 * m + h + 1)
                    if m >= 2 and h == 0:
                        dve.wait_ge(gh_mm, 2 * (m - 1))
                    V.tensor_tensor(mb[:, m % 2, 2 * h:2 * h + 2, :],
                                    ps[:, h, :].rearrange("p (c v) -> p c v", c=2),
                                    kc[:, K_M1:K_MG].unsqueeze(1).broadcast_to((P, 2, 4 * C)), ALU.mult).then_inc(ab_ready, 1)

            def masked_gh(m):
                for h in range(2):
                    dve.wait_ge(gh_mm, 2 * m + h + 1)
                    if m >= 2 and h == 0:
                        dve.wait_ge(o_mm, m - 1)
                    V.tensor_tensor(gh[:, m % 2, 4 * h:4 * h + 4, :],
                                    ps[:, 4 + h, :].rearrange("p (c v) -> p c v", c=4),
                                    kc[:, K_MG:K_RESET].unsqueeze(1).broadcast_to((P, 4, 2 * C)), ALU.mult).then_inc(gh_ready, 1)

            def to_oc(m):
                b = m // 2
                dve.wait_ge(o_mm, m + 1)
                src = ps[:, 7, 0:T]
                if m % 2:
                    V.tensor_tensor(oc[:, b, :], oc[:, b, :], src[:, ::-1], ALU.add).then_inc(o_ready, 1)
                else:
                    V.tensor_copy(oc[:, b, :], src).then_inc(o_ready, 1)

            for m in range(2):
                ends(m)
                masked_ab(m)
            masked_gh(0)
            dve.wait_ge(st_out[0], 16 * 7)
            dve.wait_ge(st_out[1], 16 * 7)
            for m in range(NM):
                if m + 2 < NM:
                    ends(m + 2)
                    masked_ab(m + 2)
                to_oc(m)
                dve.wait_ge(o_ready, m + 1)
                if m + 1 < NM:
                    masked_gh(m + 1)
            dve.wait_ge(gn_sum, 1)
            V.tensor_scalar(o16[:, 0, :], ps[0:NH, 0, 0:T], 1.0 / 64, None, ALU.mult).then_inc(gn_mean, 1)
            for b in range(NPAIR):
                dve.wait_ge(gn_bc, b + 1)
                V.tensor_tensor(oc[:, b, :], oc[:, b, :], ps[:, 4 + b % 4, 0:T], ALU.subtract).then_inc(gn_cent, 1)
            dve.wait_ge(gn_var, NPAIR)
            V.tensor_scalar(o16[:, 1, :], ps[0:NH, 1, 0:T], 1.0 / 64, GN_EPS, ALU.mult, ALU.add).then_inc(gn_varv, 1)
            dve.wait_ge(gn_sqrt, 1)
            V.reciprocal(o16[:, 3, :], o16[:, 2, :]).then_inc(gn_rec, 1)
            dve.wait_ge(gn_in, 16 * 3)
            for b in range(NPAIR):
                dve.wait_ge(gn_bc2, b + 1)
                y = oc[:, b, :]
                link(V.scalar_tensor_tensor(out=y, in0=y, scalar=vec[:, R_GNW + b:R_GNW + b + 1],
                                            in1=ps[:, 4 + b % 4, 0:T], op0=ALU.mult, op1=ALU.mult))
                link(V.scalar_tensor_tensor(out=y, in0=y, scalar=vec[:, R_GNB + b:R_GNB + b + 1], in1=bo[:, b, :],
                                            op0=ALU.add, op1=ALU.add))
                V.tensor_tensor(y, y, gg[:, b, :], ALU.mult).then_inc(ya_y, 1)
            for b in range(NPAIR):
                dve.wait_ge(ya_hi, b + 1)
                V.tensor_tensor(ytlo[:, b, :], oc[:, b, :], ythi[:, b, :].bitcast(F32), ALU.subtract).then_inc(ya_lo, 1)

            def merge_a(c):
                b = p_ya.pair(0)
                dve.wait_ge(slots_used, p_ya.end(c // 2, c % 2))
                dve.wait_ge(gt_in[c % 2], 16 * (c // 2 + 1))
                if c == 0:
                    dve.wait_ge(k_roped, 2 * NT)
                V.tensor_tensor(mg[:, c, 0, :], ps[:, 2 * b, :], gbuf[:, c % 2, 0, :], ALU.mult).then_inc(pair_free[1 - b], 1)
                V.tensor_tensor(mg[:, c, 1, :], ps[:, 2 * b + 1, :], gbuf[:, c % 2, 1, :], ALU.mult).then_inc(pair_free[b], 1)

            def merge_b(c):
                b = p_yb.pair(c % 2)
                dve.wait_ge(slots_used, p_yb.end(c // 2, c % 2))
                dve.wait_ge(gt_in[c % 2], 16 * (c // 2 + 3))
                if c:
                    dve.wait_ge(mg_ready, c)
                for t in range(NT):
                    last = V.tensor_tensor(mt[:, t, :], ps[:, 2 * b + t, :], gbuf[:, c % 2, t, :], ALU.mult)
                last.then_inc(pair_free[b], 1)
                dve.wait_ge(pair_free[b], p_yb.uses(c // 2, c % 2) + 1)
                V.tensor_tensor(mg[:, c, :, :], mg[:, c, :, :], mt[:, :, :], ALU.add).then_inc(mg_ready, 1)

            first_yb = [lambda k=k: split_lo(p_yb)(p_yb.n0 + k, 0, k // 4, k % 4) for k in range(RING)]
            fill = filler(in_steps(p_ya, split_lo(p_ya), [], first_yb, skip=RING))
            dve.wait_ge(ya_lo, NPAIR)
            dve.wait_ge(k_in, 16)
            for t in range(NT):
                rope(V, qk[:, t, 0:RW], t, ra, rb, roped, t, dve)
                fill((LEAD + IN_ROPE) // NT if t else LEAD + IN_ROPE - (LEAD + IN_ROPE) // NT)
            dve.wait_ge(at_in, 16 * 5)
            for i in range(2):
                link(V.tensor_tensor(lamv[:, 2 * i, :], lamv[:, 2 * i, :], lamv[:, 2 * i + 1, :], ALU.mult))
                last = V.tensor_reduce(lamb[:, i:i + 1], lamv[:, 2 * i, :], AX.X, ALU.add)
            last.then_inc(lam_sum, 1)
            dve.wait_ge(lam_exp, 1)
            link(V.tensor_tensor(lamb[:, 4:5], lamb[:, 3:4], lamb[:, 2:3], ALU.subtract))
            link(V.tensor_scalar(lamb[:, 5:6], lamb[:, 4:5], -LAM_INIT, None, ALU.add))

            def maxima(n):
                dve.wait_ge(sc_mm, n + 1)
                for s in range(2):
                    last = V.tensor_reduce(mx[:, 2 * (n % 2):2 * (n % 2) + 2, s],
                                           ps[:, s, :].rearrange("p (v t) -> p v t", v=2), AX.X, ALU.max)
                link(last)
                pair = mx[:, 2 * (n % 2):2 * (n % 2) + 2, :]
                V.tensor_scalar(pair, pair, -0.125, None, ALU.mult).then_inc(mx_ready, 1)

            def maps(n):
                dve.wait_ge(ex_p, n + 1)
                if n >= 2:
                    dve.wait_ge(am_t, n - 1)
                vs = (2 * (n % 2), 2 * (n % 2) + 1)
                pair = su[:, vs[0]:vs[1] + 1, :]
                link(V.reciprocal(pair, pair))
                link(V.tensor_tensor(pair[:, :, 1], pair[:, :, 1], lamb[:, 5:6].broadcast_to((P, 2)), ALU.mult))
                for v in vs:
                    last = V.tensor_scalar(am[:, v, :], pex[:, v, 1, :], su[:, v, 1:2], None, ALU.mult)
                link(last)
                for v in vs:
                    last = V.scalar_tensor_tensor(out=am[:, v, :], in0=pex[:, v, 0, :], scalar=su[:, v, 0:1],
                                                  in1=am[:, v, :], op0=ALU.mult, op1=ALU.add)
                last.then_inc(am_ready, 1)

            def norm_heads(g):
                dve.wait_ge(pv_rs, g + 1)
                if g:
                    dve.wait_ge(yb_t, g)
                V.tensor_tensor(ov[:, :, :], ps[:, 6, :].rearrange("p (v i) -> p v i", v=4),
                                os_[:, 8:12].unsqueeze(2).broadcast_to((P, 4, P)), ALU.mult).then_inc(yb_ready, 1)

            def head_squares(g):
                dve.wait_ge(pv_sq, g + 1)
                V.tensor_scalar(os_[:, 4:8], os_[:, 0:4], 1.0 / P, SUBLN_EPS, ALU.mult, ALU.add).then_inc(pv_ms, 1)

            def yb_low(g):
                hs, t = 4 * (g % 2), g // 2
                dve.wait_ge(yb_hi, g + 1)
                V.scalar_tensor_tensor(out=ytlo[:, 8 + hs:12 + hs, t * P:(t + 1) * P],
                                       in0=ps[:, 7, :].rearrange("p (v t) -> p v t", v=4), scalar=vecd[:, D_SUB:D_SUB + 1],
                                       in1=ythi[:, 8 + hs:12 + hs, t * P:(t + 1) * P].bitcast(F32),
                                       op0=ALU.mult, op1=ALU.subtract).then_inc(yb_lo, 1)

            maxima(0)
            maxima(1)
            for g in range(4):
                maps(2 * g)
                if g < 3:
                    maxima(2 * g + 2)
                merge_a(g)
                if g:
                    head_squares(g - 1)
                maps(2 * g + 1)
                if g:
                    norm_heads(g - 1)
                if g < 3:
                    fill(IN_HEADS[0])
                    maxima(2 * g + 3)
                    if g:
                        yb_low(g - 1)
                    fill(IN_HEADS[1])
            yb_low(2)
            head_squares(3)
            norm_heads(3)
            yb_low(3)

            fill(1)
            for k in range(4 * p_yb.slots):
                if k >= RING:
                    split_lo(p_yb)(p_yb.n0 + k, 0, k // 4, k % 4)
                if k % 4 == 3 and k > 4:
                    merge_b(k // 4 - 1)
            merge_b(3)
            ahead(p_out)
            transposed_lo(2, None)

            def out_to_f(i, u):
                dve.wait_ge(slots_used, p_out.end(i, u))
                for t in range(NT):
                    last = V.tensor_copy(F2[1][:, t, bass.ds((2 * i + u) * CW, CW)], ps[:, 2 * p_out.pair(u) + t, :])
                last.then_inc(pair_free[p_out.pair(u)], 1)

            carried = walk(dve, p_out, split_lo(p_out), each_chunk(p_out, out_to_f) + gain_hooks(p_out, 1, F2), (), skip=RING)
            ahead(ffn2[0][0], range(LEAD))
            carried[0][1]()
            dve.wait_ge(h_back, 16)
            post_norm(3, 1, F2, 1.0)
            transposed_lo(3, R_F2, ffn2[0][0])
            feed_forward(1, F2, ffn2, 4, None)
            post_norm(5, 2, F2, 0.5)

        @block.tensor
        def _(pe):
            mm = nc.tensor.matmul

            def product(p, hi, lo, ready=None):
                def slot(n, i, u, j):
                    s = slot_of(p, u, j)
                    first = isinstance(i, int) and i == 0 and u == 0
                    if first and ready is not None:
                        ready(j)
                    if j == 0 and not (isinstance(i, int) and p.uses(i, u) == 0):
                        pe.wait_ge(pair_free[p.pair(u)], p.uses(i, u))
                    pe.wait_ge(lo_ready, n + 1)
                    for k in range(SB):
                        a, b = hi(u, SB * j + k), lo(u, SB * j + k)
                        for t in range(NT):
                            o = ps[:, 2 * p.pair(u) + t, 0:p.width]
                            at, bt = a[:, t * P:(t + 1) * P], b[:, t * P:(t + 1) * P]
                            w_, l_ = whi[:, s, k, 0:p.width], wlo[:, s, k, 0:p.width]
                            mm(o, at, w_, start=(j == 0 and k == 0), stop=False)
                            mm(o, at, l_, start=False, stop=False)
                            last = mm(o, bt, w_, start=False, stop=(j == p.slots - 1 and k == SB - 1))
                    last.then_inc(slots_used, 1)
                return slot

            def from_u(p, e):
                return product(p, lambda u, k: uhi[:, k, :], lambda u, k: ulo[:, k, :],
                               (lambda j: pe.wait_ge(ut_lo, ut_base(e) + SB * (j + 1))) if e is not None else None)

            def transpose_u(e, src, nth):
                for k in range(KB):
                    if src is None and k % 4 == 0:
                        pe.wait_ge(mg_ready, k // 4 + 1)
                    if nth and k % (CW // P) == 0:
                        pe.wait_ge(h_ready, H_PARTS * (nth - 1) + NT * (k // (CW // P) + 1))
                    if k >= 4:
                        pe.wait_ge(ut_lo, ut_base(e) + k - 3)
                    for t in range(NT):
                        block_ = mg[:, k // 4, t, (k % 4) * P:(k % 4 + 1) * P] if src is None else src[:, t, k * P:(k + 1) * P]
                        last = nc.tensor.transpose(ps[:, 4 + k % 4, t * P:(t + 1) * P], block_, ident)
                    last.then_inc(ut_done, 1)

            def feed_forward(w, F, groups, e):
                h, f, hthi, htlo, sg, hm, gain = F

                def group(g, gu, dn, carried):
                    f0, f1 = FF_GROUPS[g]
                    fb = w * FFC + f0

                    def turn_h(i):
                        pe.wait_ge(pair_free[gu.pair(1)], gu.uses(i, 1) + 1)
                        pe.wait_ge(ht_lo, 2 * (fb + i) + 2)
                        for b in range(2):
                            for k in range(2):
                                for t in range(NT):
                                    kk = 2 * b + k
                                    last = nc.tensor.transpose(ps[:, 4 + b, (2 * k + t) * P:(2 * k + t + 1) * P],
                                                               hm[:, t, kk * P:(kk + 1) * P], ident)
                            last.then_inc(hm_t, 1)

                    def h_ready_(j):
                        if j == 0:
                            pe.wait_ge(ht_lo, 2 * (fb + f1 - f0 - 1) + 2)
                        if j == dn.slots - 2:
                            pe.wait_ge(ht_lo, 2 * (fb + f1 - f0) + 2)

                    carried = walk(pe, gu, from_u(gu, e if g == 0 else None), [(3, 1, turn_h)], carried)
                    carried = walk(pe, dn, product(dn, lambda u, k: hthi[:, k, :], lambda u, k: htlo[:, k, :], h_ready_),
                                   [], carried)
                    return carried

                carried = []
                for g, (gu, dn) in enumerate(groups):
                    carried = group(g, gu, dn, carried)
            pe.wait_ge(c_in, 16)
            pe.wait_ge(vr_in, 16 * (N_VEC - N_VEC // 2))
            pe.wait_ge(vr_in_a, 16 * (N_VEC // 2))
            nc.tensor.transpose(ps[:, 4, 0:P], vrows[:, 0, 0:P], ident)
            nc.tensor.transpose(ps[:, 4, P:2 * P], vrows[:, 0, P:2 * P], ident).then_inc(vec_t, 1)
            pe.wait_ge(vec_copied, 1)
            pe.wait_ge(x_in, 16)
            transpose_u(0, F1[0], 0)
            feed_forward(0, F1, ffn1, 0)
            transpose_u(1, F1[0], 1)
            for p in (p_rw, p_rw7):
                walk(pe, p, from_u(p, 1 if p is p_rw else None))
            fill = filler(in_steps(p_dif, from_u(p_dif, None), [], []))
            fill(BEFORE_SHIFT)

            pe.wait_ge(pair_free[p_rw7.pair(0)], p_rw7.uses(0, 0) + 1)
            pe.wait_ge(pair_free[p_rw.pair(1)], p_rw.uses(2, 1) + 1)
            for n, j in enumerate(BLOCKS):
                w = 32 if j == NBLK - 1 else P
                if n >= 4:
                    pe.wait_ge(sh_y, n - 3)
                for t in range(NT):
                    last = nc.tensor.transpose(ps[0:w, 4 + n % 4, t * P:(t + 1) * P], proj[:, t, j * P:j * P + w], ident)
                last.then_inc(sh_t, 1)
                fill(IN_SHIFT[n % 2])
            for b in range(NPAIR):
                pe.wait_ge(kk_sq, b + 1)
                mm(ps[0:NH, 6, 0:T], kc[:, K_SEL + NH * b:K_SEL + NH * (b + 1)], sqb[:, b % 2, :],
                   start=(b == 0), stop=(b == NPAIR - 1)).then_inc(kk_sum, 1)
                fill(IN_KK[b % 2])
            pe.wait_ge(gd_ready, 1)
            pe.wait_ge(par_in, 16 * 5)
            for b in range(NPAIR):
                if b >= 2:
                    pe.wait_ge(g_st, b - 1)
                o = ps[:, 4 + b % 2, 0:T]
                mm(o, gupa[:, b * P:(b + 1) * P], lgd[:, 0, :], start=True, stop=False)
                mm(o, gupb[:, b * P:(b + 1) * P], lgd[0:32, 1, :], start=False, stop=True).then_inc(g_mm, 1)
                fill(IN_G[b % 2])
            pe.wait_ge(kk_rec, 1)
            for b in range(NPAIR):
                if b >= 2:
                    pe.wait_ge(kk_ready, b - 1)
                mm(ps[:, 6 + b % 2, 0:T], selt1[:, b * P:(b + 1) * P], s16[:, 0, :], start=True, stop=True).then_inc(kk_bc, 1)

            def low_rank(m):
                b, d = m // 2, m % 2
                if m >= 2:
                    pe.wait_ge(za_act, m - 1)
                rows = slice(LORA * d, LORA * (d + 1))
                sgn = slice(None, None, -1) if d else slice(None)
                mm(ps[:, 4 + m % 2, 0:T], wup[rows, b * P:(b + 1) * P], lwa[rows, 0, sgn], start=True, stop=True)
                mm(ps[:, 4 + m % 2, T:2 * T], aup[rows, b * P:(b + 1) * P], lwa[rows, 1, sgn],
                   start=True, stop=True).then_inc(za_mm, 1)

            def n_products(m):
                pe.wait_ge(q_ready, m + 1)
                pe.wait_ge(ra_ready, 2 * m + 2)
                if m >= 2:
                    pe.wait_ge(n_st, m - 1)
                    if m % 2 == 0:
                        pe.wait_ge(bon_st, m // 2)
                else:
                    pe.wait_ge(kk_ready, NPAIR)
                for c in range(NC_):
                    for h in range(2):
                        r = slice(C * h, C * (h + 1))
                        last = mm(ps[r, 6 + m % 2, c * C:(c + 1) * C], beta[r, m, c * C:(c + 1) * C],
                                  q[r, 1 + 3 * (NC_ * m + c) + 2, :], start=True, stop=True)
                last.then_inc(n_mm, 1)

            pe.wait_ge(g_st, NPAIR)
            pe.wait_ge(lora_act, 1)
            low_rank(0)
            low_rank(1)
            for m in range(NM):
                fill(IN_CHUNKS[m % 2])
                n_products(m)
                if m % 2:
                    b = m // 2
                    pe.wait_ge(bon_in, b + 1)
                    pe.wait_ge(n_st, m)
                    mm(ps[:, 6, T:2 * T], headsum[:, :], kds[:, :], start=True, stop=True).then_inc(bon_mm, 1)
                if m + 2 < NM:
                    low_rank(m + 2)

            walk(pe, p_gate, from_u(p_gate, None))

            pe.wait_ge(zs_in, 32)
            for b in range(2):
                pe.wait_ge(pair_free[b], (p_gate.q0 + 8 - b + 1) // 2)

            def alpha_beta(m, c):
                if c == 0:
                    pe.wait_ge(dd_ready, m + 1)
                    if m:
                        pe.wait_ge(ab_ready, 2 * m)
                at = 1 + 3 * (NC_ * m + c)
                dd = 1 + 3 * NC_ * NM + NC_ * (m % 2) + c
                for h in range(2):
                    r = slice(C * h, C * (h + 1))
                    o = ps[r, c // 2, (c % 2) * 4 * C:(c % 2 + 1) * 4 * C]
                    mm(o[:, 0:2 * C], beta[r, m, c * C:(c + 1) * C], q[r, at:dd + 1:dd - at, :], start=True, stop=True)
                    last = mm(o[:, 2 * C:4 * C], q[r, at + 2, :], q[r, 0:at + 2:at + 1, :], start=True, stop=True)
                if c % 2:
                    last.then_inc(ab_mm, 1)

            def values_t(m):
                b, d = m // 2, m % 2
                if d:
                    pe.wait_ge(vr_ready, b + 1)
                else:
                    pe.wait_ge(vb_in, 16 * (b + 1))
                if m:
                    pe.wait_ge(vt_ready, m)
                vt = vrev if d else vb
                for c in range(NC_):
                    last = mm(ps[C:P, 2, c * P:(c + 1) * P], vt[:, c * C:(c + 1) * C], ident, start=True, stop=True)
                last.then_inc(vt_mm, 1)

            def w_products(m):
                pe.wait_ge(ab_ready, 2 * m + 2)
                if m:
                    pe.wait_ge(w_ready, m)
                for c in range(NC_):
                    for h in range(2):
                        r = slice(C * h, C * (h + 1))
                        last = mm(ps[r, 3, c * P:(c + 1) * P], zs[r, NC_ * m + c, :], mb[r, m % 2, c, 2 * C:4 * C],
                                  start=True, stop=True)
                last.then_inc(w_mm, 1)

            def gh_products(m):
                pe.wait_ge(w_ready, m + 1)
                if m:
                    pe.wait_ge(gh_ready, 2 * m)
                pe.wait_ge(ik_ready, m + 1)
                for c in range(NC_):
                    at = 1 + 3 * (NC_ * m + c)
                    dd = 1 + 3 * NC_ * NM + NC_ * (m % 2) + c
                    for h in range(2):
                        r = slice(C * h, C * (h + 1))
                        o = ps[:, 4 + h, c * P:(c + 1) * P]
                        mm(o, wt[r, m % 2, c, :], mb[r, m % 2, c, 0:2 * C], start=True, stop=False)
                        last = mm(o, ik[r, c, :], q[r, at:dd + 1:dd - at, :], start=False, stop=True)
                        if c == NC_ - 1:
                            last.then_inc(gh_mm, 1)

            def recur(m, c):
                if c == 0:
                    pe.wait_ge(gh_ready, 2 * m + 2)
                    pe.wait_ge(vt_ready, m + 1)
                    pe.wait_ge(sv_zero, 1)
                    if m:
                        pe.wait_ge(o_ready, m)
                else:
                    pe.wait_ge(s_ready, 3 * m + c)
                if c < NC_ - 1:
                    for h in range(2):
                        last = mm(ps[0:C, 6, h * C:(h + 1) * C], gh[:, m % 2, NC_ * h + c, C:2 * C],
                                  sv[:, m % 2, c, h * C:(h + 1) * C], start=True, stop=True)
                    last.then_inc(s_mm, 1)
                for h in range(2):
                    last = mm(ps[C * h:C * (h + 1), 7, c * C:(c + 1) * C], sv[:, m % 2, c, h * C:(h + 1) * C],
                              gh[:, m % 2, NC_ * h + c, 0:C], start=True, stop=True)
                if c == NC_ - 1:
                    last.then_inc(o_mm, 1)

            for c in range(NC_):
                alpha_beta(0, c)
            w_products(0)
            values_t(0)
            for c in range(NC_):
                alpha_beta(1, c)
            gh_products(0)
            for m in range(NM):
                if m + 1 < NM:
                    w_products(m + 1)
                    values_t(m + 1)
                for c in range(NC_):
                    recur(m, c)
                    if m + 2 < NM:
                        alpha_beta(m + 2, c)
                if m + 1 < NM:
                    gh_products(m + 1)
            pe.wait_ge(ab_ready, 2 * NM)
            pe.wait_ge(o_ready, NM)
            for b in range(NPAIR):
                last = mm(ps[0:NH, 0, 0:T], kc[:, K_SEL + NH * b:K_SEL + NH * (b + 1)], oc[:, b, :],
                          start=(b == 0), stop=(b == NPAIR - 1))
            last.then_inc(gn_sum, 1)
            pe.wait_ge(gn_mean, 1)
            pe.wait_ge(gn_in, 16 * 3)
            for b in range(NPAIR):
                if b >= 4:
                    pe.wait_ge(gn_cent, b - 3)
                mm(ps[:, 4 + b % 4, 0:T], selt2[:, b * P:(b + 1) * P], o16[:, 0, :], start=True, stop=True).then_inc(gn_bc, 1)
            for b in range(NPAIR):
                pe.wait_ge(gn_sq, b + 1)
                mm(ps[0:NH, 1, 0:T], kc[:, K_SEL + NH * b:K_SEL + NH * (b + 1)], osq[:, b % 2, :],
                   start=(b == 0), stop=(b == NPAIR - 1)).then_inc(gn_var, 1)
            pe.wait_ge(gn_rec, 1)
            for b in range(NPAIR):
                if b >= 4:
                    pe.wait_ge(ya_y, b - 3)
                mm(ps[:, 4 + b % 4, 0:T], selt2[:, b * P:(b + 1) * P], o16[:, 3, :], start=True, stop=True).then_inc(gn_bc2, 1)

            pe.wait_ge(ya_lo, NPAIR)
            fill = filler(in_steps(p_ya, product(p_ya, lambda u, k: ythi[:, k, :], lambda u, k: ytlo[:, k, :]), [], []))
            fill(IN_ROPE)
            pe.wait_ge(roped, 2 * NT)
            pe.wait_ge(k_roped, 2 * NT)
            for n in range(16):
                if n >= 4:
                    pe.wait_ge(qt_ready, n - 3)
                for t in range(NT):
                    last = nc.tensor.transpose(ps[:, 4 + n % 4, t * P:(t + 1) * P],
                                               qk[:, t, n * P:(n + 1) * P], ident)
                last.then_inc(qt_mm, 1)
            pe.wait_ge(qt_ready, 16)
            pe.wait_ge(at_in, 16 * 5)

            def scores(n):
                t, hd = n // 4, 2 * (n % 4)
                if n:
                    pe.wait_ge(ex_p, n)
                for v in range(2):
                    for s in range(2):
                        r = slice(C * s, C * (s + 1))
                        last = mm(ps[:, s, v * T:(v + 1) * T], qt_[r, hd + v, t * P:(t + 1) * P], kt_[r, hd + v, :],
                                  start=True, stop=True)
                last.then_inc(sc_mm, 1)

            def transpose_maps(n):
                pe.wait_ge(am_ready, n + 1)
                if n >= 2:
                    pe.wait_ge(amt_ready, n - 1)
                for v in range(2):
                    for k in range(NT):
                        last = nc.tensor.transpose(ps[:, 4 + n % 2, v * T + k * P:v * T + (k + 1) * P],
                                                   am[:, 2 * (n % 2) + v, k * P:(k + 1) * P], ident)
                last.then_inc(am_t, 1)

            def values_by_maps(g):
                hs = 4 * (g % 2)
                pe.wait_ge(amt_ready, 2 * g + 2)
                if g:
                    pe.wait_ge(yb_ready, g)
                for v in range(4):
                    for k in range(NT):
                        last = mm(ps[:, 6, v * P:(v + 1) * P], amt[:, v, k * P:(k + 1) * P],
                                  va[:, k, (hs + v) * P:(hs + v + 1) * P], start=(k == 0), stop=(k == NT - 1))
                last.then_inc(pv_mm, 1)

            def transpose_heads(g):
                pe.wait_ge(yb_ready, g + 1)
                if g:
                    pe.wait_ge(yb_lo, g)
                for v in range(4):
                    last = nc.tensor.transpose(ps[:, 7, v * P:(v + 1) * P], ov[:, v, :], ident)
                last.then_inc(yb_t, 1)

            scores(0)
            scores(1)
            for g in range(4):
                transpose_maps(2 * g)
                if g < 3:
                    scores(2 * g + 2)
                transpose_maps(2 * g + 1)
                if g:
                    transpose_heads(g - 1)
                if g < 3:
                    fill(IN_HEADS[0])
                    scores(2 * g + 3)
                    fill(IN_HEADS[1])
                values_by_maps(g)
            transpose_heads(3)

            pe.wait_ge(yb_lo, 4)
            walk(pe, p_yb, product(p_yb, lambda u, k: ythi[:, 8 + k, :], lambda u, k: ytlo[:, 8 + k, :]))
            transpose_u(2, None, None)
            walk(pe, p_out, from_u(p_out, 2))
            transpose_u(3, F2[0], 2)
            feed_forward(1, F2, ffn2, 3)

        @block.gpsimd
        def _(pool):
            links = [0]
            G = nc.gpsimd

            def link(ins):
                links[0] += 1
                ins.then_inc(pool_link, 1)
                pool.wait_ge(pool_link, links[0])

            def inverse_norm(e):
                pool.wait_ge(ms_ready, e + 1)
                G.tensor_tensor(sm[:, RS[e]], sm[:, MS[e]], sm[:, HALF][:, 0:2], ALU.pow).then_inc(rstd_ready, 1)

            def gain(F, g):
                pool.dma_start(F[6][:, :], g.partition_broadcast(P)).then_inc(gain_in, 16)

            link(G.memset(sm[:, HALF], -0.5))
            pool.wait_ge(vr_zero, 1)
            for v, r, n in VECTORS[N_VEC // 2:]:
                dst = vrows[r % P:r % P + n, 0, (r // P) * P:(r // P) * P + v.shape[-1]]
                pool.dma_start(dst, v).then_inc(vr_in, 16)
            inverse_norm(0)
            gain(F1, ffn[0][3][0])
            inverse_norm(1)
            pool.wait_ge(h_ready, H_PARTS)
            pool.dma_start(h_dram.rearrange("(t p) d -> p t d", p=P), F1[0][:, :, :]).then_inc(h_saved, 16)
            inverse_norm(2)

            pool.dma_start(wup[:, :], w_up[0].rearrange("d r c -> (d r) c")).then_inc(par_in, 16)
            pool.dma_start(aup[:, :], a_up[0].rearrange("d r c -> (d r) c")).then_inc(par_in, 16)
            pool.dma_start(gupa[:, :], g_up[0, 0:P, :]).then_inc(par_in, 16)
            pool.dma_start(gupb[:, :], g_up[0, P:GLORA, :]).then_inc(par_in, 16)
            pool.dma_start(selt1[:, :], sel_t).then_inc(par_in, 16)

            def store_chunk(c):
                b = p_dif.pair(c % 2)
                pool.wait_ge(pair_free[b], p_dif.uses(c // 2, c % 2) + 1)
                pool.dma_start(dif_dram[:, c * CW:(c + 1) * CW].rearrange("(t p) n -> p t n", p=P),
                               dst_a[:, b, :, :]).then_inc(st_out[b], 16)

            def stores():
                for n in range(p_dif.chunks * p_dif.slots):
                    if n and n % p_dif.slots == 0:
                        store_chunk(n // p_dif.slots - 1)
                    yield

            fill = filler(stores())
            fill(BEFORE_SHIFT + (NBLK - NPAIR) // 2 * sum(IN_SHIFT))
            for b in range(NPAIR):
                pool.wait_ge(shifted, NBLK - NPAIR + b + 1)
                pool.dma_start(v_dram[b], vst[:, b % 2, :]).then_inc((v_out0, v_out1)[b % 2], 16)
                fill(IN_SHIFT[b % 2])
            fill(sum(IN_KK) * NPAIR // 2)
            for b in range(NPAIR):
                pool.wait_ge(g_st, b + 1)
                pool.dma_start(g_dram[b], gst[:, b % 2, :]).then_inc(g_out[b % 2], 16)
                fill(IN_G[b % 2])
            pool.wait_ge(v_out0, 16 * 4)
            pool.wait_ge(v_out1, 16 * 4)
            pool.wait_ge(g_out[0], 16 * 4)
            pool.wait_ge(g_out[1], 16 * 4)
            pool.wait_ge(kk_ready, NPAIR)
            for m in range(NM):
                b, d = m // 2, m % 2
                if d == 0:
                    if b:
                        pool.wait_ge(bon_st, b)
                    pool.dma_start(vb1[:, :], v_dram[b]).then_inc(v1_in, 16)
                sgn = slice(None, None, -1) if d else slice(None)
                s0 = 1 + 3 * NC_ * m
                qv = q[:, s0:s0 + 3 * NC_, :].rearrange("p (c w) t -> p c w t", w=3)
                ch = lambda a: a.rearrange("p (c t) -> p c t", c=NC_)
                pool.wait_ge(ex_out, m + 1)
                G.tensor_tensor(qv[:, :, 0, :], ch(rr[:, b, sgn]), ch(eie[:, 0, :]), ALU.mult).then_inc(ra_ready, 1)
                G.tensor_tensor(qv[:, :, 2, :], ch(kkn[:, b, sgn]), ch(eie[:, 1, :]), ALU.mult).then_inc(ra_ready, 1)
                if d == 0 and b:
                    pool.wait_ge(bon_st, b)
                    pool.dma_start(bonus_dram[b - 1], bst[:, :]).then_inc(bon_out, 16)
                fill(IN_CHUNKS[d])
            store_chunk(p_dif.chunks - 1)
            pool.wait_ge(bon_st, NPAIR)
            pool.dma_start(bonus_dram[NPAIR - 1], bst[:, :]).then_inc(bon_out, 16)
            pool.wait_ge(n_out[0], 32 * (NM // 2))
            pool.wait_ge(n_out[1], 32 * (NM // 2))
            pool.wait_ge(bon_out, 16 * NPAIR)
            pool.dma_start(z[:, :, :].rearrange("p c t -> p (c t)"),
                           n_dram.rearrange("h m c s t -> (h m c) (s t)")).then_inc(z_in, 16)
            def store_gates(chunks):
                for c in chunks:
                    b = p_gate.pair(c % 2)
                    pool.wait_ge(pair_free[b], p_gate.uses(c // 2, c % 2) + 1)
                    pool.dma_start(gate_dram[:, c * CW:(c + 1) * CW].rearrange("(t p) n -> p t n", p=P),
                                   gst_g[:, b, :, :]).then_inc(st_out[b], 16)

            store_gates(range(6))
            pool.wait_ge(z_done, 1)
            pool.dma_start(z_dram.rearrange("h m c s t -> (h m c) (s t)"),
                           z[:, :, :].rearrange("p c t -> p (c t)")).then_inc(z_out, 16)
            pool.wait_ge(z_out, 16)
            for h in range(2):
                pool.dma_start(zs[C * h:C * (h + 1), :, :],
                               z_dram[h].rearrange("m c s t -> s (m c) t")).then_inc(zs_in, 16)
            store_gates(range(6, 8))

            pool.wait_ge(zs_in, 32)

            def kappas(m):
                if m:
                    pool.wait_ge(gh_mm, 2 * m)
                at = 1 + 3 * NC_ * m
                G.tensor_copy(ik[:, :, C:2 * C], q[:, at:at + 3 * NC_, :].rearrange("p (c w) t -> p c w t", w=3)[:, :, 1, :]).then_inc(ik_ready, 1)

            link(G.tensor_copy(ik[:, :, 0:C], q[:, 0:1, :].broadcast_to((P, NC_, C))))
            kappas(0)
            for b in range(NPAIR):
                if b:
                    pool.wait_ge(vt_mm, 2 * b - 1)
                    pool.wait_ge(vr_ready, b)
                pool.dma_start(vb[:, :], v_dram[b]).then_inc(vb_in, 16)
                pool.wait_ge(vb_in, 16 * (b + 1))
                if b:
                    pool.wait_ge(vt_mm, 2 * b)
                G.tensor_copy(vrev[:, :], vb[:, ::-1]).then_inc(vr_ready, 1)
                if b:
                    kappas(2 * b - 1)
                    kappas(2 * b)
            kappas(NM - 1)
            pool.wait_ge(gh_mm, 2 * NM)
            pool.dma_start(selt2[:, :], sel_t).then_inc(gn_in, 16)
            pool.dma_start(bo[:, :, :], bonus_dram.rearrange("b p t -> p b t")).then_inc(gn_in, 16)
            pool.dma_start(gg[:, :, :], g_dram.rearrange("b p t -> p b t")).then_inc(gn_in, 16)
            dif = dif_dram.rearrange("(t p) c -> p t c", p=P)
            pool.dma_start(qk[:, :, :], dif[:, :, 0:2 * RW]).then_inc(k_in, 16)
            pool.dma_start(va[:, :, :], dif[:, :, 2 * RW:3 * RW]).then_inc(at_in, 16)
            pool.wait_ge(k_in, 16)
            for t in range(NT):
                rope(G, qk[:, t, RW:2 * RW], t, pa, pb, k_roped, t, pool)
            pool.wait_ge(ya_lo, NPAIR)
            for i, n in enumerate(("lambda_q1", "lambda_k1", "lambda_q2", "lambda_k2")):
                pool.dma_start(lamv[:, i, :], a[n][0].partition_broadcast(P)).then_inc(at_in, 16)
            gates = gate_dram.rearrange("(t p) (w c n) -> p w c t n", p=P, w=2, n=CW)

            def load_gate(w, c):
                if w and c >= 2:
                    pool.wait_ge(mg_ready, c - 1)
                elif w or c >= 2:
                    pool.wait_ge(pair_free[p_ya.pair(0)], p_ya.uses(w, c % 2) + 1)
                pool.dma_start(gbuf[:, c % 2, :, :], gates[:, w, c, :, :]).then_inc(gt_in[c % 2], 16)

            load_gate(0, 0)
            load_gate(0, 1)
            load_gate(0, 2)
            for g in range(4):
                pool.wait_ge(pv_ms, g + 1)
                if g:
                    pool.wait_ge(yb_ready, g)
                G.tensor_tensor(os_[:, 8:12], os_[:, 4:8], sm[:, HALF][:, 0:4], ALU.pow).then_inc(pv_rs, 1)
                if g < 3:
                    load_gate((g + 3) // 4, (g + 3) % 4)
            for c in range(2, 4):
                load_gate(1, c)
            pool.wait_ge(mg_ready, 4)
            pool.wait_ge(slots_used, p_yb.end(1, 1))
            pool.dma_start(F2[0][:, :, :], h_dram.rearrange("(t p) d -> p t d", p=P)).then_inc(h_back, 16)
            gain(F2, mix_post_g[0])
            inverse_norm(3)
            inverse_norm(4)
            pool.wait_ge(h_ready, 2 * H_PARTS)
            gain(F2, ffn[1][3][0])
            inverse_norm(5)
            for c in range(D // CW):
                cols = slice(c * CW, (c + 1) * CW)
                pool.wait_ge(h_ready, 2 * H_PARTS + NT * (c + 1))
                pool.dma_start(out[0].rearrange("(t p) d -> p t d", p=P)[:, :, cols], F2[0][:, :, cols]).then_inc(out_done, 16)
            pool.wait_ge(out_done, 16 * (D // CW))
            pool.wait_ge(h_saved, 16)


_NAMES = ['x', 'ffn1_pre_g', 'ffn1_w_gu', 'ffn1_w_down', 'ffn1_post_g', 'mix_pre_g', 'w_in', 'mu_prev', 'mu_next',
          'w0', 'w_up', 'a0', 'a_up', 'g_up', 'k_k', 'k_a', 'r_k', 'gn_w', 'gn_b', 'lambda_q1', 'lambda_k1',
          'lambda_q2', 'lambda_k2', 'subln_g', 'w_branch_a', 'w_branch_b', 'w_out', 'mix_post_g', 'ffn2_pre_g',
          'ffn2_w_gu', 'ffn2_w_down', 'ffn2_post_g']


def kernel(**inputs):
    import concourse.bacc as bacc
    from concourse.bass_utils import run_bass_kernel_spmd

    nc = bacc.Bacc("TRN2", target_bir_lowering=False, num_devices=1)
    arrays, a = {}, {}
    consts, sel_t = constants()
    for name, array in [(n, np.ascontiguousarray(inputs[n])) for n in _NAMES] + [("consts", consts), ("sel_t", sel_t)]:
        arrays["in_" + name] = array
        a[name] = nc.dram_tensor("in_" + name, array.shape, F32, kind="ExternalInput").ap()
    out = nc.dram_tensor("out_0", (1, T, D), F32, kind="ExternalOutput").ap()
    layer(nc, a, out)
    r = run_bass_kernel_spmd(nc, [arrays], core_ids=[0])
    return r.results[0]["out_0"]
```
